# Optimizing a Trainium2 kernel written in Bass

```python
import jax
import jax.numpy as jnp
from jax import lax

D_MODEL = 1024
BATCH = 1
SEQ = 256
DEPTH = 2

MEM_LEN = 256
GRID_W = 64
Q_BLOCK = 128
ROPE_THETA = 500000.0
NORM_EPS = 1e-6

MLA_HEADS = 8
MLA_Q_LORA = 384
MLA_KV_LORA = 256
MLA_NOPE_DIM = 64
MLA_ROPE_DIM = 32
MLA_V_DIM = 64

GQA_Q_HEADS = 8
GQA_KV_HEADS = 2
GQA_GROUP = GQA_Q_HEADS // GQA_KV_HEADS
GQA_HEAD_DIM = 64

DIFF_HEADS = 8
DIFF_QK_DIM = 32
DIFF_V_DIM = 2 * DIFF_QK_DIM
DIFF_ROPE_DIM = DIFF_QK_DIM // 4

N_BRANCHES = 3
BRANCH_WIDTH = 512

MEM_HEADS = 4
MEM_HEAD_DIM = D_MODEL // MEM_HEADS

D_FF = 2816
N_EXPERTS = 8
TOP_K = 2

IN_SPLITS = (MLA_Q_LORA, MLA_KV_LORA, MLA_ROPE_DIM,
             GQA_Q_HEADS * GQA_HEAD_DIM, GQA_KV_HEADS * GQA_HEAD_DIM, GQA_KV_HEADS * GQA_HEAD_DIM,
             DIFF_HEADS * 2 * DIFF_QK_DIM, DIFF_HEADS * 2 * DIFF_QK_DIM, DIFF_HEADS * DIFF_V_DIM,
             N_BRANCHES * D_MODEL)
IN_COLS = sum(IN_SPLITS)

kernel_name = 'hybrid_gated_mla_gqa_diff_moe_encoder'

def rms_norm(x, g):
    xf = x.astype(jnp.float32)
    y = xf * lax.rsqrt(jnp.mean(xf * xf, axis=-1, keepdims=True) + NORM_EPS)
    return (y * g.astype(jnp.float32)).astype(x.dtype)

def rope_cos_sin(pos, rot_dim):
    inv = ROPE_THETA ** (-jnp.arange(0, rot_dim, 2, dtype=jnp.float32) / rot_dim)
    ang = pos.astype(jnp.float32)[:, None] * inv[None, :]
    return jnp.cos(ang), jnp.sin(ang)

def apply_rotary(x, cos, sin):
    cos = cos.astype(x.dtype)
    sin = sin.astype(x.dtype)
    x1, x2 = jnp.split(x, 2, axis=-1)
    return jnp.concatenate([x1 * cos - x2 * sin, x2 * cos + x1 * sin], axis=-1)

def split_cols(z, sizes):
    out, start = [], 0
    for n in sizes:
        out.append(z[..., start:start + n])
        start += n
    return out

def blocked_attention(q, k, v, scale):
    B, S = q.shape[0], q.shape[1]
    nb = S // Q_BLOCK
    qb = q.reshape(B, nb, Q_BLOCK, *q.shape[2:]).swapaxes(0, 1)

    def one_block(q_blk):
        s = jnp.einsum('bqgrd,bkgd->bgrqk', q_blk, k, preferred_element_type=jnp.float32) * scale
        p = jax.nn.softmax(s, axis=-1).astype(v.dtype)
        return jnp.einsum('bgrqk,bkgv->bqgrv', p, v)

    out = lax.map(one_block, qb)
    return out.swapaxes(0, 1).reshape(B, S, *out.shape[3:])

def blocked_diff_attention(q, k, v, lam, scale):
    B, S = q.shape[0], q.shape[1]
    nb = S // Q_BLOCK
    qb = q.reshape(B, nb, Q_BLOCK, *q.shape[2:]).swapaxes(0, 1)

    def one_block(q_blk):
        s = jnp.einsum('bqhcd,bkhcd->bhcqk', q_blk, k, preferred_element_type=jnp.float32) * scale
        p = jax.nn.softmax(s, axis=-1)
        a = (p[:, :, 0] - lam * p[:, :, 1]).astype(v.dtype)
        return jnp.einsum('bhqk,bkhv->bqhv', a, v)

    out = lax.map(one_block, qb)
    return out.swapaxes(0, 1).reshape(B, S, *out.shape[3:])

def mla_branch(c_q, c_kv, k_rope, q_norm_g, w_q_up, kv_norm_g, w_kv_up, cos, sin):
    B, S, _ = c_q.shape
    q = (rms_norm(c_q, q_norm_g) @ w_q_up).reshape(B, S, MLA_HEADS, MLA_NOPE_DIM + MLA_ROPE_DIM)
    kv = (rms_norm(c_kv, kv_norm_g) @ w_kv_up).reshape(B, S, MLA_HEADS, MLA_NOPE_DIM + MLA_V_DIM)
    q_nope, q_rot = q[..., :MLA_NOPE_DIM], q[..., MLA_NOPE_DIM:]
    k_nope, v = kv[..., :MLA_NOPE_DIM], kv[..., MLA_NOPE_DIM:]
    q_rot = apply_rotary(q_rot, cos[:, None, :], sin[:, None, :])
    k_rot = apply_rotary(k_rope, cos, sin)
    k_rot = jnp.broadcast_to(k_rot[:, :, None, :], (B, S, MLA_HEADS, MLA_ROPE_DIM))
    q_full = jnp.concatenate([q_nope, q_rot], axis=-1)[:, :, :, None, :]
    k_full = jnp.concatenate([k_nope, k_rot], axis=-1)
    o = blocked_attention(q_full, k_full, v, (MLA_NOPE_DIM + MLA_ROPE_DIM) ** -0.5)
    return o.reshape(B, S, MLA_HEADS * MLA_V_DIM)

def gqa_branch(q, k, v, q_norm_g, k_norm_g, cos_ax, sin_ax):
    B, S, _ = q.shape
    q = rms_norm(q.reshape(B, S, GQA_Q_HEADS, GQA_HEAD_DIM), q_norm_g)
    k = rms_norm(k.reshape(B, S, GQA_KV_HEADS, GQA_HEAD_DIM), k_norm_g)
    v = v.reshape(B, S, GQA_KV_HEADS, GQA_HEAD_DIM)
    q = apply_rotary(q, cos_ax[:, None, :], sin_ax[:, None, :])
    k = apply_rotary(k, cos_ax[:, None, :], sin_ax[:, None, :])
    q = q.reshape(B, S, GQA_KV_HEADS, GQA_GROUP, GQA_HEAD_DIM)
    o = blocked_attention(q, k, v, GQA_HEAD_DIM ** -0.5)
    return o.reshape(B, S, GQA_Q_HEADS * GQA_HEAD_DIM)

def diff_branch(q, k, v, lq1, lk1, lq2, lk2, subln_g, lambda_init, cos_p, sin_p):
    B, S, _ = q.shape
    q = q.reshape(B, S, DIFF_HEADS, 2, DIFF_QK_DIM)
    k = k.reshape(B, S, DIFF_HEADS, 2, DIFF_QK_DIM)
    v = v.reshape(B, S, DIFF_HEADS, DIFF_V_DIM)
    c4, s4 = cos_p[:, None, None, :], sin_p[:, None, None, :]
    q = jnp.concatenate([apply_rotary(q[..., :DIFF_ROPE_DIM], c4, s4), q[..., DIFF_ROPE_DIM:]], axis=-1)
    k = jnp.concatenate([apply_rotary(k[..., :DIFF_ROPE_DIM], c4, s4), k[..., DIFF_ROPE_DIM:]], axis=-1)
    f32 = jnp.float32
    lam = (jnp.exp(jnp.sum(lq1.astype(f32) * lk1.astype(f32)))
           - jnp.exp(jnp.sum(lq2.astype(f32) * lk2.astype(f32))) + lambda_init)
    o = blocked_diff_attention(q, k, v, lam, DIFF_QK_DIM ** -0.5)
    o = rms_norm(o, subln_g) * (1.0 - lambda_init)
    return o.reshape(B, S, DIFF_HEADS * DIFF_V_DIM)

def hybrid_mixer(h, w_in, mla_q_norm_g, mla_w_q_up, mla_kv_norm_g, mla_w_kv_up,
                 gqa_q_norm_g, gqa_k_norm_g, lq1, lk1, lq2, lk2, diff_subln_g,
                 w_branch, w_out, lambda_init, rope):
    cos_m, sin_m, cos_ax, sin_ax, cos_p, sin_p = rope
    (c_q, c_kv, k_rope, g_q, g_k, g_v, d_q, d_k, d_v, gate_pre) = split_cols(h @ w_in, IN_SPLITS)
    a = mla_branch(c_q, c_kv, k_rope, mla_q_norm_g, mla_w_q_up, mla_kv_norm_g, mla_w_kv_up, cos_m, sin_m)
    b = gqa_branch(g_q, g_k, g_v, gqa_q_norm_g, gqa_k_norm_g, cos_ax, sin_ax)
    c = diff_branch(d_q, d_k, d_v, lq1, lk1, lq2, lk2, diff_subln_g, lambda_init, cos_p, sin_p)
    branches = jnp.stack([a, b, c], axis=2)
    proj = jnp.einsum('bsnw,nwd->bsnd', branches, w_branch)
    gates = jax.nn.sigmoid(gate_pre.reshape(*gate_pre.shape[:2], N_BRANCHES, D_MODEL))
    merged = jnp.sum(gates * proj, axis=2)
    return merged @ w_out

def memory_cross_attention(h, m, wq, wkv, wo):
    B, S, _ = h.shape
    M = m.shape[1]
    q = (h @ wq).reshape(B, S, MEM_HEADS, MEM_HEAD_DIM)
    kv = (m @ wkv).reshape(B, M, 2, MEM_HEADS, MEM_HEAD_DIM)
    s = jnp.einsum('bshd,bmhd->bhsm', q, kv[:, :, 0], preferred_element_type=jnp.float32) * MEM_HEAD_DIM ** -0.5
    p = jax.nn.softmax(s, axis=-1).astype(h.dtype)
    o = jnp.einsum('bhsm,bmhd->bshd', p, kv[:, :, 1]).reshape(B, S, MEM_HEADS * MEM_HEAD_DIM)
    return o @ wo

def swiglu(h, w_gate, w_up, w_down):
    return (jax.nn.silu(h @ w_gate) * (h @ w_up)) @ w_down

def moe_swiglu(h, w_router, b_router, w_gate, w_up, w_down):
    logits = jnp.einsum('bsd,de->bse', h, w_router, preferred_element_type=jnp.float32) + b_router.astype(jnp.float32)
    top_val, top_idx = lax.top_k(logits, TOP_K)
    top_w = jax.nn.softmax(top_val, axis=-1)
    gates = jnp.einsum('bsk,bske->bse', top_w, jax.nn.one_hot(top_idx, N_EXPERTS, dtype=jnp.float32)).astype(h.dtype)
    y = jnp.zeros_like(h)
    for e in range(N_EXPERTS):
        y = y + gates[..., e:e + 1] * swiglu(h, w_gate[e], w_up[e], w_down[e])
    return y

def setup_inputs(seed: int = 0) -> dict:
    key = jax.random.key(seed)
    keys = iter(jax.random.split(key, 64))
    L = DEPTH
    n_dense = (DEPTH + 1) // 2
    n_moe = DEPTH // 2

    def normal(shape, scale):
        return jax.random.normal(next(keys), shape, jnp.float32) * scale

    def gain(shape):
        return 1.0 + normal(shape, 0.02)

    return {
        'x': normal((BATCH, SEQ, D_MODEL), 1.0),
        'mem': normal((BATCH, MEM_LEN, D_MODEL), 1.0),
        'mix_pre_g': gain((L, D_MODEL)),
        'mix_post_g': gain((L, D_MODEL)),
        'w_in': normal((L, D_MODEL, IN_COLS), D_MODEL ** -0.5),
        'mla_q_norm_g': gain((L, MLA_Q_LORA)),
        'mla_w_q_up': normal((L, MLA_Q_LORA, MLA_HEADS * (MLA_NOPE_DIM + MLA_ROPE_DIM)), MLA_Q_LORA ** -0.5),
        'mla_kv_norm_g': gain((L, MLA_KV_LORA)),
        'mla_w_kv_up': normal((L, MLA_KV_LORA, MLA_HEADS * (MLA_NOPE_DIM + MLA_V_DIM)), MLA_KV_LORA ** -0.5),
        'gqa_q_norm_g': gain((L, GQA_HEAD_DIM)),
        'gqa_k_norm_g': gain((L, GQA_HEAD_DIM)),
        'diff_lambda_q1': normal((L, DIFF_QK_DIM), 0.1),
        'diff_lambda_k1': normal((L, DIFF_QK_DIM), 0.1),
        'diff_lambda_q2': normal((L, DIFF_QK_DIM), 0.1),
        'diff_lambda_k2': normal((L, DIFF_QK_DIM), 0.1),
        'diff_subln_g': gain((L, DIFF_V_DIM)),
        'w_branch': normal((L, N_BRANCHES, BRANCH_WIDTH, D_MODEL), BRANCH_WIDTH ** -0.5),
        'w_out': normal((L, D_MODEL, D_MODEL), D_MODEL ** -0.5),
        'mem_pre_g': gain((L, D_MODEL)),
        'mem_post_g': gain((L, D_MODEL)),
        'mem_norm_g': gain((L, D_MODEL)),
        'mem_wq': normal((L, D_MODEL, MEM_HEADS * MEM_HEAD_DIM), D_MODEL ** -0.5),
        'mem_wkv': normal((L, D_MODEL, 2 * MEM_HEADS * MEM_HEAD_DIM), D_MODEL ** -0.5),
        'mem_wo': normal((L, MEM_HEADS * MEM_HEAD_DIM, D_MODEL), (MEM_HEADS * MEM_HEAD_DIM) ** -0.5),
        'ffn_pre_g': gain((L, D_MODEL)),
        'ffn_post_g': gain((L, D_MODEL)),
        'dense_w_gate': normal((n_dense, D_MODEL, D_FF), D_MODEL ** -0.5),
        'dense_w_up': normal((n_dense, D_MODEL, D_FF), D_MODEL ** -0.5),
        'dense_w_down': normal((n_dense, D_FF, D_MODEL), D_FF ** -0.5),
        'moe_w_router': normal((n_moe, D_MODEL, N_EXPERTS), D_MODEL ** -0.5),
        'moe_b_router': normal((n_moe, N_EXPERTS), 0.01),
        'moe_w_gate': normal((n_moe, N_EXPERTS, D_MODEL, D_FF), D_MODEL ** -0.5),
        'moe_w_up': normal((n_moe, N_EXPERTS, D_MODEL, D_FF), D_MODEL ** -0.5),
        'moe_w_down': normal((n_moe, N_EXPERTS, D_FF, D_MODEL), D_FF ** -0.5),
    }

def reference(x, mem, mix_pre_g, mix_post_g, w_in, mla_q_norm_g, mla_w_q_up, mla_kv_norm_g,
              mla_w_kv_up, gqa_q_norm_g, gqa_k_norm_g, diff_lambda_q1, diff_lambda_k1,
              diff_lambda_q2, diff_lambda_k2, diff_subln_g, w_branch, w_out, mem_pre_g,
              mem_post_g, mem_norm_g, mem_wq, mem_wkv, mem_wo, ffn_pre_g, ffn_post_g,
              dense_w_gate, dense_w_up, dense_w_down, moe_w_router, moe_b_router,
              moe_w_gate, moe_w_up, moe_w_down):
    S = x.shape[1]
    rows = S // GRID_W
    pos = jnp.arange(S)
    row = jnp.repeat(jnp.arange(rows), GRID_W)
    col = jnp.tile(jnp.arange(GRID_W), rows)
    cos_m, sin_m = rope_cos_sin(pos, MLA_ROPE_DIM)
    cos_r, sin_r = rope_cos_sin(row, GQA_HEAD_DIM // 2)
    cos_c, sin_c = rope_cos_sin(col, GQA_HEAD_DIM // 2)
    cos_ax = jnp.concatenate([cos_r, cos_c], axis=-1)
    sin_ax = jnp.concatenate([sin_r, sin_c], axis=-1)
    cos_p, sin_p = rope_cos_sin(pos, DIFF_ROPE_DIM)
    rope = (cos_m, sin_m, cos_ax, sin_ax, cos_p, sin_p)

    for layer in range(DEPTH):
        lambda_init = 0.8 - 0.6 * float(jnp.exp(-0.3 * layer)) if False else 0.8 - 0.6 * (2.718281828459045 ** (-0.3 * layer))
        h = rms_norm(x, mix_pre_g[layer])
        y = hybrid_mixer(h, w_in[layer], mla_q_norm_g[layer], mla_w_q_up[layer], mla_kv_norm_g[layer],
                         mla_w_kv_up[layer], gqa_q_norm_g[layer], gqa_k_norm_g[layer],
                         diff_lambda_q1[layer], diff_lambda_k1[layer], diff_lambda_q2[layer],
                         diff_lambda_k2[layer], diff_subln_g[layer], w_branch[layer], w_out[layer],
                         lambda_init, rope)
        x = x + rms_norm(y, mix_post_g[layer])

        h = rms_norm(x, mem_pre_g[layer])
        m = rms_norm(mem, mem_norm_g[layer])
        y = memory_cross_attention(h, m, mem_wq[layer], mem_wkv[layer], mem_wo[layer])
        x = x + rms_norm(y, mem_post_g[layer])

        h = rms_norm(x, ffn_pre_g[layer])
        if layer % 2 == 0:
            i = layer // 2
            y = swiglu(h, dense_w_gate[i], dense_w_up[i], dense_w_down[i])
        else:
            i = layer // 2
            y = moe_swiglu(h, moe_w_router[i], moe_b_router[i], moe_w_gate[i], moe_w_up[i], moe_w_down[i])
        x = x + rms_norm(y, ffn_post_g[layer])
    return x


_drawn_inputs = setup_inputs


def setup_inputs(seed=0):
    import zlib

    import numpy as np

    out = dict(_drawn_inputs(seed))
    spreads = {}
    factors = {'mla_q_norm_g': 8.0,
     'mla_kv_norm_g': 8.0,
     'gqa_q_norm_g': 8.0,
     'gqa_k_norm_g': 8.0,
     'ffn_post_g': 3.182,
     'moe_b_router': 3.163,
     'diff_subln_g': 4.249}
    for name, (base, spread) in spreads.items():
        noise = np.random.default_rng([zlib.crc32(name.encode()), seed]).standard_normal(out[name].shape)
        drawn = base * np.exp(spread * noise) if base else spread * noise
        out[name] = jnp.asarray(drawn.astype(out[name].dtype))
    for name, factor in factors.items():
        out[name] = (out[name] * factor).astype(out[name].dtype)
    return out
```

```python
import concourse.bass as bass
from concourse import mybir
from contextlib import ExitStack

D = 1024
SEQ = 256
P = 128
NT = SEQ // P
DEPTH = 2
MEM_LEN = 256
EPS = 1e-6
MLA_H, Q_LORA, KV_LORA, NOPE, ROT, MLA_V = 8, 384, 256, 64, 32, 64
GQA_QH, GQA_KVH, HD = 8, 2, 64
DIFF_H, DQK, DV, DROT = 8, 32, 64, 8
BW = 512
NBR = 3
MEM_H, MEM_HD = 4, 256
F = 2816
NE = 8
QK_MLA = NOPE + ROT
C_ROPE = Q_LORA + KV_LORA
C_GQA = C_ROPE + ROT
N1 = C_GQA + (GQA_QH + 2 * GQA_KVH) * HD
N2 = 3 * DIFF_H * DV
GATE0 = N1 + N2
W1C, W2C = N1 // 3, N2 // 3
FB = 256
NSTEP = F // FB
LAMBDA_INIT = [0.8 - 0.6 * (2.718281828459045 ** (-0.3 * layer)) for layer in range(DEPTH)]
SG_Q, SG_KV, SG_GQ, SG_GK, SG_SUB, SG_LAM, SG_N = 0, 384, 640, 704, 768, 832, 960
RC_M, RS_M, RC_A, RS_A, RC_P, RS_P, R_N = 0, 16, 32, 64, 96, 100, 104
RAW_SLOTS, UNIT_SLOTS = 6, 4
LOOP_UNITS = 12


def unit_widths():
    w = [2 * W1C] * 12
    w += [2 * Q_LORA, Q_LORA] * 2
    w += [1024] * 2
    w += [1024] * 12 * 2
    w += [2 * W2C] * 12
    w += [1024] * 12
    w += [1024] * (8 + 16 + 8 + 8)
    return w


class Counts:

    def __init__(self):
        self.unit = 0
        self.done = 0
        self.acc = 0
        self.rdy = 0
        self.acc_hi = 0
        self.pt = 0
        self.sc = 0
        self.comb = 0
        self.gates = 0
        self.rows = 0
        self.norm = 0
        self.gain = 0
        self.chain = 0


def build(nc, A):
    f32, f32r, i32 = mybir.dt.float32, mybir.dt.float32r, mybir.dt.int32
    ACT, ALU, AX = mybir.ActivationFunctionType, mybir.AluOpType, mybir.AxisListType.X
    ctx = ExitStack()
    WIDTHS = unit_widths()
    LAYER_UNITS = len(WIDTHS)
    FFN_UNITS = 6 * NSTEP
    LAYER0 = [0, LAYER_UNITS + FFN_UNITS]
    FFN0 = [LAYER_UNITS, 2 * LAYER_UNITS + FFN_UNITS]

    def width_of(u):
        for layer in range(DEPTH):
            if LAYER0[layer] <= u < LAYER0[layer] + LAYER_UNITS:
                return WIDTHS[u - LAYER0[layer]]
        return 1024

    with ctx:
        def sb(name, shape, dt=f32):
            return ctx.enter_context(nc.sbuf_tensor(name, shape, dt))

        def sem(name):
            return ctx.enter_context(nc.semaphore(name))

        raw = sb("raw", [P, RAW_SLOTS, 2048])
        w_hi = sb("w_hi", [P, UNIT_SLOTS, 1024], f32r)
        w_lo = sb("w_lo", [P, UNIT_SLOTS, 1024], f32r)
        x = sb("x", [P, NT, D])
        S1 = sb("S1", [P, NT, D])
        ZU = sb("ZU", [P, NT, 2048])
        hT_hi = sb("hT_hi", [P, 8, SEQ], f32r)
        hT_lo = sb("hT_lo", [P, 8, SEQ], f32r)
        oT_hi = sb("oT_hi", [P, 8, SEQ], f32r)
        oT_lo = sb("oT_lo", [P, 8, SEQ], f32r)
        Z = sb("Z", [P, NT, N2])
        qT = sb("qT", [P, 8, SEQ])
        kT = sb("kT", [P, 8, SEQ])
        Pr = sb("Pr", [P, 2, 512])
        PT = sb("PT", [P, 2, 512])
        Ad = sb("Ad", [P, 2, 256])
        E4 = sb("E4", [P, 2, 512])
        hidT_hi = sb("hidT_hi", [P, 2, 256], f32r)
        hidT_lo = sb("hidT_lo", [P, 2, 256], f32r)
        gains = sb("gains", [P, 2, D])
        sg = sb("sg", [P, SG_N])
        rope = sb("rope", [P, NT, R_N])
        ident = sb("ident", [P, P])
        iota = sb("iota", [P, P])
        oh = sb("oh", [P, NT, P], f32r)
        ohT = sb("ohT", [P, 2, SEQ], f32r)
        wr = sb("wr", [P, 8, NE])
        wr_hi = sb("wr_hi", [P, 8, NE], f32r)
        wr_lo = sb("wr_lo", [P, 8, NE], f32r)
        brt = sb("brt", [P, NE])
        misc = sb("misc", [P, 112])
        ssq, ms, rstd, mhalf = (misc[:, 20 * n:20 * n + 20] for n in range(4))
        nmax, sums, rsum = (misc[:, 80 + 8 * n:88 + 8 * n].rearrange("p (u h) -> p u h", h=2) for n in range(3))
        lam = misc[:, 104:108]
        nlam = misc[:, 108:109]
        rounds = sb("rounds", [P, 1], i32)
        ps = ctx.enter_context(nc.psum_tensor("ps", [P, 8, 512], f32))

        scratch = kT[:, :, :].rearrange("p a b -> p (a b)")
        sl = E4[:, 0, :]
        hid = E4[:, 1, :]
        Zf = Z[:, :, :].rearrange("p a b -> p (a b)")
        tri, ones = Zf[:, 0:128], Zf[:, 128:256]

        def small(n, shape_t=True):
            v = Zf[:, 256 + 16 * n:272 + 16 * n]
            return v.rearrange("p (t e) -> p t e", t=2)

        LG, EQ, CC, OH1, OH2, L2, GATE, MASK, RANKM = (small(n) for n in range(9))
        M1, M2, I1, EX, W1, W2 = (Zf[:, 420 + 2 * n:422 + 2 * n] for n in range(6))
        MX, NR = Zf[:, 440:441], Zf[:, 441:442]

        s_x = sem("x_landed")
        s_const = sem("constants_landed")
        s_tri = sem("triangle_landed")
        s_raw = [sem(f"raw_landed{n}") for n in range(RAW_SLOTS)]
        s_hi = sem("unit_hi_ready")
        s_lo = sem("unit_lo_ready")
        s_used = sem("unit_used")
        s_gain = [sem(f"gain_landed{n}") for n in range(2)]
        s_gain_used = sem("gain_used")
        s_sg = sem("small_gains_landed")
        s_mem = sem("mem_landed")
        s_ssq = sem("squares_summed")
        s_pool = sem("pool_chain")
        s_rstd = sem("rstd_ready")
        s_rows = sem("rows_ready")
        s_acc = sem("acc_ready")
        s_acc_hi = sem("acc_hi_copied")
        s_acc_free = sem("acc_free")
        s_gexp = sem("gate_exp_ready")
        s_pt = sem("pt_ready")
        s_pt_copied = sem("pt_copied")
        s_sc = sem("scores_ready")
        s_max = sem("max_ready")
        s_p = sem("probs_ready")
        s_comb = sem("difference_ready")
        s_lamq = sem("lambda_dots_ready")
        s_lame = sem("lambda_exp_ready")
        s_chain = sem("dve_chain")
        s_wr = sem("router_hi_ready")
        s_wrl = sem("router_lo_ready")
        s_silu = sem("silu_ready")
        s_hid = sem("hidden_ready")
        s_hidT = sem("hiddenT_ready")
        s_hidT_hi = sem("hiddenT_hi_copied")
        s_hidT_lo = sem("hiddenT_lo_ready")
        s_yhi = sem("y_hi_copied")
        s_ylo = sem("y_lo_ready")
        s_hrow_hi = sem("rows_hi_ready")
        s_hrow = sem("rows_lo_ready")
        s_topd = sem("top_gap_ready")
        s_tope = sem("top_exp_ready")
        s_rank = sem("ranks_ready")
        s_rounds = sem("rounds_ready")
        s_oh = sem("onehot_ready")
        s_gath = sem("gather_ready")
        s_ohT = sem("onehotT_copied")
        s_gath_hi = sem("gather_hi_copied")
        s_gath_lo = sem("gather_lo_ready")
        s_scat = sem("scatter_ready")
        s_added = sem("scatter_added")
        s_final = sem("result_ready")
        s_out = sem("out_stored")

        def acc_bank(a):
            return 4 + a % 4

        def hi_slot(us):
            return us % UNIT_SLOTS

        def raw_of(us):
            t = us // 2
            off = width_of(us - 1) if us % 2 else 0
            return raw[:, t % RAW_SLOTS, off:off + width_of(us)]

        def act_split(act, us, it=0):
            w = width_of(us)
            if us % 2 == 0:
                act.wait_ge(s_raw[(us // 2) % RAW_SLOTS], it * 32 + 32 * (us // LOOP_UNITS + 1))
            if us >= UNIT_SLOTS:
                act.wait_ge(s_used, it * LOOP_UNITS + (us - UNIT_SLOTS + 1))
            nc.scalar.activation(w_hi[:, hi_slot(us), 0:w], raw_of(us), ACT.Copy).then_inc(s_hi, 1)

        def dve_split(dve, us, it=0):
            w = width_of(us)
            dve.wait_ge(s_hi, it * LOOP_UNITS + (us + 1))
            nc.vector.tensor_tensor(w_lo[:, hi_slot(us), 0:w], raw_of(us),
                                    w_hi[:, hi_slot(us), 0:w].bitcast(f32), ALU.subtract).then_inc(s_lo, 1)

        blk = ctx.enter_context(nc.Block())

        @blk.sync
        def _(sp):
            sp.dma_start(x[:, :, :], A["x"][0].rearrange("(t p) d -> p t d", p=P)).then_inc(s_x, 16)
            n = [0]

            def chunks(W, k0, nk, c0, nc_):
                return W[k0 * P:(k0 + nk) * P, c0:c0 + nc_].rearrange("(k p) n -> p k n", p=P)

            def put(ts, parts, it=0):
                if ts >= RAW_SLOTS:
                    sp.wait_ge(s_lo, it * LOOP_UNITS + 2 * (ts - RAW_SLOTS) + 2)
                slot = ts % RAW_SLOTS
                for off, nk, w, src in parts:
                    dst = raw[:, slot, off:off + nk * w].rearrange("p (k n) -> p k n", k=nk)
                    sp.dma_start(dst, src).then_inc(s_raw[slot], 16)

            def block(W, k_chunks, c0, w):
                for k0 in range(0, k_chunks, 4):
                    nk = min(4, k_chunks - k0)
                    parts = [(0, 2, w, chunks(W, k0, 2, c0, w)),
                             (2 * w, nk - 2, w, chunks(W, k0 + 2, nk - 2, c0, w))]
                    put(n[0], parts)
                    n[0] += 1

            def gate_up(Wg, Wu, row0, col, tile0, it):
                for h in range(2):
                    if tile0 + h >= RAW_SLOTS:
                        sp.wait_ge(s_lo, it * LOOP_UNITS + 2 * (tile0 + h - RAW_SLOTS) + 2)
                    slot = (tile0 + h) % RAW_SLOTS
                    for g, W in enumerate((Wg, Wu)):
                        dst = raw[:, slot, :].rearrange("p (k g n) -> p k g n", k=4, g=2)[:, :, g, :]
                        src = W[bass.ds(row0 + 512 * h, 512), bass.ds(col, FB)]
                        sp.dma_start(dst, src.rearrange("(k p) n -> p k n", p=P)).then_inc(s_raw[slot], 16)

            def down(Wd, row0, tile0, it):
                sp.wait_ge(s_lo, it * LOOP_UNITS + 2 * (tile0 - RAW_SLOTS) + 2)
                slot = tile0 % RAW_SLOTS
                for h in range(2):
                    sp.dma_start(raw[:, slot, 1024 * h:1024 * h + 1024],
                                 Wd[bass.ds(row0 + P * h, P), :]).then_inc(s_raw[slot], 16)

            def ffn(Wg, Wu, Wd, row_in, row_h, tile0, it0):
                gate_up(Wg, Wu, row_in, 0, tile0, it0)
                with sp.Fori(0, (NSTEP - 1) // 2) as i:
                    it = it0 + i
                    for j in range(2):
                        gate_up(Wg, Wu, row_in, i * (2 * FB) + FB * (j + 1), tile0 + 2 + 3 * j, it)
                        down(Wd, row_h + i * (2 * FB) + FB * j, tile0 + 4 + 3 * j, it)
                down(Wd, row_h + FB * (NSTEP - 1), tile0 + 3 * NSTEP - 1, it0)

            for L in range(DEPTH):
                w_in = A["w_in"][L]
                for b in range(3):
                    block(w_in, 8, W1C * b, W1C)
                for b in range(2):
                    block(A["mla_w_q_up"][L], 3, Q_LORA * b, Q_LORA)
                put(n[0], [(1024 * k, 1, 1024, chunks(A["mla_w_kv_up"][L], k, 1, 0, 1024)) for k in range(2)])
                n[0] += 1

                def gated(br):
                    for half in range(2):
                        block(w_in, 8, GATE0 + D * br + 512 * half, 512)
                        block(A["w_branch"][L, br], 4, 512 * half, 512)

                gated(0)
                gated(1)
                for b in range(3):
                    block(w_in, 8, N1 + W2C * b, W2C)
                gated(2)
                for name, cols in (("w_out", D), ("mem_wkv", 2 * D), ("mem_wq", D), ("mem_wo", D)):
                    for b in range(cols // 512):
                        block(A[name][L], 8, 512 * b, 512)
                if L == 0:
                    ffn(A["dense_w_gate"][0], A["dense_w_up"][0], A["dense_w_down"][0], 0, 0, n[0], 0)
                    n[0] += 3 * NSTEP
            Wg = A["moe_w_gate"][0].rearrange("e k n -> (e k) n")
            Wu = A["moe_w_up"][0].rearrange("e k n -> (e k) n")
            Wd = A["moe_w_down"][0].rearrange("e f n -> (e f) n")

            def experts(r):
                with sp.Fori(0, NE // 2) as pr:
                    it = sp.snap(pr * 11 + 11 * (NE // 2) * r)
                    for e in range(2):
                        ffn(Wg, Wu, Wd, pr * (2 * D) + D * e, pr * (2 * F) + F * e, n[0] + 3 * NSTEP * e, it)

            experts(0)
            sp.wait_ge(s_rounds, 1)
            nr = sp.value_load(rounds[0:1, 0:1], min_val=1, max_val=2)
            with sp.If(nr > 1):
                experts(1)
            sp.wait_ge(s_final, 1)
            sp.dma_start(A["out"][0].rearrange("(t p) d -> p t d", p=P), x[:, :, :]).then_inc(s_out, 16)
            sp.wait_ge(s_out, 16)

        @blk.gpsimd
        def _(pool):
            GAINS = ["mix_pre_g", "mem_norm_g", "mix_post_g", "mem_pre_g", "mem_post_g", "ffn_pre_g", "ffn_post_g"]
            order = [(g, L) for L in range(DEPTH) for g in GAINS]
            chain, requests, used = [0], [0], [0]

            def load_gain(k):
                g, L = order[k]
                nc.gpsimd.dma_start(gains[:, k % 2, :], A[g][L].partition_broadcast(P)).then_inc(s_gain[k % 2], 16)

            def load_small(L):
                for name, c in (("mla_q_norm_g", SG_Q), ("mla_kv_norm_g", SG_KV), ("gqa_q_norm_g", SG_GQ),
                                ("gqa_k_norm_g", SG_GK), ("diff_subln_g", SG_SUB), ("diff_lambda_q1", SG_LAM),
                                ("diff_lambda_k1", SG_LAM + 32), ("diff_lambda_q2", SG_LAM + 64),
                                ("diff_lambda_k2", SG_LAM + 96)):
                    w = A[name].shape[1]
                    nc.gpsimd.dma_start(sg[:, c:c + w], A[name][L].partition_broadcast(P)).then_inc(s_sg, 16)

            def step(ins):
                chain[0] += 1
                ins.then_inc(s_pool, 1)
                pool.wait_ge(s_pool, chain[0])

            def rsqrt(*parts):
                requests[0] += 1
                pool.wait_ge(s_ssq, requests[0])
                for c0, c1, n in parts:
                    step(nc.gpsimd.tensor_scalar(ms[:, c0:c1], ssq[:, c0:c1], 1.0 / n, EPS, ALU.mult, ALU.add))
                c0, c1 = parts[0][0], parts[-1][1]
                nc.gpsimd.tensor_tensor(rstd[:, c0:c1], ms[:, c0:c1], mhalf[:, c0:c1], ALU.pow).then_inc(s_rstd, 1)

            def norm():
                rsqrt((0, 2, D))
                used[0] += 1
                if used[0] + 1 < len(order):
                    pool.wait_ge(s_gain_used, used[0])
                    load_gain(used[0] + 1)

            load_gain(0)
            load_small(0)
            load_gain(1)
            step(nc.gpsimd.memset(mhalf[:, :], -0.5))
            for L in range(DEPTH):
                norm()
                rsqrt((0, 2, Q_LORA), (2, 4, KV_LORA))
                rsqrt((0, 20, HD))
                pool.wait_ge(s_rows, 5 * L + 3)
                nc.gpsimd.dma_start(ZU[:, :, 1024:2048], A["mem"][0].rearrange("(t p) d -> p t d", p=P)).then_inc(s_mem, 16)
                rsqrt((0, 16, DV))
                if L + 1 < DEPTH:
                    pool.wait_ge(s_rows, 5 * L + 5)
                    load_small(L + 1)
                norm()
                norm()
                norm()
                norm()
                norm()
                if L + 1 == DEPTH:
                    nc.gpsimd.dma_start(tri, A["consts"][2]).then_inc(s_tri, 16)
                    nc.gpsimd.dma_start(ones, A["consts"][3]).then_inc(s_tri, 16)
                norm()

        @blk.scalar
        def _(act):
            act.dma_start(rope[:, :, :], A["rope"].rearrange("(t p) c -> p t c", p=P)).then_inc(s_const, 16)
            act.dma_start(ident[:, :], A["consts"][0]).then_inc(s_const, 16)
            act.dma_start(iota[:, :], A["consts"][1]).then_inc(s_const, 16)
            act.dma_start(wr[:, :, :], A["moe_w_router"][0].rearrange("(k p) e -> p k e", p=P)).then_inc(s_const, 16)
            act.dma_start(brt[:, :], A["moe_b_router"][0].partition_broadcast(P)).then_inc(s_const, 16)
            act.wait_ge(s_const, 80)
            nc.scalar.activation(wr_hi[:, :, :], wr[:, :, :], ACT.Copy).then_inc(s_wr, 1)
            c = Counts()

            def advance(limit):
                while c.unit < limit:
                    act_split(act, c.unit)
                    c.unit += 1

            def acc_hi(dst):
                c.rdy += 1
                act.wait_ge(s_acc, c.rdy)
                nc.scalar.activation(dst, bank(c.acc, dst), ACT.Copy).then_inc(s_acc_hi, 1)
                c.acc += 1

            def bank(a, dst):
                w = 1
                for n in dst.shape[1:]:
                    w *= n
                v = ps[:, acc_bank(a), 0:w]
                return v.rearrange("p (k t) -> p k t", k=dst.shape[1]) if len(dst.shape) == 3 else v

            def pt_copy(dst, scale=1.0):
                act.wait_ge(s_pt, c.pt + 1)
                rows = dst.shape[0]
                src = ps[0:rows, 2 + c.pt % 2, 0:512].rearrange("p (h t) -> p h t", h=2) if len(dst.shape) == 3 \
                    else ps[0:rows, 2 + c.pt % 2, 0:dst.shape[1]]
                nc.scalar.activation(dst, src, ACT.Copy, scale=scale).then_inc(s_pt_copied, 1)
                c.pt += 1

            def attention(n, diff=False):
                pt_of, first = {}, c.sc
                for s in range(n + 1):
                    if s < n:
                        u = c.sc
                        act.wait_ge(s_max, u + 1)
                        if s >= 2 and not diff:
                            act.wait_ge(s_pt, pt_of[s - 2] + 1)
                        if s >= 2 and diff:
                            act.wait_ge(s_comb, c.comb + s - 1)
                        for hh in range(2):
                            ins = nc.scalar.activation(Pr[:, u % 2, 256 * hh:256 * hh + 256],
                                                       ps[:, u % 2, 256 * hh:256 * hh + 256], ACT.Exp,
                                                       bias=nmax[:, u % 4, hh:hh + 1],
                                                       accum_out=sums[:, u % 4, hh:hh + 1])
                        ins.then_inc(s_p, 1)
                        c.sc += 1
                    if s >= 1:
                        pt_of[s - 1] = c.pt
                        v = (first + s - 1) % 2
                        pt_copy(PT[:, v, 0:256] if diff else PT[:, v, :])
                if diff:
                    c.comb += n

            def transposed(hi, k0, widths):
                for w in widths:
                    acc_hi(hi[:, k0:k0 + w, :])
                    k0 += w

            def gated():
                for half in range(2):
                    assert c.acc % 4 == 0
                    advance(c.done + 4)
                    c.done += 6
                    advance(c.done + 2)
                    act.wait_ge(s_used, c.done - 2)
                    if half:
                        act.wait_ge(s_acc_free, c.acc)
                    nc.scalar.activation(E4[:, :, :], ps[:, 4:6, :], ACT.Exp, scale=-1.0).then_inc(s_gexp, 1)
                    c.acc += 4
                    c.gates += 1
                    advance(c.done + 4)

            def linear(blocks, units, accs=2):
                for b in range(blocks):
                    c.done += units
                    advance(c.done + 4)
                    c.acc += accs

            def skip_attention(n):
                c.acc += n
                c.rdy += n

            def ffn(step0, u0, it0, nt):
                def silu(j, k, it, last):
                    act.wait_ge(s_used, it * LOOP_UNITS + last)
                    if not (step0 + j == 0):
                        act.wait_ge(s_hid, it * 2 + (step0 + j))
                    src = ps[:, 4:6, 0:FB] if nt == 2 else ps[:, 4 + k, 0:FB]
                    dst = sl[:, :].rearrange("p (t n) -> p t n", t=2) if nt == 2 else sl[:, 0:FB]
                    nc.scalar.activation(dst, src, ACT.Silu).then_inc(s_silu, 1)

                def hidT(j, par, it):
                    act.wait_ge(s_hidT, it * 2 + (step0 + j + 1))
                    nc.scalar.activation(hidT_hi[:, :, 0:P * nt],
                                         ps[:, 6 + par, 0:2 * P * nt].rearrange("p (k t) -> p k t", k=2),
                                         ACT.Copy).then_inc(s_hidT_hi, 1)

                for k in (2, 3):
                    act_split(act, u0 + k, it0)
                silu(0, 0, it0, u0 + 4)
                for k in (4, 5):
                    act_split(act, u0 + k, it0)
                with act.Fori(0, (NSTEP - 1) // 2) as i:
                    it = it0 + i
                    for j in range(2):
                        u = u0 + 4 + 6 * j
                        for k in (2, 3):
                            act_split(act, u + k, it)
                        hidT(j, j, it)
                        for k in (4, 5):
                            act_split(act, u + k, it)
                        silu(j + 1, (j + 1) % 2, it, u + 4)
                        for k in (6, 7):
                            act_split(act, u + k, it)

            def ffn_tail(step0, it0, nt):
                act.wait_ge(s_hidT, it0 * 2 + (step0 + NSTEP))
                nc.scalar.activation(hidT_hi[:, :, 0:P * nt],
                                     ps[:, 6, 0:2 * P * nt].rearrange("p (k t) -> p k t", k=2),
                                     ACT.Copy).then_inc(s_hidT_hi, 1)

            advance(4)
            for L in range(DEPTH):
                transposed(hT_hi, 0, (2, 2, 2, 2))
                linear(3, 4)
                if L == 0:
                    act.wait_ge(s_lamq, 1)
                else:
                    act.wait_ge(s_lamq, 2)
                nc.scalar.activation(lam[:, 2:4], lam[:, 0:2], ACT.Exp).then_inc(s_lame, 1)
                transposed(oT_hi, 0, (1, 1, 1, 2))
                linear(2, 2)
                linear(1, 2, 4)
                for h in range(0, MLA_H, 2):
                    pt_copy(qT[0:QK_MLA, h:h + 2, :], QK_MLA ** -0.5)
                for h in range(0, MLA_H, 2):
                    pt_copy(kT[0:QK_MLA, h:h + 2, :])
                attention(8)
                skip_attention(8)
                transposed(oT_hi, 0, (2, 2))
                gated()
                for h in range(0, GQA_QH, 2):
                    pt_copy(qT[0:HD, h:h + 2, :], HD ** -0.5)
                pt_copy(kT[0:HD, 0:2, :])
                attention(8)
                skip_attention(8)
                transposed(oT_hi, 0, (1, 1, 1, 1))
                gated()
                linear(3, 4)
                for g in range(2):
                    for h in range(0, 8, 2):
                        pt_copy(qT[0:DQK, h:h + 2, :], DQK ** -0.5)
                    for h in range(0, 8, 2):
                        pt_copy(kT[0:DQK, h:h + 2, :])
                    attention(8, diff=True)
                    skip_attention(8)
                transposed(oT_hi, 0, (2, 2))
                gated()
                transposed(hT_hi, 0, (2, 2, 2, 2))
                linear(2, 4)
                transposed(oT_hi, 0, (2, 2, 2, 2))
                linear(4, 4)
                for h in range(0, 8, 2):
                    pt_copy(kT[:, h:h + 2, :])
                transposed(hT_hi, 0, (2, 2, 2, 2))
                linear(2, 4)
                for h in range(0, 8, 2):
                    pt_copy(qT[:, h:h + 2, :], MEM_HD ** -0.5)
                attention(4)
                skip_attention(4)
                transposed(hT_hi, 0, (2, 2, 2, 2))
                c.done += 4
                advance(c.done + 4)
                c.done += 4
                advance(c.done + (2 if L == 0 else 0))
                c.acc += 4
                transposed(hT_hi, 0, (2, 2, 2, 2))
                if L == 0:
                    ffn(0, FFN0[0], 0, NT)
                    ffn_tail(0, 0, NT)
                    c.unit = c.done = LAYER0[1]
                    advance(c.done + 4)
            act.wait_ge(s_acc, c.rdy + 1)
            hrow = hT_hi[:, :, :].rearrange("p (t a) b -> p t (a b)", t=NT)
            nc.scalar.activation(hrow, ZU[:, :, 0:D], ACT.Copy).then_inc(s_hrow_hi, 1)
            act.wait_ge(s_topd, 1)
            nc.scalar.activation(EX, W1, ACT.Exp).then_inc(s_tope, 1)
            act.wait_ge(s_rounds, 1)
            nr = act.value_load(rounds[0:1, 0:1], min_val=1, max_val=2)

            def gather_hi(e, q):
                act.wait_ge(s_gath, q * 2 + (e + 1))
                nc.scalar.activation(ohT[:, e, :], ps[:, 7, 0:SEQ], ACT.Copy).then_inc(s_ohT, 1)
                nc.scalar.activation(oT_hi[:, :, 0:P],
                                     ps[:, 2 * e:2 * e + 2, :].rearrange("p b (k s) -> p (b k) s", k=4),
                                     ACT.Copy).then_inc(s_gath_hi, 1)

            def y_hi(e, q):
                act.wait_ge(s_used, q * (11 * LOOP_UNITS) + (FFN0[1] + FFN_UNITS * (e + 1)))
                nc.scalar.activation(oT_hi[:, :, P:2 * P],
                                     ps[:, 2 * e:2 * e + 2, :].rearrange("p b (k s) -> p (b k) s", k=4),
                                     ACT.Copy).then_inc(s_yhi, 1)

            with act.Fori(0, nr) as r:
                with act.Fori(0, NE // 2) as pr:
                    q = act.snap(r * (NE // 2) + pr)
                    it = act.snap(q * 11)
                    u0, st = FFN0[1], NSTEP
                    for k in (0, 1):
                        act_split(act, u0 + k, it)
                    gather_hi(0, q)
                    ffn(st, u0, it, 1)
                    gather_hi(1, q)
                    ffn_tail(st, it, 1)
                    for k in (0, 1):
                        act_split(act, u0 + FFN_UNITS + k, it)
                    y_hi(0, q)
                    ffn(st + NSTEP, u0 + FFN_UNITS, it, 1)
                    ffn_tail(st + NSTEP, it, 1)
                    y_hi(1, q)

        @blk.vector
        def _(dve):
            V = nc.vector
            c = Counts()

            def link(ins):
                c.chain += 1
                ins.then_inc(s_chain, 1)
                dve.wait_ge(s_chain, c.chain)

            def advance(limit):
                while c.unit < limit:
                    dve_split(dve, c.unit)
                    c.unit += 1

            def rows_done(ins):
                c.rows += 1
                ins.then_inc(s_rows, 1)

            def transposed(lo, hi, k0, widths):
                for w in widths:
                    dve.wait_ge(s_acc_hi, c.acc_hi + 1)
                    src = ps[:, acc_bank(c.acc), 0:w * SEQ].rearrange("p (k t) -> p k t", k=w)
                    V.tensor_tensor(lo[:, k0:k0 + w, :], src, hi[:, k0:k0 + w, :].bitcast(f32),
                                    ALU.subtract).then_inc(s_acc_free, 1)
                    c.acc += 1
                    c.rdy += 1
                    c.acc_hi += 1
                    k0 += w

            def evac(dst, w):
                V.tensor_copy(dst, ps[:, acc_bank(c.acc), 0:w]).then_inc(s_acc_free, 1)
                c.acc += 1

            def linear(blocks, units, dst, w):
                for b in range(blocks):
                    c.done += units
                    advance(c.done + 4)
                    dve.wait_ge(s_used, c.done)
                    for t in range(NT):
                        evac(dst(b, t), w)

            def own_rows():
                dve.wait_ge(s_acc_free, c.acc)

            def sum_squares(src, parts):
                if c.acc:
                    own_rows()
                last = len(parts) * NT - 1
                n = at = 0
                for c0, c1, s in parts:
                    for t in range(NT):
                        ins = V.tensor_tensor_reduce(out=scratch[:, at:at + c1 - c0], in0=src[:, t, c0:c1],
                                                     in1=src[:, t, c0:c1], scale=1.0, scalar=0.0, op0=ALU.mult,
                                                     op1=ALU.add, accum_out=ssq[:, s + t:s + t + 1])
                        if n == last:
                            ins.then_inc(s_ssq, 1)
                        n += 1
                        at += c1 - c0
                c.norm += 1
                dve.wait_ge(s_rstd, c.norm)

            def wait_gain():
                k = c.gain
                dve.wait_ge(s_gain[k % 2], 16 * (k // 2 + 1))
                c.gain += 1
                return k % 2

            def pre_norm(src, dst):
                sum_squares(src, [(0, D, 0)])
                g = wait_gain()
                for t in range(NT):
                    ins = V.scalar_tensor_tensor(dst[:, t, :], src[:, t, :], rstd[:, t:t + 1], gains[:, g, :],
                                                 ALU.mult, ALU.mult)
                ins.then_inc(s_gain_used, 1)

            def post_norm(done=None):
                sum_squares(S1, [(0, D, 0)])
                g = wait_gain()
                for t in range(NT):
                    ins = V.scalar_tensor_tensor(scratch[:, D * t:D * t + D], S1[:, t, :], rstd[:, t:t + 1],
                                                 gains[:, g, :], ALU.mult, ALU.mult)
                ins.then_inc(s_gain_used, 1)
                dve.wait_ge(s_gain_used, c.gain)
                ins = V.tensor_tensor(x[:, :, :], x[:, :, :], scratch[:, 0:NT * D].rearrange("p (t d) -> p t d", t=NT),
                                      ALU.add)
                if done is None:
                    link(ins)
                else:
                    ins.then_inc(done, 1)

            def rotate(view, dst, cos0, sin0, heads, half):
                n = heads * 2 * half
                own_rows()
                for t in range(NT):
                    v = view(t)
                    a = scratch[:, 0:n].rearrange("p (h a d) -> p h a d", h=heads, a=2)
                    b = scratch[:, n:2 * n].rearrange("p (h a d) -> p h a d", h=heads, a=2)
                    co = rope[:, t, cos0:cos0 + half].unsqueeze(1).unsqueeze(1).broadcast_to([P, heads, 2, half])
                    si = rope[:, t, sin0:sin0 + half].unsqueeze(1).unsqueeze(1).broadcast_to([P, heads, 2, half])
                    V.tensor_tensor(a, v, co, ALU.mult)
                    link(V.tensor_tensor(b, v, si, ALU.mult))
                    d = dst(t)
                    V.tensor_tensor(d[0], a[:, :, 0, :], b[:, :, 1, :], ALU.subtract)
                    ins = V.tensor_tensor(d[1], a[:, :, 1, :], b[:, :, 0, :], ALU.add)
                    if t + 1 < NT:
                        link(ins)
                return ins

            def attention(n, out, hd, diff=False):
                u0 = c.sc
                for s in range(n + 2):
                    if s < n:
                        u = u0 + s
                        dve.wait_ge(s_sc, u + 1)
                        V.tensor_reduce(nmax[:, u % 4, :], ps[:, u % 2, :].rearrange("p (h k) -> p h k", h=2), AX,
                                        ALU.max, negate=True).then_inc(s_max, 1)
                    if 1 <= s <= n:
                        u = u0 + s - 1
                        dve.wait_ge(s_p, u + 1)
                        link(V.reciprocal(rsum[:, u % 4, :], sums[:, u % 4, :]))
                        if diff:
                            link(V.tensor_tensor(rsum[:, u % 4, 1:2], rsum[:, u % 4, 1:2], nlam[:, :], ALU.mult))
                            if s >= 3:
                                dve.wait_ge(s_pt, c.pt + s - 2)
                            link(V.tensor_scalar(Ad[:, u % 2, :], Pr[:, u % 2, 256:512], rsum[:, u % 4, 1:2], None,
                                                 ALU.mult))
                            V.scalar_tensor_tensor(Ad[:, u % 2, :], Pr[:, u % 2, 0:256], rsum[:, u % 4, 0:1],
                                                   Ad[:, u % 2, :], ALU.mult, ALU.add).then_inc(s_comb, 1)
                    if s >= 2:
                        u = u0 + s - 2
                        c.rdy += 1
                        dve.wait_ge(s_acc, c.rdy)
                        dst = out(s - 2)
                        if diff:
                            V.tensor_copy(dst, ps[:, acc_bank(c.acc), 0:hd]).then_inc(s_acc_free, 1)
                        else:
                            src = ps[:, acc_bank(c.acc), 0:2 * hd].rearrange("p (h d) -> p h d", h=2)
                            V.tensor_tensor(dst, src, rsum[:, u % 4, :].unsqueeze(2).broadcast_to([P, 2, hd]),
                                            ALU.mult).then_inc(s_acc_free, 1)
                        c.acc += 1
                c.sc += n
                c.pt += n

            def gated(br):
                for half in range(2):
                    advance(c.done + 4)
                    c.done += 6
                    advance(c.done + 2)
                    dve.wait_ge(s_gexp, c.gates + 1)
                    link(V.tensor_scalar(E4[:, :, :], E4[:, :, :], 1.0, None, ALU.add))
                    link(V.reciprocal(E4[:, :, :], E4[:, :, :]))
                    advance(c.done + 4)
                    dve.wait_ge(s_used, c.done)
                    m = S1[:, :, 512 * half:512 * half + 512]
                    if br == 0:
                        V.tensor_tensor(m, E4[:, :, :], ps[:, 6:8, :], ALU.mult).then_inc(s_acc_free, 4)
                    else:
                        link(V.tensor_tensor(E4[:, :, :], E4[:, :, :], ps[:, 6:8, :], ALU.mult))
                        V.tensor_tensor(m, m, E4[:, :, :], ALU.add).then_inc(s_acc_free, 4)
                    c.acc += 4
                    c.gates += 1

            def ffn(step0, u0, it0, nt, between=None):
                def hidden(j, k, it):
                    dve.wait_ge(s_silu, it * 2 + (step0 + j + 1))
                    if not (step0 + j == 0):
                        dve.wait_ge(s_hidT, it * 2 + (step0 + j))
                    up = ps[:, 4:6, FB:2 * FB] if nt == 2 else ps[:, 4 + k, FB:2 * FB]
                    a = sl[:, :].rearrange("p (t n) -> p t n", t=2) if nt == 2 else sl[:, 0:FB]
                    h = hid[:, :].rearrange("p (t n) -> p t n", t=2) if nt == 2 else hid[:, 0:FB]
                    V.tensor_tensor(h, a, up, ALU.mult).then_inc(s_hid, 1)

                for k in (2, 3):
                    dve_split(dve, u0 + k, it0)
                hidden(0, 0, it0)
                if between is not None:
                    between()
                for k in (4, 5):
                    dve_split(dve, u0 + k, it0)
                with dve.Fori(0, (NSTEP - 1) // 2) as i:
                    it = it0 + i
                    for j in range(2):
                        u = u0 + 4 + 6 * j
                        for k in (2, 3):
                            dve_split(dve, u + k, it)
                        hidT(step0, j, j, it, nt)
                        for k in (4, 5):
                            dve_split(dve, u + k, it)
                        hidden(j + 1, (j + 1) % 2, it)
                        for k in (6, 7):
                            dve_split(dve, u + k, it)

            def hidT(step0, j, par, it, nt):
                dve.wait_ge(s_hidT_hi, it * 2 + (step0 + j + 1))
                V.tensor_tensor(hidT_lo[:, :, 0:P * nt],
                                ps[:, 6 + par, 0:2 * P * nt].rearrange("p (k t) -> p k t", k=2),
                                hidT_hi[:, :, 0:P * nt].bitcast(f32), ALU.subtract).then_inc(s_hidT_lo, 1)

            dve.wait_ge(s_x, 16)
            for L in range(DEPTH):
                pre_norm(x, ZU[:, :, 0:D])
                if L == 0:
                    dve.wait_ge(s_wr, 1)
                    V.tensor_tensor(wr_lo[:, :, :], wr[:, :, :], wr_hi[:, :, :].bitcast(f32),
                                    ALU.subtract).then_inc(s_wrl, 1)
                dve.wait_ge(s_sg, 16 * 9 * (L + 1))
                lq = sg[:, SG_LAM:SG_LAM + 128].rearrange("p (m a d) -> p m a d", m=2, a=2)
                lp = scratch[:, 0:64].rearrange("p (m d) -> p m d", m=2)
                link(V.tensor_tensor(lp, lq[:, :, 0, :], lq[:, :, 1, :], ALU.mult))
                V.tensor_reduce(lam[:, 0:2], lp, AX, ALU.add).then_inc(s_lamq, 1)
                advance(c.done + 4)
                transposed(hT_lo, hT_hi, 0, (2, 2, 2, 2))
                linear(3, 4, lambda b, t: Z[:, t, W1C * b:W1C * b + W1C], W1C)
                dve.wait_ge(s_lame, L + 1)
                link(V.tensor_tensor(nlam[:, :], lam[:, 3:4], lam[:, 2:3], ALU.subtract))
                link(V.tensor_scalar(nlam[:, :], nlam[:, :], -LAMBDA_INIT[L], None, ALU.add))
                sum_squares(Z, [(0, Q_LORA, 0), (Q_LORA, C_ROPE, 2)])
                for t in range(NT):
                    for c0, c1, s, g in ((0, Q_LORA, 0, SG_Q), (Q_LORA, C_ROPE, 2, SG_KV)):
                        ins = V.scalar_tensor_tensor(Z[:, t, c0:c1], Z[:, t, c0:c1], rstd[:, s + t:s + t + 1],
                                                     sg[:, g:g + c1 - c0], ALU.mult, ALU.mult)
                rows_done(ins)
                transposed(oT_lo, oT_hi, 0, (1, 1, 1, 2))
                linear(2, 2, lambda b, t: ZU[:, t, Q_LORA * b:Q_LORA * b + Q_LORA], Q_LORA)
                KF = ZU[:, :, 768:1536].rearrange("p t (h d) -> p t h d", d=QK_MLA)
                VM = ZU[:, :, 1536:2048]
                c.done += 2
                advance(c.done + 4)
                dve.wait_ge(s_used, c.done)
                for n in range(4):
                    t, hf = n // 2, n % 2
                    kv = ps[:, acc_bank(c.acc), :].rearrange("p (h a d) -> p h a d", h=4, a=2)
                    V.tensor_copy(KF[:, t, 4 * hf:4 * hf + 4, 0:NOPE], kv[:, :, 0, :])
                    V.tensor_copy(VM[:, t, 256 * hf:256 * hf + 256].rearrange("p (h d) -> p h d", h=4),
                                  kv[:, :, 1, :]).then_inc(s_acc_free, 1)
                    c.acc += 1
                Q = ZU[:, :, 0:768].rearrange("p t (h d) -> p t h d", d=QK_MLA)
                link(rotate(lambda t: Q[:, t, :, NOPE:].rearrange("p h (a d) -> p h a d", a=2),
                       lambda t: (Q[:, t, :, NOPE:NOPE + 16], Q[:, t, :, NOPE + 16:]), RC_M, RS_M, MLA_H, 16))
                KR = Z[:, :, C_ROPE:C_ROPE + ROT]
                link(rotate(lambda t: KR[:, t, :].rearrange("p (h a d) -> p h a d", h=1, a=2),
                       lambda t: (KR[:, t, 0:16].unsqueeze(1), KR[:, t, 16:32].unsqueeze(1)), RC_M, RS_M, 1, 16))
                for t in range(NT):
                    ins = V.tensor_copy(KF[:, t, :, NOPE:], KR[:, t, :].unsqueeze(1).broadcast_to([P, MLA_H, ROT]))
                rows_done(ins)
                O = ZU[:, :, 0:BW]

                def out_pair(n):
                    return O[:, n % 2, P * (n // 2):P * (n // 2) + P].rearrange("p (h d) -> p h d", h=2)

                c.pt += 8
                attention(8, out_pair, HD)
                QKH = GQA_QH + GQA_KVH
                G = Z[:, :, C_GQA:C_GQA + QKH * HD]
                transposed(oT_lo, oT_hi, 0, (2, 2))
                gated(0)
                own_rows()
                for t in range(NT):
                    sq = scratch[:, QKH * HD * t:QKH * HD * (t + 1)]
                    link(V.tensor_tensor(sq, G[:, t, :], G[:, t, :], ALU.mult))
                    ins = V.tensor_reduce(ssq[:, QKH * t:QKH * t + QKH],
                                          sq.rearrange("p (h d) -> p h d", d=HD), AX, ALU.add)
                ins.then_inc(s_ssq, 1)
                c.norm += 1
                dve.wait_ge(s_rstd, c.norm)
                for t in range(NT):
                    v = G[:, t, :].rearrange("p (h d) -> p h d", d=HD)
                    link(V.tensor_tensor(v, v, rstd[:, QKH * t:QKH * t + QKH].unsqueeze(2).broadcast_to([P, QKH, HD]),
                                         ALU.mult))
                    V.tensor_tensor(v[:, 0:GQA_QH, :], v[:, 0:GQA_QH, :],
                                    sg[:, SG_GQ:SG_GQ + HD].unsqueeze(1).broadcast_to([P, GQA_QH, HD]), ALU.mult)
                    link(V.tensor_tensor(v[:, GQA_QH:, :], v[:, GQA_QH:, :],
                                         sg[:, SG_GK:SG_GK + HD].unsqueeze(1).broadcast_to([P, GQA_KVH, HD]), ALU.mult))
                G4 = G.rearrange("p t (h a d) -> p t h a d", a=2, d=HD // 2)
                rows_done(rotate(lambda t: G4[:, t], lambda t: (G4[:, t, :, 0, :], G4[:, t, :, 1, :]), RC_A, RS_A,
                                 QKH, HD // 2))
                c.pt += 5
                attention(8, out_pair, HD)
                transposed(oT_lo, oT_hi, 0, (1, 1, 1, 1))
                gated(1)
                linear(3, 4, lambda b, t: Z[:, t, W2C * b:W2C * b + W2C], W2C)
                R = Z[:, :, 0:1024].rearrange("p t (h d) -> p t h d", d=DQK)
                rows_done(rotate(lambda t: R[:, t, :, 0:DROT].rearrange("p h (a d) -> p h a d", a=2),
                                 lambda t: (R[:, t, :, 0:4], R[:, t, :, 4:8]), RC_P, RS_P, 32, 4))
                for g in range(2):
                    c.pt += 8
                    attention(8, lambda n: O[:, n % 2, HD * (4 * g + n // 2):HD * (4 * g + n // 2) + HD], HD, diff=True)
                own_rows()
                for t in range(NT):
                    sq = scratch[:, BW * t:BW * t + BW]
                    link(V.tensor_tensor(sq, O[:, t, :], O[:, t, :], ALU.mult))
                    ins = V.tensor_reduce(ssq[:, 8 * t:8 * t + 8], sq.rearrange("p (h d) -> p h d", d=DV),
                                          AX, ALU.add)
                ins.then_inc(s_ssq, 1)
                c.norm += 1
                dve.wait_ge(s_rstd, c.norm)
                for t in range(NT):
                    v = O[:, t, :].rearrange("p (h d) -> p h d", d=DV)
                    link(V.tensor_tensor(v, v, rstd[:, 8 * t:8 * t + 8].unsqueeze(2).broadcast_to([P, DIFF_H, DV]),
                                         ALU.mult))
                    link(V.tensor_tensor(v, v, sg[:, SG_SUB:SG_SUB + DV].unsqueeze(1).broadcast_to([P, DIFF_H, DV]),
                                         ALU.mult))
                rows_done(V.tensor_scalar(O, O, 1.0 - LAMBDA_INIT[L], None, ALU.mult))
                transposed(oT_lo, oT_hi, 0, (2, 2))
                gated(2)
                transposed(hT_lo, hT_hi, 0, (2, 2, 2, 2))
                dve.wait_ge(s_mem, 16 * (L + 1))
                MR = ZU[:, :, 1024:2048]
                pre_norm(MR, MR)
                linear(2, 4, lambda b, t: S1[:, t, 512 * b:512 * b + 512], 512)
                transposed(oT_lo, oT_hi, 0, (2, 2, 2, 2))
                post_norm()
                pre_norm(x, ZU[:, :, 0:D])
                linear(4, 4, lambda b, t: (ZU[:, t, 1024 + 512 * b:1536 + 512 * b] if b < 2 else
                                           Z[:, t, 512 * (b - 2):512 * (b - 2) + 512]), 512)
                c.pt += 4
                transposed(hT_lo, hT_hi, 0, (2, 2, 2, 2))
                linear(2, 4, lambda b, t: ZU[:, t, 512 * b:512 * b + 512], 512)
                c.pt += 4
                attention(4, lambda n: S1[:, n % 2, 512 * (n // 2):512 * (n // 2) + 512]
                          .rearrange("p (h d) -> p h d", h=2), MEM_HD)
                transposed(hT_lo, hT_hi, 0, (2, 2, 2, 2))
                for b in range(2):
                    c.done += 4
                    advance(c.done + (4 if b == 0 else 2 if L == 0 else 0))
                    dve.wait_ge(s_used, c.done)
                    for t in range(NT):
                        evac(S1[:, t, 512 * b:512 * b + 512], 512)
                post_norm()
                pre_norm(x, ZU[:, :, 0:D])
                transposed(hT_lo, hT_hi, 0, (2, 2, 2, 2))
                if L == 0:
                    ffn(0, FFN0[0], 0, NT)
                    hidT(0, NSTEP - 1, 0, 0, NT)
                    dve.wait_ge(s_used, FFN0[0] + FFN_UNITS)
                    for t in range(NT):
                        ins = V.tensor_copy(S1[:, t, :], ps[:, 2 * t:2 * t + 2, :].rearrange("p b n -> p (b n)"))
                    link(ins)
                    post_norm()
                    c.unit = c.done = LAYER0[1]
            hrow_lo = hT_lo[:, :, :].rearrange("p (t a) b -> p t (a b)", t=NT)
            hrow_hi = hT_hi[:, :, :].rearrange("p (t a) b -> p t (a b)", t=NT)

            def bc(v):
                return v.unsqueeze(2).broadcast_to([P, NT, NE])

            io8 = iota[:, 0:NE].unsqueeze(1).broadcast_to([P, NT, NE])

            def first_max(src, m, onehot):
                link(V.tensor_reduce(m, src, AX, ALU.max))
                link(V.tensor_tensor(EQ, src, bc(m), ALU.is_equal))
                link(V.tensor_scalar(CC, EQ, -99.0, 99.0, ALU.mult, ALU.add))
                link(V.tensor_tensor(CC, CC, io8, ALU.add))
                link(V.tensor_reduce(I1, CC, AX, ALU.min))
                link(V.tensor_tensor(onehot, CC, bc(I1), ALU.is_equal))

            dve.wait_ge(s_acc, c.rdy + 1)
            lg = ps[:, acc_bank(c.acc), 0:16].rearrange("p (t e) -> p t e", t=NT)
            link(V.tensor_tensor(LG, lg, brt[:, :].unsqueeze(1).broadcast_to([P, NT, NE]), ALU.add))
            first_max(LG, M1, OH1)
            link(V.tensor_scalar(L2, OH1, -3.0e38, None, ALU.mult))
            link(V.tensor_tensor(L2, L2, LG, ALU.add))
            first_max(L2, M2, OH2)
            V.tensor_tensor(W1, M2, M1, ALU.subtract).then_inc(s_topd, 1)
            rows_done(V.tensor_tensor(MASK, OH1, OH2, ALU.add))
            dve.wait_ge(s_hrow_hi, 1)
            V.tensor_tensor(hrow_lo, ZU[:, :, 0:D], hrow_hi.bitcast(f32), ALU.subtract).then_inc(s_hrow, 1)
            dve.wait_ge(s_tope, 1)
            link(V.tensor_scalar(W1, EX, 1.0, None, ALU.add))
            link(V.reciprocal(W1, W1))
            link(V.tensor_tensor(W2, EX, W1, ALU.mult))
            link(V.tensor_tensor(OH1, OH1, bc(W1), ALU.mult))
            link(V.tensor_tensor(OH2, OH2, bc(W2), ALU.mult))
            link(V.tensor_tensor(GATE, OH1, OH2, ALU.add))
            V.memset(S1[:, :, :], 0.0).then_inc(s_added, 1)
            dve.wait_ge(s_rows, c.rows)
            dve.wait_ge(s_acc, c.rdy + 2)
            rk = ps[:, acc_bank(c.acc + 1), 0:16].rearrange("p (t e) -> p t e", t=NT)
            link(V.tensor_scalar(RANKM, MASK, -1000.0, 1000.0, ALU.mult, ALU.add))
            V.tensor_tensor(RANKM, RANKM, rk, ALU.add).then_inc(s_rank, 1)
            link(V.tensor_reduce(MX, ps[:, acc_bank(c.acc + 1), 16:24], AX, ALU.max))
            link(V.tensor_scalar(NR, MX, float(P), 1.0, ALU.is_gt, ALU.add))
            V.tensor_copy(rounds[:, :], NR).then_inc(s_rounds, 1)
            dve.wait_ge(s_rounds, 1)
            nr = dve.value_load(rounds[0:1, 0:1], min_val=1, max_val=2)

            def one_hot(e, q, pr, r):
                if e == 0:
                    dve.wait_ge(s_rank, r + 1)
                else:
                    dve.wait_ge(s_gath, q * 2 + 1)
                for t in range(NT):
                    ins = V.tensor_scalar(oh[:, t, :], iota[:, :], RANKM[:, t, bass.ds(pr * 2 + e, 1)], None, ALU.is_equal)
                ins.then_inc(s_oh, 1)

            def banks(e):
                return ps[:, 2 * e:2 * e + 2, :].rearrange("p b (k s) -> p (b k) s", k=4)

            def gather_lo(e, q):
                dve.wait_ge(s_gath_hi, q * 2 + (e + 1))
                V.tensor_tensor(oT_lo[:, :, 0:P], banks(e), oT_hi[:, :, 0:P].bitcast(f32),
                                ALU.subtract).then_inc(s_gath_lo, 1)

            def y_lo(e, q):
                dve.wait_ge(s_yhi, q * 2 + (e + 1))
                V.tensor_tensor(oT_lo[:, :, P:2 * P], banks(e), oT_hi[:, :, P:2 * P].bitcast(f32),
                                ALU.subtract).then_inc(s_ylo, 1)

            def add_scattered(e, q, pr):
                for n in range(4):
                    t, hf = n // 2, n % 2
                    dve.wait_ge(s_scat, q * 8 + (4 * e + n + 1))
                    if n == 0:
                        dve.wait_ge(s_added, q * 8 + (4 * e + 1))
                    bk = (2 * e, 2 * e + 1, 6, 7)[n]
                    dst = S1[:, t, 512 * hf:512 * hf + 512]
                    V.scalar_tensor_tensor(dst, ps[:, bk, :], GATE[:, t, bass.ds(pr * 2 + e, 1)], dst,
                                           ALU.mult, ALU.add).then_inc(s_added, 1)

            with dve.Fori(0, nr) as r:
                with dve.Fori(0, NE // 2) as pr:
                    q = dve.snap(r * (NE // 2) + pr)
                    it = dve.snap(q * 11)
                    u0, st = FFN0[1], NSTEP
                    one_hot(0, q, pr, r)
                    for k in (0, 1):
                        dve_split(dve, u0 + k, it)
                    gather_lo(0, q)
                    one_hot(1, q, pr, r)
                    ffn(st, u0, it, 1)
                    gather_lo(1, q)
                    hidT(st, NSTEP - 1, 0, it, 1)
                    for k in (0, 1):
                        dve_split(dve, u0 + FFN_UNITS + k, it)
                    y_lo(0, q)
                    ffn(st + NSTEP, u0 + FFN_UNITS, it, 1, between=lambda: add_scattered(0, q, pr))
                    hidT(st + NSTEP, NSTEP - 1, 0, it, 1)
                    y_lo(1, q)
                    add_scattered(1, q, pr)
                V.tensor_scalar(RANKM, RANKM, -float(P), None, ALU.add).then_inc(s_rank, 1)
            dve.wait_ge(s_added, nr * (4 * NE) + 1)
            post_norm(s_final)

        @blk.tensor
        def _(pe):
            T = nc.tensor
            c = Counts()

            def three(out, a_hi, a_lo, b_hi, b_lo, start, stop):
                T.matmul(out, a_hi, b_hi, start=start, stop=False)
                T.matmul(out, a_hi, b_lo, start=False, stop=False)
                return T.matmul(out, a_lo, b_hi, start=False, stop=stop)

            def unit(us, it, nk, w, k0, act, outs, first, last):
                pe.wait_ge(s_lo, it * LOOP_UNITS + (us + 1))
                a_hi, a_lo = act
                for k in range(nk):
                    for a, bk, c0, n in outs:
                        col = k * w + c0
                        b_hi = w_hi[:, hi_slot(us), col:col + n]
                        b_lo = w_lo[:, hi_slot(us), col:col + n]
                        ins = three(ps[:, bk, 0:n], a(a_hi, k0 + k), a(a_lo, k0 + k), b_hi, b_lo,
                                    first and k == 0, last and k == nk - 1)
                ins.then_inc(s_used, 1)

            def tok(t):
                return lambda src, k: src[:, k, P * t:P * t + P]

            def claim(n):
                if c.acc + n > 4:
                    pe.wait_ge(s_acc_free, c.acc + n - 4)

            def block(w, nks, act):
                claim(2)
                outs = [(tok(t), acc_bank(c.acc + t), 0, w) for t in range(NT)]
                k0 = 0
                for n, nk in enumerate(nks):
                    unit(c.done, 0, nk, w, k0, act, outs, n == 0, n == len(nks) - 1)
                    c.done += 1
                    k0 += nk
                c.acc += 2

            def split_T(src, widths):
                k = 0
                for w in widths:
                    claim(1)
                    for n in range(w * NT):
                        kk, t = k + n // NT, n % NT
                        ins = T.transpose(ps[:, acc_bank(c.acc), P * n:P * n + P], src(t)[:, P * kk:P * kk + P],
                                          ident[:, :])
                    ins.then_inc(s_acc, 1)
                    c.acc += 1
                    c.rdy += 1
                    k += w

            def split_ready():
                pe.wait_ge(s_acc_free, c.acc)

            def plain_T(cols, heads, width):
                for h in range(0, heads, 2):
                    if c.pt >= 2:
                        pe.wait_ge(s_pt_copied, c.pt - 1)
                    for n in range(4):
                        hh, t = h + n // 2, n % 2
                        ins = T.transpose(ps[0:width, 2 + c.pt % 2, P * n:P * n + P], cols(t, hh), ident[:, :])
                    ins.then_inc(s_pt, 1)
                    c.pt += 1

            def attention(n, scores, values, hd, diff=False):
                u0 = c.sc
                copied = {}
                for s in range(n + 2):
                    if s < n:
                        u = u0 + s
                        if u >= 2:
                            pe.wait_ge(s_p, u - 1)
                        if s == 0:
                            pe.wait_ge(s_pt_copied, c.pt)
                        for hh in range(2):
                            pairs = scores(s, hh)
                            for m, (q, k) in enumerate(pairs):
                                ins = T.matmul(ps[:, u % 2, 256 * hh:256 * hh + 256], q, k, start=m == 0,
                                               stop=m == len(pairs) - 1)
                        ins.then_inc(s_sc, 1)
                    if 1 <= s <= n:
                        u = u0 + s - 1
                        if diff:
                            c.comb += 1
                            pe.wait_ge(s_comb, c.comb)
                        else:
                            pe.wait_ge(s_p, u + 1)
                        pe.wait_ge(s_pt_copied, c.pt - 1)
                        for m in range(2 if diff else 4):
                            src = Ad if diff else Pr
                            ins = T.transpose(ps[:, 2 + c.pt % 2, P * m:P * m + P], src[:, u % 2, P * m:P * m + P],
                                              ident[:, :])
                        ins.then_inc(s_pt, 1)
                        c.pt += 1
                        copied[s - 1] = c.pt
                    if s >= 2:
                        u = u0 + s - 2
                        pe.wait_ge(s_pt_copied, copied[s - 2])
                        claim(1)
                        for hh in range(1 if diff else 2):
                            for kt in range(2):
                                ins = T.matmul(ps[:, acc_bank(c.acc), hd * hh:hd * hh + hd],
                                               PT[:, u % 2, 256 * hh + P * kt:256 * hh + P * kt + P],
                                               values(s - 2, hh, kt), start=kt == 0, stop=kt == 1)
                        ins.then_inc(s_acc, 1)
                        c.acc += 1
                        c.rdy += 1
                c.sc += n

            def gated():
                for half in range(2):
                    block(512, (2, 2, 2, 2), (hT_hi, hT_lo))
                    block(512, (2, 2), (oT_hi, oT_lo))

            def hid_T(step0, j, par, it, nt):
                pe.wait_ge(s_hid, it * 2 + (step0 + j + 1))
                for k in range(2):
                    for t in range(nt):
                        ins = T.transpose(ps[:, 6 + par, P * (k * nt + t):P * (k * nt + t) + P],
                                          hid[:, FB * t + P * k:FB * t + P * k + P], ident[:, :])
                ins.then_inc(s_hidT, 1)

            def gate_up(us, it, step0, j, par, nt, act, half):
                if half == 0 and j > 0:
                    pe.wait_ge(s_hid, it * 2 + (step0 + j - (0 if nt == 2 else 1)))
                outs = [(tok(t), 4 + (t if nt == 2 else par), 0, 512) for t in range(nt)]
                for k in range(2):
                    unit(us + k, it, 2, 512, 4 * half + 2 * k, act, outs, half == 0 and k == 0, half == 1 and k == 1)

            def down(us, it, step0, j, nt, y0, first, last):
                pe.wait_ge(s_hidT_lo, it * 2 + (step0 + j + 1))
                for k in range(2):
                    outs = [(tok(t), y0 + 2 * t + hf, 512 * hf, 512) for t in range(nt) for hf in range(2)]
                    unit(us + k, it, 1, 1024, k, (hidT_hi, hidT_lo), outs, first and k == 0, last and k == 1)

            def ffn_steps(step0, u0, it0, nt, act, y0):
                def pair(it, first):
                    for j in range(2):
                        u = u0 + 4 + 6 * j
                        gate_up(u, it, step0, j + 1, (j + 1) % 2, nt, act, 0)
                        hid_T(step0, j, j, it, nt)
                        gate_up(u + 2, it, step0, j + 1, (j + 1) % 2, nt, act, 1)
                        down(u + 4, it, step0, j, nt, y0, first and j == 0, False)

                pair(it0, True)
                with pe.Fori(1, (NSTEP - 1) // 2) as i:
                    pair(it0 + i, False)

            def ffn_end(step0, u0, it0, nt, y0):
                hid_T(step0, NSTEP - 1, 0, it0, nt)
                down(u0 + FFN_UNITS - 2, it0, step0, NSTEP - 1, nt, y0, False, True)

            def rows_ready():
                c.rows += 1
                pe.wait_ge(s_rows, c.rows)

            def norm_ready():
                c.gain += 1
                pe.wait_ge(s_gain_used, c.gain)

            def head(base, t, h, stride, width):
                return base[:, t, h * stride:h * stride + width]

            pe.wait_ge(s_const, 80)
            for L in range(DEPTH):
                norm_ready()
                split_T(lambda t: ZU[:, t, 0:D], (2, 2, 2, 2))
                split_ready()
                for b in range(3):
                    block(W1C, (2, 2, 2, 2), (hT_hi, hT_lo))
                rows_ready()
                split_T(lambda t: Z[:, t, 0:C_ROPE], (1, 1, 1, 2))
                split_ready()
                for b in range(2):
                    block(Q_LORA, (2, 1), (oT_hi, oT_lo))
                claim(4)
                for k in range(2):
                    unit(c.done, 0, 1, 1024, 3 + k, (oT_hi, oT_lo),
                         [(tok(t), acc_bank(c.acc + 2 * t + hf), 512 * hf, 512) for t in range(NT) for hf in range(2)],
                         k == 0, k == 1)
                    c.done += 1
                c.acc += 4
                rows_ready()
                plain_T(lambda t, h: ZU[:, t, QK_MLA * h:QK_MLA * h + QK_MLA], MLA_H, QK_MLA)
                plain_T(lambda t, h: ZU[:, t, 768 + QK_MLA * h:768 + QK_MLA * h + QK_MLA], MLA_H, QK_MLA)

                def mla_scores(s, hh):
                    h, t = 2 * (s // 2) + hh, s % 2
                    return [(qT[0:QK_MLA, h, P * t:P * t + P], kT[0:QK_MLA, h, :])]

                def mla_values(s, hh, kt):
                    c0 = 1536 + MLA_V * (2 * (s // 2) + hh)
                    return ZU[:, kt, c0:c0 + MLA_V]

                attention(8, mla_scores, mla_values, HD)
                pe.wait_ge(s_acc_free, c.acc)
                split_T(lambda t: ZU[:, t, 0:BW], (2, 2))
                split_ready()
                gated()
                rows_ready()
                plain_T(lambda t, h: Z[:, t, C_GQA + HD * h:C_GQA + HD * h + HD], GQA_QH + GQA_KVH, HD)

                def gqa_scores(s, hh):
                    h, t = 2 * (s // 2) + hh, s % 2
                    return [(qT[0:HD, h, P * t:P * t + P], kT[0:HD, h // (GQA_QH // GQA_KVH), :])]

                def gqa_values(s, hh, kt):
                    h = 2 * (s // 2) + hh
                    c0 = C_GQA + HD * (GQA_QH + GQA_KVH + h // (GQA_QH // GQA_KVH))
                    return Z[:, kt, c0:c0 + HD]

                attention(8, gqa_scores, gqa_values, HD)
                pe.wait_ge(s_acc_free, c.acc)
                split_T(lambda t: ZU[:, t, 0:BW], (1, 1, 1, 1))
                split_ready()
                gated()
                for b in range(3):
                    block(W2C, (2, 2, 2, 2), (hT_hi, hT_lo))
                rows_ready()
                for g in range(2):
                    plain_T(lambda t, h: Z[:, t, DQK * (8 * g + h):DQK * (8 * g + h) + DQK], 8, DQK)
                    plain_T(lambda t, h: Z[:, t, 512 + DQK * (8 * g + h):512 + DQK * (8 * g + h) + DQK], 8, DQK)

                    def diff_scores(s, m):
                        h, t = 2 * (s // 2) + m, s % 2
                        return [(qT[0:DQK, h, P * t:P * t + P], kT[0:DQK, h, :])]

                    def diff_values(s, hh, kt):
                        c0 = 1024 + DV * (4 * g + s // 2)
                        return Z[:, kt, c0:c0 + DV]

                    attention(8, diff_scores, diff_values, DV, diff=True)
                rows_ready()
                split_T(lambda t: ZU[:, t, 0:BW], (2, 2))
                split_ready()
                gated()
                pe.wait_ge(s_acc_free, c.acc)
                split_T(lambda t: S1[:, t, :], (2, 2, 2, 2))
                split_ready()
                for b in range(2):
                    block(512, (2, 2, 2, 2), (hT_hi, hT_lo))
                norm_ready()
                split_T(lambda t: ZU[:, t, 1024:2048], (2, 2, 2, 2))
                split_ready()
                for b in range(4):
                    block(512, (2, 2, 2, 2), (oT_hi, oT_lo))
                pe.wait_ge(s_acc_free, c.acc - 4)
                plain_T(lambda t, h: ZU[:, t, 1024 + P * h:1024 + P * h + P], 8, P)
                norm_ready()
                norm_ready()
                split_T(lambda t: ZU[:, t, 0:D], (2, 2, 2, 2))
                split_ready()
                for b in range(2):
                    block(512, (2, 2, 2, 2), (hT_hi, hT_lo))
                pe.wait_ge(s_acc_free, c.acc)
                plain_T(lambda t, h: ZU[:, t, P * h:P * h + P], 8, P)

                def mem_scores(s, hh):
                    h, t = 2 * (s // 2) + hh, s % 2
                    return [(qT[:, 2 * h + k, P * t:P * t + P], kT[:, 2 * h + k, :]) for k in range(2)]

                def mem_values(s, hh, kt):
                    h = 2 * (s // 2) + hh
                    return Z[:, kt, MEM_HD * h:MEM_HD * h + MEM_HD]

                attention(4, mem_scores, mem_values, MEM_HD)
                pe.wait_ge(s_acc_free, c.acc)
                split_T(lambda t: S1[:, t, :], (2, 2, 2, 2))
                split_ready()
                for b in range(2):
                    block(512, (2, 2, 2, 2), (hT_hi, hT_lo))
                norm_ready()
                norm_ready()
                split_T(lambda t: ZU[:, t, 0:D], (2, 2, 2, 2))
                split_ready()
                if L == 0:
                    for half in range(2):
                        gate_up(FFN0[0] + 2 * half, 0, 0, 0, 0, NT, (hT_hi, hT_lo), half)
                    ffn_steps(0, FFN0[0], 0, NT, (hT_hi, hT_lo), 0)
                    ffn_end(0, FFN0[0], 0, NT, 0)
                    norm_ready()
                    c.done = LAYER0[1]
            pe.wait_ge(s_wrl, 1)
            claim(2)
            bk = acc_bank(c.acc)
            for t in range(NT):
                for k in range(8):
                    ins = three(ps[:, bk, NE * t:NE * t + NE], hT_hi[:, k, P * t:P * t + P],
                                hT_lo[:, k, P * t:P * t + P], wr_hi[:, k, :], wr_lo[:, k, :], k == 0, k == 7)
            ins.then_inc(s_acc, 1)
            pe.wait_ge(s_tri, 32)
            rows_ready()
            bk = acc_bank(c.acc + 1)
            T.matmul(ps[:, bk, 0:NE], tri, MASK[:, 0, :], start=True, stop=True)
            T.matmul(ps[:, bk, NE:2 * NE], tri, MASK[:, 1, :], start=True, stop=False)
            T.matmul(ps[:, bk, NE:2 * NE], ones, MASK[:, 0, :], start=False, stop=True)
            T.matmul(ps[:, bk, 2 * NE:3 * NE], ones, MASK[:, 0, :], start=True, stop=False)
            T.matmul(ps[:, bk, 2 * NE:3 * NE], ones, MASK[:, 1, :], start=False, stop=True).then_inc(s_acc, 1)
            pe.wait_ge(s_hrow, 1)
            pe.wait_ge(s_rounds, 1)
            nr = pe.value_load(rounds[0:1, 0:1], min_val=1, max_val=2)
            rows_hi = hT_hi[:, :, :].rearrange("p (t a) b -> p t (a b)", t=NT)
            rows_lo = hT_lo[:, :, :].rearrange("p (t a) b -> p t (a b)", t=NT)

            def gather(e, q):
                pe.wait_ge(s_oh, q * 2 + (e + 1))
                pe.wait_ge(s_added, q * 8 + 1)
                for t in range(NT):
                    T.transpose(ps[:, 7, P * t:P * t + P], oh[:, t, :].bitcast(f32), ident[:, :])
                for k in range(8):
                    out = ps[:, 2 * e + k // 4, P * (k % 4):P * (k % 4) + P]
                    for n in range(4):
                        t, src = n // 2, (rows_hi, rows_lo)[n % 2]
                        ins = T.matmul(out, src[:, t, P * k:P * k + P], oh[:, t, :], start=n == 0, stop=n == 3)
                ins.then_inc(s_gath, 1)

            def scatter(e, q):
                pe.wait_ge(s_ylo, q * 2 + (e + 1))
                pe.wait_ge(s_ohT, q * 2 + 2)
                for n in range(4):
                    t, hf = n // 2, n % 2
                    bk = (2 * e, 2 * e + 1, 6, 7)[n]
                    for m, src in enumerate((oT_hi, oT_lo)):
                        ins = T.matmul(ps[:, bk, :], ohT[:, e, P * t:P * t + P], src[:, 4 * hf:4 * hf + 4, P:2 * P],
                                       start=m == 0, stop=m == 1)
                    ins.then_inc(s_scat, 1)

            def expert_start(e, q, it):
                pe.wait_ge(s_gath_lo, q * 2 + (e + 1))
                pe.wait_ge(s_hid, it * 2 + (NSTEP + NSTEP * e))
                for half in range(2):
                    gate_up(FFN0[1] + FFN_UNITS * e + 2 * half, it, NSTEP * (e + 1), 0, 0, 1, (oT_hi, oT_lo), half)

            with pe.Fori(0, nr) as r:
                with pe.Fori(0, NE // 2) as pr:
                    q = pe.snap(r * (NE // 2) + pr)
                    it = pe.snap(q * 11)
                    gather(0, q)
                    expert_start(0, q, it)
                    ffn_steps(NSTEP, FFN0[1], it, 1, (oT_hi, oT_lo), 0)
                    gather(1, q)
                    ffn_end(NSTEP, FFN0[1], it, 1, 0)
                    expert_start(1, q, it)
                    scatter(0, q)
                    pe.wait_ge(s_added, q * 8 + 5)
                    ffn_steps(2 * NSTEP, FFN0[1] + FFN_UNITS, it, 1, (oT_hi, oT_lo), 2)
                    ffn_end(2 * NSTEP, FFN0[1] + FFN_UNITS, it, 1, 2)
                    scatter(1, q)


_INS = ['x', 'mem', 'mix_pre_g', 'mix_post_g', 'w_in', 'mla_q_norm_g', 'mla_w_q_up', 'mla_kv_norm_g', 'mla_w_kv_up',
        'gqa_q_norm_g', 'gqa_k_norm_g', 'diff_lambda_q1', 'diff_lambda_k1', 'diff_lambda_q2', 'diff_lambda_k2',
        'diff_subln_g', 'w_branch', 'w_out', 'mem_pre_g', 'mem_post_g', 'mem_norm_g', 'mem_wq', 'mem_wkv', 'mem_wo',
        'ffn_pre_g', 'ffn_post_g', 'dense_w_gate', 'dense_w_up', 'dense_w_down', 'moe_w_router', 'moe_b_router',
        'moe_w_gate', 'moe_w_up', 'moe_w_down']


def rope_table():
    import numpy as np
    f = np.float32

    def cos_sin(pos, rot):
        inv = f(500000.0) ** (-np.arange(0, rot, 2, dtype=f) / f(rot))
        ang = pos.astype(f)[:, None] * inv.astype(f)[None, :]
        return np.cos(ang), np.sin(ang)

    pos = np.arange(SEQ)
    cm, sm = cos_sin(pos, ROT)
    cr, sr = cos_sin(pos // 64, HD // 2)
    cc, sc = cos_sin(pos % 64, HD // 2)
    cp, sp = cos_sin(pos, DROT)
    return np.concatenate([cm, sm, cr, cc, sr, sc, cp, sp], axis=1).astype(f)


def constants():
    import numpy as np
    return np.stack([np.eye(P), np.tile(np.arange(P), (P, 1)), np.triu(np.ones((P, P)), 1), np.ones((P, P))]).astype(np.float32)


def kernel(**inputs):
    import numpy as _np
    import concourse.bacc as _bacc
    from concourse import mybir as _mybir
    from concourse.bass_utils import run_bass_kernel_spmd as _run

    nc = _bacc.Bacc("TRN2", target_bir_lowering=False, num_devices=1)
    arrays, aps = {}, {}
    named = [(name, _np.ascontiguousarray(inputs[name])) for name in _INS]
    named += [("rope", rope_table()), ("consts", constants())]
    for name, a in named:
        arrays[f"in_{name}_dram"] = a
        aps[name] = nc.dram_tensor(f"in_{name}_dram", a.shape, _mybir.dt.from_np(a.dtype), kind="ExternalInput").ap()
    aps["out"] = nc.dram_tensor("out_0_dram", (1, SEQ, D), _mybir.dt.float32, kind="ExternalOutput").ap()
    build(nc, aps)
    r = _run(nc, [arrays], core_ids=[0])
    return r.results[0]["out_0_dram"]
```

```python
import concourse.bass as bass
from concourse import mybir
from contextlib import ExitStack
from itertools import islice

D = 1024
SEQ = 256
P = 128
NT = SEQ // P
DEPTH = 2
MEM_LEN = 256
EPS = 1e-6
MLA_H, Q_LORA, KV_LORA, NOPE, ROT, MLA_V = 8, 384, 256, 64, 32, 64
GQA_QH, GQA_KVH, HD = 8, 2, 64
DIFF_H, DQK, DV, DROT = 8, 32, 64, 8
BW = 512
NBR = 3
MEM_H, MEM_HD = 4, 256
F = 2816
NE = 8
QK_MLA = NOPE + ROT
C_ROPE = Q_LORA + KV_LORA
C_GQA = C_ROPE + ROT
N1 = C_GQA + (GQA_QH + 2 * GQA_KVH) * HD
N2 = 3 * DIFF_H * DV
GATE0 = N1 + N2
W1C, W2C = N1 // 3, N2 // 3
FB = 256
NSTEP = F // FB
LAMBDA_INIT = [0.8 - 0.6 * (2.718281828459045 ** (-0.3 * layer)) for layer in range(DEPTH)]
SG_Q, SG_KV, SG_GQ, SG_GK, SG_SUB, SG_LAM, SG_N = 0, 384, 640, 704, 768, 832, 960
RC_M, RS_M, RC_A, RS_A, RC_P, RS_P, R_N = 0, 16, 32, 64, 96, 100, 104
RAW_SLOTS, UNIT_SLOTS = 6, 4
KV_BANK, LAYER_BANKS = 26, 96
ACC_LAYER = 4 + 4 + 4 + 2 + 2 + 4 + 4 + 4 + 4
N_MIX, N_MEM, N_LAT, N_DIFF, N_POST, N_PRE, N_POST2, N_FFN, N_COLS = 0, 2, 4, 8, 24, 28, 30, 34, 36
LOOP_UNITS = 12


def unit_widths():
    w = [2 * W1C] * 12
    w += [2 * Q_LORA, Q_LORA] * 2
    w += [1024] * 2
    w += [1024] * 16
    w += [1024] * 12
    w += [2 * W2C] * 12
    w += [1024] * 12 * 2
    w += [1024] * (8 + 8 + 8)
    return w


def run(work, units=None):
    for _ in islice(work, units):
        pass


def share(fill, units, s, steps):
    run(fill, (s + 1) * units // steps - s * units // steps)


class Counts:

    def __init__(self):
        self.unit = 0
        self.done = 0
        self.acc = 0
        self.rdy = 0
        self.acc_hi = 0
        self.pt = 0
        self.sc = 0
        self.pv = 0
        self.gates = 0
        self.rows = 0
        self.norm = 0
        self.gain = 0
        self.pre = 0
        self.sq1 = 0
        self.post = 0
        self.sums = 0
        self.chain = 0


def build(nc, A):
    f32, f32r, i32 = mybir.dt.float32, mybir.dt.float32r, mybir.dt.int32
    ACT, ALU, AX = mybir.ActivationFunctionType, mybir.AluOpType, mybir.AxisListType.X
    ctx = ExitStack()
    WIDTHS = unit_widths()
    LAYER_UNITS = len(WIDTHS)
    FFN_UNITS = 6 * NSTEP
    LAYER0 = [0, LAYER_UNITS + FFN_UNITS]
    FFN0 = [LAYER_UNITS, 2 * LAYER_UNITS + FFN_UNITS]

    def width_of(u):
        for layer in range(DEPTH):
            if LAYER0[layer] <= u < LAYER0[layer] + LAYER_UNITS:
                return WIDTHS[u - LAYER0[layer]]
        return 1024

    with ctx:
        def sb(name, shape, dt=f32):
            return ctx.enter_context(nc.sbuf_tensor(name, shape, dt))

        def sem(name):
            return ctx.enter_context(nc.semaphore(name))

        raw = sb("raw", [P, RAW_SLOTS, 2048])
        w_hi = sb("w_hi", [P, UNIT_SLOTS, 1024], f32r)
        w_lo = sb("w_lo", [P, UNIT_SLOTS, 1024], f32r)
        x = sb("x", [P, NT, D])
        S1 = sb("S1", [P, NT, D])
        ZU = sb("ZU", [P, NT, 2048])
        hT_hi = sb("hT_hi", [P, 8, SEQ], f32r)
        hT_lo = sb("hT_lo", [P, 8, SEQ], f32r)
        oT_hi = sb("oT_hi", [P, 8, SEQ], f32r)
        oT_lo = sb("oT_lo", [P, 8, SEQ], f32r)
        Z = sb("Z", [P, NT, N2])
        qT = sb("qT", [P, 8, SEQ])
        kT = sb("kT", [P, 8, SEQ])
        Pr = sb("Pr", [P, 2, 512])
        PT = sb("PT", [P, 2, 512])
        E4 = sb("E4", [P, 2, 512])
        hidT_hi = sb("hidT_hi", [P, 2, 256], f32r)
        hidT_lo = sb("hidT_lo", [P, 2, 256], f32r)
        gains = sb("gains", [P, 2, D])
        sg = sb("sg", [P, SG_N])
        rope = sb("rope", [P, NT, R_N])
        ident = sb("ident", [P, P])
        iota = sb("iota", [P, P])
        oh = sb("oh", [P, NT, P], f32r)
        ohT = sb("ohT", [P, 2, SEQ], f32r)
        wr = sb("wr", [P, 8, NE])
        wr_hi = sb("wr_hi", [P, 8, NE], f32r)
        wr_lo = sb("wr_lo", [P, 8, NE], f32r)
        brt = sb("brt", [P, NE])
        misc = sb("misc", [P, 4 * N_COLS + 32])
        ssq, ms, rstd, mhalf = (misc[:, N_COLS * n:N_COLS * (n + 1)] for n in range(4))
        m0 = 4 * N_COLS
        nmax, sums, rsum = (misc[:, m0 + 8 * n:m0 + 8 * n + 8].rearrange("p (u h) -> p u h", h=2) for n in range(3))
        lam = misc[:, m0 + 24:m0 + 28]
        nlam = misc[:, m0 + 28:m0 + 29]
        rounds = sb("rounds", [P, 1], i32)
        ps = ctx.enter_context(nc.psum_tensor("ps", [P, 8, 512], f32))

        kv_dram = [nc.dram_tensor(f"kv_spill{L}", (MEM_LEN, 2 * D), f32, kind="Internal").ap() for L in range(DEPTH)]
        T_MEM = [ACC_LAYER * L + 12 for L in range(DEPTH)]

        scratch = kT[:, :, :].rearrange("p a b -> p (a b)")
        sl = E4[:, 0, :]
        hid = E4[:, 1, :]
        Zf = Z[:, :, :].rearrange("p a b -> p (a b)")
        tri, ones = Zf[:, 0:128], Zf[:, 128:256]

        def small(n, shape_t=True):
            v = Zf[:, 256 + 16 * n:272 + 16 * n]
            return v.rearrange("p (t e) -> p t e", t=2)

        LG, EQ, CC, OH1, OH2, L2, GATE, MASK, RANKM = (small(n) for n in range(9))
        M1, M2, I1, EX, W1, W2 = (Zf[:, 420 + 2 * n:422 + 2 * n] for n in range(6))
        MX, NR = Zf[:, 440:441], Zf[:, 441:442]

        s_x = sem("x_landed")
        s_ident = sem("identity_landed")
        s_const = sem("constants_landed")
        s_tri = sem("triangle_landed")
        s_raw = [sem(f"raw_landed{n}") for n in range(RAW_SLOTS)]
        s_hi = sem("unit_hi_ready")
        s_lo = sem("unit_lo_ready")
        s_used = sem("unit_used")
        s_gain = [sem(f"gain_landed{n}") for n in range(2)]
        s_gain_first = sem("first_gain_landed")
        s_norm = sem("gained_tiles_ready")
        s_res = sem("residual_tiles_ready")
        s_sg = sem("small_gains_landed")
        s_mem = sem("mem_landed")
        s_spill = sem("memory_kv_spilled")
        s_kmem = sem("memory_keys_landed")
        s_vmem = sem("memory_values_landed")
        s_gqa = sem("gqa_rows_ready")
        s_pv = sem("attention_out_ready")
        s_pv_free = sem("attention_out_copied")
        s_ssq = sem("squares_summed")
        s_sq1 = sem("second_tile_squares_summed")
        s_y0 = sem("dense_outputs_gained")
        s_pool = sem("pool_chain")
        s_rstd = sem("rstd_ready")
        s_rows = sem("rows_ready")
        s_acc = sem("acc_ready")
        s_acc_hi = sem("acc_hi_copied")
        s_acc_free = sem("acc_free")
        s_gexp = sem("gate_tanh_ready")
        s_pt = sem("pt_ready")
        s_pt_copied = sem("pt_copied")
        s_sc = sem("scores_ready")
        s_max = sem("max_ready")
        s_p = sem("probs_ready")
        s_subT = sem("diff_transposes_lo_ready")
        s_lamq = sem("lambda_dots_ready")
        s_lame = sem("lambda_exp_ready")
        s_chain = sem("dve_chain")
        s_wr = sem("router_hi_ready")
        s_wrl = sem("router_lo_ready")
        s_silu = sem("silu_ready")
        s_hid = sem("hidden_ready")
        s_hidT = sem("hiddenT_ready")
        s_hidT_hi = sem("hiddenT_hi_copied")
        s_hidT_lo = sem("hiddenT_lo_ready")
        s_yhi = sem("y_hi_copied")
        s_ylo = sem("y_lo_ready")
        s_hrow_hi = sem("rows_hi_ready")
        s_hrow = sem("rows_lo_ready")
        s_topd = sem("top_gap_ready")
        s_tope = sem("top_exp_ready")
        s_rank = sem("ranks_ready")
        s_rounds = sem("rounds_ready")
        s_oh = sem("onehot_ready")
        s_gath = sem("gather_ready")
        s_ohT = sem("onehotT_copied")
        s_gath_hi = sem("gather_hi_copied")
        s_gath_lo = sem("gather_lo_ready")
        s_scat = sem("scatter_ready")
        s_added = sem("scatter_added")
        s_final = sem("result_ready")
        s_out = sem("out_stored")

        def acc_bank(a):
            return 4 + a % 4

        def hi_slot(us):
            return us % UNIT_SLOTS

        def raw_of(us):
            t = us // 2
            off = width_of(us - 1) if us % 2 else 0
            return raw[:, t % RAW_SLOTS, off:off + width_of(us)]

        def act_split(act, us, it=0):
            w = width_of(us)
            if us % 2 == 0:
                act.wait_ge(s_raw[(us // 2) % RAW_SLOTS], it * 32 + 32 * (us // LOOP_UNITS + 1))
            if us >= UNIT_SLOTS:
                act.wait_ge(s_used, it * LOOP_UNITS + (us - UNIT_SLOTS + 1))
            nc.scalar.activation(w_hi[:, hi_slot(us), 0:w], raw_of(us), ACT.Copy).then_inc(s_hi, 1)

        def dve_split(dve, us, it=0):
            w = width_of(us)
            dve.wait_ge(s_hi, it * LOOP_UNITS + (us + 1))
            nc.vector.tensor_tensor(w_lo[:, hi_slot(us), 0:w], raw_of(us),
                                    w_hi[:, hi_slot(us), 0:w].bitcast(f32), ALU.subtract).then_inc(s_lo, 1)

        blk = ctx.enter_context(nc.Block())

        @blk.sync
        def _(sp):
            sp.dma_start(x[:, :, :], A["x"][0].rearrange("(t p) d -> p t d", p=P)).then_inc(s_x, 16)
            sp.dma_start(gains[:, 0, :], A["mix_pre_g"][0].partition_broadcast(P)).then_inc(s_gain_first, 16)
            n = [0]

            def chunks(W, k0, nk, c0, nc_):
                return W[k0 * P:(k0 + nk) * P, c0:c0 + nc_].rearrange("(k p) n -> p k n", p=P)

            def put(ts, parts, it=0):
                if ts >= RAW_SLOTS:
                    sp.wait_ge(s_lo, it * LOOP_UNITS + 2 * (ts - RAW_SLOTS) + 2)
                slot = ts % RAW_SLOTS
                for off, nk, w, src in parts:
                    dst = raw[:, slot, off:off + nk * w].rearrange("p (k n) -> p k n", k=nk)
                    sp.dma_start(dst, src).then_inc(s_raw[slot], 16)

            def block(W, k_chunks, c0, w):
                for k0 in range(0, k_chunks, 4):
                    nk = min(4, k_chunks - k0)
                    parts = [(0, 2, w, chunks(W, k0, 2, c0, w)),
                             (2 * w, nk - 2, w, chunks(W, k0 + 2, nk - 2, c0, w))]
                    put(n[0], parts)
                    n[0] += 1

            def gate_up(Wg, Wu, row0, col, tile0, it):
                for h in range(2):
                    if tile0 + h >= RAW_SLOTS:
                        sp.wait_ge(s_lo, it * LOOP_UNITS + 2 * (tile0 + h - RAW_SLOTS) + 2)
                    slot = (tile0 + h) % RAW_SLOTS
                    for g, W in enumerate((Wg, Wu)):
                        dst = raw[:, slot, :].rearrange("p (k g n) -> p k g n", k=4, g=2)[:, :, g, :]
                        src = W[bass.ds(row0 + 512 * h, 512), bass.ds(col, FB)]
                        sp.dma_start(dst, src.rearrange("(k p) n -> p k n", p=P)).then_inc(s_raw[slot], 16)

            def down(Wd, row0, tile0, it):
                sp.wait_ge(s_lo, it * LOOP_UNITS + 2 * (tile0 - RAW_SLOTS) + 2)
                slot = tile0 % RAW_SLOTS
                for h in range(2):
                    sp.dma_start(raw[:, slot, 1024 * h:1024 * h + 1024],
                                 Wd[bass.ds(row0 + P * h, P), :]).then_inc(s_raw[slot], 16)

            def ffn(Wg, Wu, Wd, row_in, row_h, tile0, it0):
                gate_up(Wg, Wu, row_in, 0, tile0, it0)
                with sp.Fori(0, (NSTEP - 1) // 2) as i:
                    it = it0 + i
                    for j in range(2):
                        gate_up(Wg, Wu, row_in, i * (2 * FB) + FB * (j + 1), tile0 + 2 + 3 * j, it)
                        down(Wd, row_h + i * (2 * FB) + FB * j, tile0 + 4 + 3 * j, it)
                down(Wd, row_h + FB * (NSTEP - 1), tile0 + 3 * NSTEP - 1, it0)

            for L in range(DEPTH):
                w_in = A["w_in"][L]
                for b in range(3):
                    block(w_in, 8, W1C * b, W1C)
                for b in range(2):
                    block(A["mla_w_q_up"][L], 3, Q_LORA * b, Q_LORA)
                put(n[0], [(1024 * k, 1, 1024, chunks(A["mla_w_kv_up"][L], k, 1, 0, 1024)) for k in range(2)])
                n[0] += 1

                def gated(br):
                    for half in range(2):
                        block(w_in, 8, GATE0 + D * br + 512 * half, 512)
                        block(A["w_branch"][L, br], 4, 512 * half, 512)

                for b in range(4):
                    block(A["mem_wkv"][L], 8, 512 * b, 512)
                gated(0)
                for b in range(3):
                    block(w_in, 8, N1 + W2C * b, W2C)
                gated(1)
                gated(2)
                for name, cols in (("w_out", D), ("mem_wq", D), ("mem_wo", D)):
                    for b in range(cols // 512):
                        block(A[name][L], 8, 512 * b, 512)
                if L == 0:
                    ffn(A["dense_w_gate"][0], A["dense_w_up"][0], A["dense_w_down"][0], 0, 0, n[0], 0)
                    n[0] += 3 * NSTEP
            Wg = A["moe_w_gate"][0].rearrange("e k n -> (e k) n")
            Wu = A["moe_w_up"][0].rearrange("e k n -> (e k) n")
            Wd = A["moe_w_down"][0].rearrange("e f n -> (e f) n")

            def experts(r):
                with sp.Fori(0, NE // 2) as pr:
                    it = sp.snap(pr * 11 + 11 * (NE // 2) * r)
                    for e in range(2):
                        ffn(Wg, Wu, Wd, pr * (2 * D) + D * e, pr * (2 * F) + F * e, n[0] + 3 * NSTEP * e, it)

            experts(0)
            sp.wait_ge(s_rounds, 1)
            nr = sp.value_load(rounds[0:1, 0:1], min_val=1, max_val=2)
            with sp.If(nr > 1):
                experts(1)
            sp.wait_ge(s_final, 2)
            sp.dma_start(A["out"][0].rearrange("(t p) d -> p t d", p=P), x[:, :, :]).then_inc(s_out, 16)
            sp.wait_ge(s_out, 16)

        @blk.gpsimd
        def _(pool):
            GAINS = ["mix_pre_g", "mem_norm_g", "mix_post_g", "mem_pre_g", "mem_post_g", "ffn_pre_g", "ffn_post_g"]
            order = [(g, L) for L in range(DEPTH) for g in GAINS]
            chain, requests, used = [0], [0], [0]

            def load_gain(k):
                g, L = order[k]
                nc.gpsimd.dma_start(gains[:, k % 2, :], A[g][L].partition_broadcast(P)).then_inc(s_gain[k % 2], 16)

            def load_small(L):
                for name, c in (("mla_q_norm_g", SG_Q), ("mla_kv_norm_g", SG_KV), ("gqa_q_norm_g", SG_GQ),
                                ("gqa_k_norm_g", SG_GK), ("diff_subln_g", SG_SUB), ("diff_lambda_q1", SG_LAM),
                                ("diff_lambda_k1", SG_LAM + 32), ("diff_lambda_q2", SG_LAM + 64),
                                ("diff_lambda_k2", SG_LAM + 96)):
                    w = A[name].shape[1]
                    nc.gpsimd.dma_start(sg[:, c:c + w], A[name][L].partition_broadcast(P)).then_inc(s_sg, 16)

            def step(ins):
                chain[0] += 1
                ins.then_inc(s_pool, 1)
                pool.wait_ge(s_pool, chain[0])

            def rsqrt(*parts, scale=1.0, halves=False):
                requests[0] += 1
                pool.wait_ge(s_ssq, requests[0])
                if halves:
                    c0, c1, _ = parts[0]
                    step(nc.gpsimd.tensor_tensor(ssq[:, c0:c1], ssq[:, c0:c1], ssq[:, c1:2 * c1 - c0], ALU.add))
                f = 1.0 / (scale * scale)
                for c0, c1, n in parts:
                    step(nc.gpsimd.tensor_scalar(ms[:, c0:c1], ssq[:, c0:c1], f / n, f * EPS, ALU.mult, ALU.add))
                c0, c1 = parts[0][0], parts[-1][1]
                nc.gpsimd.tensor_tensor(rstd[:, c0:c1], ms[:, c0:c1], mhalf[:, c0:c1], ALU.pow).then_inc(s_rstd, 1)

            def norm(c0, scale=1.0, halves=False):
                rsqrt((c0, c0 + NT, D), scale=scale, halves=halves)
                post = "post" in order[used[0]][0]
                used[0] += 1
                if used[0] + 1 < len(order):
                    same = [g for g, _ in order[:used[0]] if ("post" in g) == post]
                    pool.wait_ge(s_res if post else s_norm, NT * len(same))
                    load_gain(used[0] + 1)

            def mem_rows():
                nc.gpsimd.dma_start(S1[:, :, :], A["mem"][0].rearrange("(t p) d -> p t d", p=P)).then_inc(s_mem, 16)

            kv_rows = [kv_dram[L].rearrange("(t p) n -> p t n", p=P) for L in range(DEPTH)]

            def spill(L, b):
                pool.wait_ge(s_acc_free, LAYER_BANKS * L + KV_BANK + 2 * (b + 1))
                nc.gpsimd.dma_start(kv_rows[L][:, :, 512 * b:512 * b + 512], E4[:, :, :]).then_inc(s_spill, 16)

            def gqa_rows(L):
                QKH, H2 = GQA_QH + GQA_KVH, HD // 2
                W = QKH * HD
                S = S1[:, :, :].rearrange("p t d -> p (t d)")
                sq, hs = S[:, 0:W], S[:, 2 * W:2 * W + 3 * QKH]
                G = nc.gpsimd
                spill(L, 0)
                for t in range(NT):
                    v = Z[:, t, C_GQA:C_GQA + W]
                    heads = v.rearrange("p (h d) -> p h d", d=HD)
                    step(G.tensor_tensor(sq, v, v, ALU.mult))
                    w = HD // 2
                    sh = sq.rearrange("p (h d) -> p h d", d=HD)
                    while w >= 1:
                        step(G.tensor_tensor(sh[:, :, 0:w], sh[:, :, 0:w], sh[:, :, w:2 * w], ALU.add))
                        w //= 2
                    step(G.tensor_scalar(hs[:, 0:QKH].unsqueeze(2), sh[:, :, 0:1], 1.0 / HD, EPS, ALU.mult, ALU.add))
                    step(G.tensor_tensor(hs[:, QKH:2 * QKH], hs[:, 0:QKH], mhalf[:, 0:QKH], ALU.pow))
                    step(G.tensor_tensor(heads, heads, hs[:, QKH:2 * QKH].unsqueeze(2).broadcast_to([P, QKH, HD]), ALU.mult))
                    step(G.tensor_tensor(heads[:, 0:GQA_QH, :], heads[:, 0:GQA_QH, :],
                                         sg[:, SG_GQ:SG_GQ + HD].unsqueeze(1).broadcast_to([P, GQA_QH, HD]), ALU.mult))
                    step(G.tensor_tensor(heads[:, GQA_QH:, :], heads[:, GQA_QH:, :],
                                         sg[:, SG_GK:SG_GK + HD].unsqueeze(1).broadcast_to([P, GQA_KVH, HD]), ALU.mult))
                    spill(L, 1 + t)
                    v4 = v.rearrange("p (h a d) -> p h a d", a=2, d=H2)
                    a = S[:, 0:W].rearrange("p (h a d) -> p h a d", a=2, d=H2)
                    b = S[:, W:2 * W].rearrange("p (h a d) -> p h a d", a=2, d=H2)
                    co = rope[:, t, RC_A:RC_A + H2].unsqueeze(1).broadcast_to([P, QKH, H2])
                    si = rope[:, t, RS_A:RS_A + H2].unsqueeze(1).broadcast_to([P, QKH, H2])
                    for h in range(2):
                        step(G.tensor_tensor(a[:, :, h, :], v4[:, :, h, :], co, ALU.mult))
                        step(G.tensor_tensor(b[:, :, h, :], v4[:, :, h, :], si, ALU.mult))
                    for h, op in ((0, ALU.subtract), (1, ALU.add)):
                        by_pair = [w[:, 0:GQA_QH, m, :].rearrange("p (g h) d -> p h g d", g=GQA_KVH)
                                   for w, m in ((a, h), (b, 1 - h))]
                        step(G.tensor_tensor(v4[:, 0:GQA_QH, h, :].rearrange("p (h g) d -> p h g d", g=GQA_KVH),
                                             by_pair[0], by_pair[1], op))
                        ins = G.tensor_tensor(v4[:, GQA_QH:, h, :], a[:, GQA_QH:, h, :], b[:, GQA_QH:, 1 - h, :], op)
                        if h == 0:
                            step(ins)
                    if t == 0:
                        step(ins)
                    else:
                        ins.then_inc(s_gqa, 1)
                spill(L, 3)

            mem_rows()
            load_gain(1)
            step(nc.gpsimd.memset(mhalf[:, :], -0.5))
            load_small(0)
            pool.wait_ge(s_const, 64)
            for L in range(DEPTH):
                norm(N_MIX, 0.5)
                norm(N_MEM)
                rsqrt((N_LAT, N_LAT + 2, Q_LORA), (N_LAT + 2, N_LAT + 4, KV_LORA))
                pool.wait_ge(s_acc, T_MEM[L])
                gqa_rows(L)
                pool.wait_ge(s_rows, 5 * L + 4)
                pool.wait_ge(s_spill, 64 * (L + 1))
                nc.gpsimd.dma_start(ZU[:, :, 1024:2048], kv_rows[L][:, :, 0:D]).then_inc(s_kmem, 16)
                rsqrt((N_DIFF, N_DIFF + 16, DV), scale=1.0 - LAMBDA_INIT[L])
                pool.wait_ge(s_rows, 5 * L + 5)
                nc.gpsimd.dma_start(Z[:, :, 0:D], kv_rows[L][:, :, D:2 * D]).then_inc(s_vmem, 16)
                if L + 1 < DEPTH:
                    load_small(L + 1)
                for c0 in (N_POST, N_PRE, N_POST2, N_FFN):
                    norm(c0, halves=c0 in (N_POST, N_POST2))
                if L + 1 == DEPTH:
                    nc.gpsimd.dma_start(tri, A["consts"][2]).then_inc(s_tri, 16)
                    nc.gpsimd.dma_start(ones, A["consts"][3]).then_inc(s_tri, 16)
                norm(N_POST)
                if L + 1 < DEPTH:
                    mem_rows()

        @blk.scalar
        def _(act):
            act.dma_start(ident[:, :], A["consts"][0]).then_inc(s_ident, 16)
            act.dma_start(rope[:, :, :], A["rope"].rearrange("(t p) c -> p t c", p=P)).then_inc(s_const, 16)
            act.dma_start(iota[:, :], A["consts"][1]).then_inc(s_const, 16)
            act.dma_start(wr[:, :, :], A["moe_w_router"][0].rearrange("(k p) e -> p k e", p=P)).then_inc(s_const, 16)
            act.dma_start(brt[:, :], A["moe_b_router"][0].partition_broadcast(P)).then_inc(s_const, 16)
            c = Counts()

            def advance(limit):
                while c.unit < limit:
                    act_split(act, c.unit)
                    c.unit += 1

            def acc_hi(dst):
                c.rdy += 1
                act.wait_ge(s_acc, c.rdy)
                nc.scalar.activation(dst, bank(c.acc, dst), ACT.Copy).then_inc(s_acc_hi, 1)
                c.acc += 1

            def bank(a, dst):
                w = 1
                for n in dst.shape[1:]:
                    w *= n
                v = ps[:, acc_bank(a), 0:w]
                return v.rearrange("p (k t) -> p k t", k=dst.shape[1]) if len(dst.shape) == 3 else v

            def pt_copy(dst, scale=1.0, bank=None):
                act.wait_ge(s_pt, c.pt + 1)
                rows = dst.shape[0]
                if bank is None:
                    bank = 2 + c.pt % 2
                src = ps[0:rows, bank, 0:SEQ * dst.shape[1]].rearrange("p (h t) -> p h t", t=SEQ) if len(dst.shape) == 3 \
                    else ps[0:rows, bank, 0:dst.shape[1]]
                nc.scalar.activation(dst, src, ACT.Copy, scale=scale).then_inc(s_pt_copied, 1)
                c.pt += 1

            def attention(n, fill=(), units=0):
                pt_of, first = {}, c.sc
                for s in range(n + 2):
                    if s < n:
                        u = c.sc
                        act.wait_ge(s_max, u + 1)
                        if s >= 2:
                            act.wait_ge(s_pt, pt_of[s - 2] + 1)
                        for hh in range(2):
                            ins = nc.scalar.activation(Pr[:, u % 2, 256 * hh:256 * hh + 256],
                                                       ps[:, u % 2, 256 * hh:256 * hh + 256], ACT.Exp,
                                                       bias=nmax[:, u % 4, hh:hh + 1],
                                                       accum_out=sums[:, u % 4, hh:hh + 1])
                        ins.then_inc(s_p, 1)
                        c.sc += 1
                    if 1 <= s <= n:
                        pt_of[s - 1] = c.pt
                        v = (first + s - 1) % 2
                        pt_copy(PT[:, v, :], bank=2)
                    share(fill, units, s, n + 2)

            def squares(parts, ready, between=None):
                if c.sums:
                    act.wait_ge(s_ssq, c.sums)
                at = 0
                junk = (Pr, PT)
                for i, (src, col) in enumerate(parts):
                    ready(i)
                    w = 1
                    for n in src.shape[1:]:
                        w *= n
                    dst = junk[at // 1024][:, :, :].rearrange("p a b -> p (a b)")[:, at % 1024:at % 1024 + w]
                    at += w
                    if len(src.shape) == 3:
                        dst = dst.rearrange("p (a b) -> p a b", a=src.shape[1])
                    ins = nc.scalar.activation(dst, src, ACT.Square, accum_out=ssq[:, col:col + 1])
                    if between is not None and i == 0:
                        ins.then_inc(s_sq1, 1)
                        act.wait_ge(*between)
                ins.then_inc(s_ssq, 1)
                c.sums += 1

            def x_squares(col, updated=True):
                squares([(x[:, t, :], col + t) for t in range(NT)],
                        lambda t: act.wait_ge(s_res, NT * c.post - NT + t + 1) if updated else None)

            def projected(col, split):
                assert c.acc % 4 == 0
                for half in range(2):
                    c.done += 4
                    advance(c.done + (4 if half == 0 else 0))
                    act.wait_ge(s_used, c.done)
                    for t in (1, 0):
                        if t == 0:
                            act.wait_ge(s_acc_free, c.acc + 1)
                        k = 2 * half + t
                        ins = nc.scalar.activation((Pr, PT)[half][:, t, :], ps[:, 4 + k, :], ACT.Square,
                                                   accum_out=ssq[:, col + k:col + k + 1])
                        if t == 1:
                            ins.then_inc(s_sq1, 1)
                    c.acc += 2
                ins.then_inc(s_ssq, 1)
                c.sums += 1
                c.post += 1
                advance(c.done + split)

            def transposed(hi, k0, widths):
                for w in widths:
                    acc_hi(hi[:, k0:k0 + w, :])
                    k0 += w

            def transposed_by_tile(hi):
                for t in range(NT):
                    for k0 in (0, 4):
                        acc_hi(hi[:, k0:k0 + 4, P * t:P * t + P])

            def linear(blocks, units, accs=2):
                for b in range(blocks):
                    for n in range(units):
                        c.done += 1
                        advance(c.done + 4)
                        yield
                    c.acc += accs

            def gated():
                for half in range(2):
                    assert c.acc % 4 == 0
                    for n in range(6):
                        c.done += 1
                        advance(c.done + 4)
                        if n == 3:
                            act.wait_ge(s_used, c.done)
                            act.wait_ge(s_acc_free, c.acc)
                            for t in range(NT):
                                ins = nc.scalar.activation(E4[:, t, :], ps[:, 4 + t, :], ACT.Tanh,
                                                           scale=rstd[:, N_MIX + t:N_MIX + t + 1])
                            ins.then_inc(s_gexp, 1)
                        yield
                    c.acc += 4

            def ffn(step0, u0, it0, nt):
                def silu(j, k, it, last):
                    act.wait_ge(s_used, it * LOOP_UNITS + last)
                    if not (step0 + j == 0):
                        act.wait_ge(s_hid, it * 2 + (step0 + j))
                    if nt == 1:
                        ins = nc.scalar.activation(sl[:, 0:FB], ps[:, 4 + k, 0:FB], ACT.Silu)
                    else:
                        for t in range(NT):
                            ins = nc.scalar.activation(sl[:, FB * t:FB * t + FB], ps[:, 4 + t, 0:FB], ACT.Silu,
                                                       scale=rstd[:, N_FFN + t:N_FFN + t + 1])
                    ins.then_inc(s_silu, 1)

                def hidT(j, par, it):
                    act.wait_ge(s_hidT, it * 2 + (step0 + j + 1))
                    nc.scalar.activation(hidT_hi[:, :, 0:P * nt],
                                         ps[:, 6 + par, 0:2 * P * nt].rearrange("p (k t) -> p k t", k=2),
                                         ACT.Copy).then_inc(s_hidT_hi, 1)

                for k in (2, 3):
                    act_split(act, u0 + k, it0)
                silu(0, 0, it0, u0 + 4)
                for k in (4, 5):
                    act_split(act, u0 + k, it0)
                with act.Fori(0, (NSTEP - 1) // 2) as i:
                    it = it0 + i
                    for j in range(2):
                        u = u0 + 4 + 6 * j
                        for k in (2, 3):
                            act_split(act, u + k, it)
                        hidT(j, j, it)
                        for k in (4, 5):
                            act_split(act, u + k, it)
                        silu(j + 1, (j + 1) % 2, it, u + 4)
                        for k in (6, 7):
                            act_split(act, u + k, it)

            def ffn_tail(step0, it0, nt):
                act.wait_ge(s_hidT, it0 * 2 + (step0 + NSTEP))
                nc.scalar.activation(hidT_hi[:, :, 0:P * nt],
                                     ps[:, 6, 0:2 * P * nt].rearrange("p (k t) -> p k t", k=2),
                                     ACT.Copy).then_inc(s_hidT_hi, 1)

            act.wait_ge(s_x, 16)
            for L in range(DEPTH):
                x_squares(N_MIX, L > 0)
                if L == 0:
                    advance(4)
                transposed_by_tile(hT_hi)
                if L == 0:
                    act.wait_ge(s_const, 64)
                    nc.scalar.activation(wr_hi[:, :, :], wr[:, :, :], ACT.Copy).then_inc(s_wr, 1)
                w_in = linear(3, 4)
                run(w_in, 2)
                act.wait_ge(s_mem, 16 * (L + 1))
                squares([(S1[:, t, :], N_MEM + t) for t in range(NT)], lambda t: None)
                run(w_in, 2)
                act.wait_ge(s_lamq, L + 1)
                nc.scalar.activation(lam[:, 2:4], lam[:, 0:2], ACT.Exp).then_inc(s_lame, 1)
                run(w_in, 5)
                act.wait_ge(s_acc_free, c.acc)
                squares([(Z[:, t, 0:Q_LORA], N_LAT + t) for t in range(NT)] +
                        [(Z[:, t, Q_LORA:C_ROPE], N_LAT + 2 + t) for t in range(NT)], lambda i: None)
                run(w_in)
                transposed(oT_hi, 0, (1, 1, 1, 2))
                run(linear(2, 2))
                run(linear(1, 2, 4))
                transposed(oT_hi, 0, (2, 2, 2, 2))
                others = linear(4, 4)
                run(others, 4)
                for h in range(0, MLA_H, 2):
                    pt_copy(qT[0:QK_MLA, h:h + 2, :], QK_MLA ** -0.5)
                for h in range(0, MLA_H, 2):
                    pt_copy(kT[0:QK_MLA, h:h + 2, :])
                attention(8, others, 12)
                run(others)
                transposed(oT_hi, 0, (2, 2))
                for h in range(0, 4, 2):
                    pt_copy(qT[:, h:h + 2, :], HD ** -0.5)
                pt_copy(kT[:, 0:1, :])
                others = gated()
                attention(8, others, 12)
                run(others)
                transposed(oT_hi, 0, (2, 2))
                run(linear(3, 4))
                for h in range(0, 4, 2):
                    pt_copy(qT[:, h:h + 2, :], DQK ** -0.5)
                for h in range(0, 4, 2):
                    pt_copy(kT[:, h:h + 2, :])
                others = gated()
                attention(16, others, 12)
                run(others)
                gates = gated()
                run(gates, 4)
                c.sums += 1
                for k in (0, 2):
                    pt_copy(oT_hi[:, k:k + 2, :])
                run(gates)
                transposed_by_tile(hT_hi)
                projected(N_POST, 4)
                for h in range(0, 8, 2):
                    pt_copy(kT[:, h:h + 2, :])
                x_squares(N_PRE)
                transposed_by_tile(hT_hi)
                run(linear(2, 4))
                for h in range(0, 8, 2):
                    pt_copy(qT[:, h:h + 2, :], MEM_HD ** -0.5)
                attention(4)
                transposed(hT_hi, 0, (2, 2, 2, 2))
                projected(N_POST2, 2 if L == 0 else 0)
                x_squares(N_FFN)
                transposed_by_tile(hT_hi)
                if L == 0:
                    act.wait_ge(s_rstd, c.sums)
                    ffn(0, FFN0[0], 0, NT)
                    ffn_tail(0, 0, NT)
                    c.unit = c.done = LAYER0[1]
                    act.wait_ge(s_used, c.done)
                    squares([(ps[:, 2 * t:2 * t + 2, :], N_POST + t) for t in (1, 0)], lambda t: None, (s_y0, 1))
                    c.post += 1
                    advance(c.done + 4)
            act.wait_ge(s_acc, c.rdy + 1)
            hrow = hT_hi[:, :, :].rearrange("p (t a) b -> p t (a b)", t=NT)
            nc.scalar.activation(hrow, ZU[:, :, 0:D], ACT.Copy).then_inc(s_hrow_hi, 1)
            act.wait_ge(s_topd, 1)
            nc.scalar.activation(EX, W1, ACT.Exp).then_inc(s_tope, 1)
            act.wait_ge(s_rounds, 1)
            nr = act.value_load(rounds[0:1, 0:1], min_val=1, max_val=2)

            def gather_hi(e, q):
                act.wait_ge(s_gath, q * 2 + (e + 1))
                nc.scalar.activation(ohT[:, e, :], ps[:, 7, 0:SEQ], ACT.Copy).then_inc(s_ohT, 1)
                nc.scalar.activation(oT_hi[:, :, 0:P],
                                     ps[:, 2 * e:2 * e + 2, :].rearrange("p b (k s) -> p (b k) s", k=4),
                                     ACT.Copy).then_inc(s_gath_hi, 1)

            def y_hi(e, q):
                act.wait_ge(s_used, q * (11 * LOOP_UNITS) + (FFN0[1] + FFN_UNITS * (e + 1)))
                nc.scalar.activation(oT_hi[:, :, P:2 * P],
                                     ps[:, 2 * e:2 * e + 2, :].rearrange("p b (k s) -> p (b k) s", k=4),
                                     ACT.Copy).then_inc(s_yhi, 1)

            with act.Fori(0, nr) as r:
                with act.Fori(0, NE // 2) as pr:
                    q = act.snap(r * (NE // 2) + pr)
                    it = act.snap(q * 11)
                    u0, st = FFN0[1], NSTEP
                    for k in (0, 1):
                        act_split(act, u0 + k, it)
                    gather_hi(0, q)
                    ffn(st, u0, it, 1)
                    gather_hi(1, q)
                    ffn_tail(st, it, 1)
                    for k in (0, 1):
                        act_split(act, u0 + FFN_UNITS + k, it)
                    y_hi(0, q)
                    ffn(st + NSTEP, u0 + FFN_UNITS, it, 1)
                    ffn_tail(st + NSTEP, it, 1)
                    y_hi(1, q)
            act.wait_ge(s_added, nr * (4 * NE) + 1)
            squares([(S1[:, t, :], N_POST + t) for t in range(NT)], lambda t: None)

        @blk.vector
        def _(dve):
            V = nc.vector
            c = Counts()

            def link(ins):
                c.chain += 1
                ins.then_inc(s_chain, 1)
                dve.wait_ge(s_chain, c.chain)

            def advance(limit):
                while c.unit < limit:
                    dve_split(dve, c.unit)
                    c.unit += 1

            def rows_done(ins):
                c.rows += 1
                ins.then_inc(s_rows, 1)

            def transposed(lo, hi, k0, widths):
                for w in widths:
                    dve.wait_ge(s_acc_hi, c.acc_hi + 1)
                    src = ps[:, acc_bank(c.acc), 0:w * SEQ].rearrange("p (k t) -> p k t", k=w)
                    V.tensor_tensor(lo[:, k0:k0 + w, :], src, hi[:, k0:k0 + w, :].bitcast(f32),
                                    ALU.subtract).then_inc(s_acc_free, 1)
                    c.acc += 1
                    c.rdy += 1
                    c.acc_hi += 1
                    k0 += w

            def transposed_by_tile():
                for t in range(NT):
                    for k0 in (0, 4):
                        dve.wait_ge(s_acc_hi, c.acc_hi + 1)
                        src = ps[:, acc_bank(c.acc), :].rearrange("p (k t) -> p k t", k=4)
                        part = (slice(None), slice(k0, k0 + 4), slice(P * t, P * t + P))
                        V.tensor_tensor(hT_lo[part], src, hT_hi[part].bitcast(f32), ALU.subtract).then_inc(s_acc_free, 1)
                        c.acc += 1
                        c.rdy += 1
                        c.acc_hi += 1

            def linear(blocks, units, dst, w, col, factor=1.0, free=None):
                for b in range(blocks):
                    for n in range(units):
                        c.done += 1
                        if n == units - 1:
                            dve.wait_ge(s_rstd, c.norm)
                            dve.wait_ge(s_used, c.done)
                            if free is not None:
                                free(b)
                            for t in range(NT):
                                to = dst(b, t)
                                for d, src in to if isinstance(to, list) else [(to, ps[:, acc_bank(c.acc), 0:w])]:
                                    ins = V.tensor_scalar(d, src, rstd[:, col + t:col + t + 1], factor, ALU.mult, ALU.mult)
                                ins.then_inc(s_acc_free, 1)
                                c.acc += 1
                        advance(c.done + 4)
                        yield

            def own_rows():
                if c.acc:
                    dve.wait_ge(s_acc_free, c.acc)
                if c.pv:
                    dve.wait_ge(s_pv_free, c.pv)

            def wait_gain():
                k = c.gain
                if k == 0:
                    dve.wait_ge(s_gain_first, 16)
                else:
                    dve.wait_ge(s_gain[k % 2], 16 * ((k + 1) // 2))
                c.gain += 1
                return k % 2

            def pre_gain(src, dst):
                g = wait_gain()
                for t in range(NT):
                    V.tensor_tensor(dst[:, t, 0:D], src[:, t, :], gains[:, g, :], ALU.mult).then_inc(s_norm, 1)
                c.pre += 1
                c.norm += 1

            def projected():
                assert c.acc % 4 == 0
                g = wait_gain()
                for half in range(2):
                    c.done += 4
                    advance(c.done + (4 if half == 0 else 0))
                    dve.wait_ge(s_used, c.done)
                    cols = slice(512 * half, 512 * half + 512)
                    for t in range(NT):
                        if t == 1:
                            c.sq1 += 1
                            dve.wait_ge(s_sq1, c.sq1)
                        V.tensor_tensor(S1[:, t, cols], ps[:, 4 + 2 * half + t, :], gains[:, g, cols],
                                        ALU.mult).then_inc(s_acc_free, 1)
                        c.acc += 1
                own_rows()

            def outputs_gained(outputs, rows, psum):
                g = wait_gain()
                for t in range(NT):
                    if psum and t == 1:
                        c.sq1 += 1
                        dve.wait_ge(s_sq1, c.sq1)
                    ins = V.tensor_tensor(rows[:, t, :], outputs(t), gains[:, g, :], ALU.mult)
                    if psum and t == 0:
                        ins.then_inc(s_y0, 1)
                        dve.wait_ge(s_y0, 1)
                    else:
                        link(ins)

            def post_norm(rows, col, split=0, then="gain"):
                advance(c.done + split)
                c.norm += 1
                if then != "end":
                    g = wait_gain()
                dve.wait_ge(s_rstd, c.norm)
                for t in range(NT):
                    V.scalar_tensor_tensor(x[:, t, :], rows[:, t, :], rstd[:, col + t:col + t + 1], x[:, t, :],
                                           ALU.mult, ALU.add).then_inc(s_final if then == "end" else s_res, 1)
                    if then == "gain":
                        dve.wait_ge(s_res, NT * c.post + t + 1)
                        V.tensor_tensor(ZU[:, t, 0:D], x[:, t, :], gains[:, g, :], ALU.mult).then_inc(s_norm, 1)
                c.post += 1
                if then != "end":
                    c.pre += 1
                    c.norm += 1
                if then == "norm":
                    dve.wait_ge(s_res, NT * c.post)
                    dve.wait_ge(s_rstd, c.norm)
                    for t in range(NT):
                        V.scalar_tensor_tensor(ZU[:, t, 0:D], x[:, t, :], rstd[:, N_FFN + t:N_FFN + t + 1], gains[:, g, :],
                                               ALU.mult, ALU.mult).then_inc(s_norm, 1)

            def rotate(view, dst, cos0, sin0, heads, half, tiles=range(NT)):
                n = heads * 2 * half
                own_rows()
                for t in tiles:
                    v = view(t)
                    a = scratch[:, 0:n].rearrange("p (h a d) -> p h a d", h=heads, a=2)
                    b = scratch[:, n:2 * n].rearrange("p (h a d) -> p h a d", h=heads, a=2)
                    co = rope[:, t, cos0:cos0 + half].unsqueeze(1).unsqueeze(1).broadcast_to([P, heads, 2, half])
                    si = rope[:, t, sin0:sin0 + half].unsqueeze(1).unsqueeze(1).broadcast_to([P, heads, 2, half])
                    V.tensor_tensor(a, v, co, ALU.mult)
                    link(V.tensor_tensor(b, v, si, ALU.mult))
                    d = dst(t)
                    V.tensor_tensor(d[0], a[:, :, 0, :], b[:, :, 1, :], ALU.subtract)
                    ins = V.tensor_tensor(d[1], a[:, :, 1, :], b[:, :, 0, :], ALU.add)
                    if t != tiles[-1]:
                        link(ins)
                return ins

            def attention(n, out, hd, diff=False, fill=(), units=0):
                u0 = c.sc
                for s in range(n + 2):
                    if s < n:
                        u = u0 + s
                        dve.wait_ge(s_sc, u + 1)
                        V.tensor_reduce(nmax[:, u % 4, :], ps[:, u % 2, :].rearrange("p (h k) -> p h k", h=2), AX,
                                        ALU.max, negate=True).then_inc(s_max, 1)
                    if 1 <= s <= n:
                        u = u0 + s - 1
                        dve.wait_ge(s_p, u + 1)
                        link(V.reciprocal(rsum[:, u % 4, :], sums[:, u % 4, :]))
                        if diff:
                            link(V.tensor_tensor(rsum[:, u % 4, 1:2], rsum[:, u % 4, 1:2], nlam[:, :], ALU.mult))
                    if s >= 2:
                        u = u0 + s - 2
                        c.pv += 1
                        dve.wait_ge(s_pv, c.pv)
                        dst = out(s - 2)
                        if diff:
                            link(V.tensor_scalar(dst, ps[:, 3, hd:2 * hd], rsum[:, u % 4, 1:2], None, ALU.mult))
                            V.scalar_tensor_tensor(dst, ps[:, 3, 0:hd], rsum[:, u % 4, 0:1], dst, ALU.mult,
                                                   ALU.add).then_inc(s_pv_free, 1)
                        else:
                            V.tensor_tensor(dst, ps[:, 3, 0:2 * hd].rearrange("p (h d) -> p h d", h=2),
                                            rsum[:, u % 4, :].unsqueeze(2).broadcast_to([P, 2, hd]),
                                            ALU.mult).then_inc(s_pv_free, 1)
                    share(fill, units, s, n + 2)
                c.sc += n
                c.pt += n

            def gated(br):
                for half in range(2):
                    for n in range(6):
                        c.done += 1
                        if n == 5:
                            c.gates += 1
                            dve.wait_ge(s_gexp, c.gates)
                            dve.wait_ge(s_used, c.done)
                            for t in range(NT):
                                m, g = S1[:, t, 512 * half:512 * half + 512], E4[:, t, :]
                                link(V.scalar_tensor_tensor(g, g, 1.0, ps[:, 6 + t, :], ALU.add, ALU.mult))
                                if br == 0:
                                    V.tensor_scalar(m, g, 0.5, None, ALU.mult).then_inc(s_acc_free, 2)
                                else:
                                    V.scalar_tensor_tensor(m, g, 0.5, m, ALU.mult, ALU.add).then_inc(s_acc_free, 2)
                            c.acc += 4
                        advance(c.done + 4)
                        yield

            def ffn(step0, u0, it0, nt, between=None):
                def hidden(j, k, it):
                    dve.wait_ge(s_silu, it * 2 + (step0 + j + 1))
                    if not (step0 + j == 0):
                        dve.wait_ge(s_hidT, it * 2 + (step0 + j))
                    if nt == 1:
                        ins = V.tensor_tensor(hid[:, 0:FB], sl[:, 0:FB], ps[:, 4 + k, FB:2 * FB], ALU.mult)
                    else:
                        for t in range(NT):
                            a = slice(FB * t, FB * t + FB)
                            ins = V.scalar_tensor_tensor(hid[:, a], ps[:, 4 + t, FB:2 * FB],
                                                         rstd[:, N_FFN + t:N_FFN + t + 1], sl[:, a], ALU.mult, ALU.mult)
                    ins.then_inc(s_hid, 1)

                for k in (2, 3):
                    dve_split(dve, u0 + k, it0)
                hidden(0, 0, it0)
                if between is not None:
                    between()
                for k in (4, 5):
                    dve_split(dve, u0 + k, it0)
                with dve.Fori(0, (NSTEP - 1) // 2) as i:
                    it = it0 + i
                    for j in range(2):
                        u = u0 + 4 + 6 * j
                        for k in (2, 3):
                            dve_split(dve, u + k, it)
                        hidT(step0, j, j, it, nt)
                        for k in (4, 5):
                            dve_split(dve, u + k, it)
                        hidden(j + 1, (j + 1) % 2, it)
                        for k in (6, 7):
                            dve_split(dve, u + k, it)

            def hidT(step0, j, par, it, nt):
                dve.wait_ge(s_hidT_hi, it * 2 + (step0 + j + 1))
                V.tensor_tensor(hidT_lo[:, :, 0:P * nt],
                                ps[:, 6 + par, 0:2 * P * nt].rearrange("p (k t) -> p k t", k=2),
                                hidT_hi[:, :, 0:P * nt].bitcast(f32), ALU.subtract).then_inc(s_hidT_lo, 1)

            dve.wait_ge(s_x, 16)
            pre_gain(x, ZU)
            for L in range(DEPTH):
                advance(c.done + 4)
                transposed_by_tile()
                w_in = linear(3, 4, lambda b, t: Z[:, t, W1C * b:W1C * b + W1C], W1C, N_MIX, 2.0)
                run(w_in, 2)
                dve.wait_ge(s_sg, 16 * 9 * (L + 1))
                lq = sg[:, SG_LAM:SG_LAM + 128].rearrange("p (m a d) -> p m a d", m=2, a=2)
                lp = scratch[:, 0:64].rearrange("p (m d) -> p m d", m=2)
                link(V.tensor_tensor(lp, lq[:, :, 0, :], lq[:, :, 1, :], ALU.mult))
                V.tensor_reduce(lam[:, 0:2], lp, AX, ALU.add).then_inc(s_lamq, 1)
                run(w_in, 3)
                if L == 0:
                    dve.wait_ge(s_wr, 1)
                    V.tensor_tensor(wr_lo[:, :, :], wr[:, :, :], wr_hi[:, :, :].bitcast(f32),
                                    ALU.subtract).then_inc(s_wrl, 1)
                dve.wait_ge(s_ssq, c.norm + 1)
                pre_gain(S1, S1)
                run(w_in, 3)
                own_rows()
                for t in range(NT):
                    for c0, c1, g in ((0, Q_LORA, SG_Q), (Q_LORA, C_ROPE, SG_KV)):
                        ins = V.tensor_tensor(ZU[:, t, c0:c1], Z[:, t, c0:c1], sg[:, g:g + c1 - c0], ALU.mult)
                rows_done(ins)
                c.norm += 1
                run(w_in, 2)
                dve.wait_ge(s_lame, L + 1)
                link(V.tensor_tensor(nlam[:, :], lam[:, 3:4], lam[:, 2:3], ALU.subtract))
                link(V.tensor_scalar(nlam[:, :], nlam[:, :], -LAMBDA_INIT[L], None, ALU.add))
                run(w_in)
                transposed(oT_lo, oT_hi, 0, (1, 1, 1, 2))
                run(linear(2, 2, lambda b, t: ZU[:, t, Q_LORA * b:Q_LORA * b + Q_LORA], Q_LORA, N_LAT))
                KF = ZU[:, :, 768:1536].rearrange("p t (h d) -> p t h d", d=QK_MLA)
                VM = ZU[:, :, 1536:2048]
                c.done += 2
                dve.wait_ge(s_used, c.done)
                for n in range(4):
                    t, hf = n // 2, n % 2
                    kv = ps[:, acc_bank(c.acc), :].rearrange("p (h a d) -> p h a d", h=4, a=2)
                    f = rstd[:, N_LAT + 2 + t:N_LAT + 3 + t]
                    V.tensor_scalar(KF[:, t, 4 * hf:4 * hf + 4, 0:NOPE], kv[:, :, 0, :], f, None, ALU.mult)
                    V.tensor_scalar(VM[:, t, 256 * hf:256 * hf + 256].rearrange("p (h d) -> p h d", h=4),
                                    kv[:, :, 1, :], f, None, ALU.mult).then_inc(s_acc_free, 1)
                    c.acc += 1
                advance(c.done + 4)
                transposed(oT_lo, oT_hi, 0, (2, 2, 2, 2))

                def spilled(b):
                    if 4 * L + b > 0:
                        dve.wait_ge(s_spill, 16 * (4 * L + b))

                others = linear(4, 4, lambda b, t: E4[:, t, :], 512, N_MEM, free=spilled)
                Q = ZU[:, :, 0:768].rearrange("p t (h d) -> p t h d", d=QK_MLA)
                KR = Z[:, :, C_ROPE:C_ROPE + ROT]
                for t in range(NT):
                    link(rotate(lambda t: Q[:, t, :, NOPE:].rearrange("p h (a d) -> p h a d", a=2),
                                lambda t: (Q[:, t, :, NOPE:NOPE + 16], Q[:, t, :, NOPE + 16:]), RC_M, RS_M, MLA_H, 16,
                                (t,)))
                    run(others, 1)
                link(rotate(lambda t: KR[:, t, :].rearrange("p (h a d) -> p h a d", h=1, a=2),
                            lambda t: (KR[:, t, 0:16].unsqueeze(1), KR[:, t, 16:32].unsqueeze(1)), RC_M, RS_M, 1, 16))
                for t in range(NT):
                    ins = V.tensor_copy(KF[:, t, :, NOPE:], KR[:, t, :].unsqueeze(1).broadcast_to([P, MLA_H, ROT]))
                rows_done(ins)
                run(others, 2)
                O = ZU[:, :, 0:BW]

                def out_pair(n):
                    return O[:, n % 2, P * (n // 2):P * (n // 2) + P].rearrange("p (h d) -> p h d", h=2)

                c.pt += 8
                attention(8, out_pair, HD, fill=others, units=12)
                run(others)
                transposed(oT_lo, oT_hi, 0, (2, 2))
                c.pt += 3
                dve.wait_ge(s_spill, 64 * (L + 1))
                others = gated(0)
                attention(8, out_pair, HD, fill=others, units=12)
                run(others)
                transposed(oT_lo, oT_hi, 0, (2, 2))
                def diff_rows(b, t):
                    src = ps[:, acc_bank(c.acc), :]
                    if b == 2:
                        return [(Z[:, t, 2 * W2C:3 * W2C], src)]
                    return [(Z[:, t, W2C * b + 256 * n:W2C * b + 256 * n + 256].rearrange("p (m h d) -> p h m d", m=2, d=DQK),
                             src[:, 256 * n:256 * n + 256].rearrange("p (h m d) -> p h m d", m=2, d=DQK)) for n in range(2)]

                w_in = linear(3, 4, diff_rows, W2C, N_MIX, 2.0)
                for b in range(2):
                    run(w_in, 5 if b == 0 else 4)
                    R = Z[:, :, 512 * b:512 * b + 512].rearrange("p t (h d) -> p t h d", d=DQK)
                    rows_done(rotate(lambda t: R[:, t, :, 0:DROT].rearrange("p h (a d) -> p h a d", a=2),
                                     lambda t: (R[:, t, :, 0:4], R[:, t, :, 4:8]), RC_P, RS_P, 16, 4))
                run(w_in)
                c.pt += 4
                others = gated(1)
                attention(16, lambda n: O[:, n % 2, DV * (n // 2):DV * (n // 2) + DV], DV, diff=True, fill=others, units=12)
                run(others)
                own_rows()
                others = gated(2)
                for t in range(NT):
                    sq = scratch[:, BW * t:BW * t + BW]
                    link(V.tensor_tensor(sq, O[:, t, :], O[:, t, :], ALU.mult))
                    ins = V.tensor_reduce(ssq[:, N_DIFF + 8 * t:N_DIFF + 8 * t + 8],
                                          sq.rearrange("p (h d) -> p h d", d=DV), AX, ALU.add)
                ins.then_inc(s_ssq, 1)
                c.norm += 1
                run(others, 1)
                gain = sg[:, SG_SUB:SG_SUB + DV].unsqueeze(1).broadcast_to([P, DIFF_H, DV])
                heads = [O[:, t, :].rearrange("p (h d) -> p h d", d=DV) for t in range(NT)]
                for v in heads:
                    link(V.tensor_tensor(v, v, gain, ALU.mult))
                run(others, 1)
                dve.wait_ge(s_rstd, c.norm)
                for t, v in enumerate(heads):
                    f = rstd[:, N_DIFF + 8 * t:N_DIFF + 8 * t + 8].unsqueeze(2).broadcast_to([P, DIFF_H, DV])
                    ins = V.tensor_tensor(v, v, f, ALU.mult)
                rows_done(ins)
                run(others, 2)
                for k in (0, 2):
                    c.pt += 1
                    dve.wait_ge(s_pt_copied, c.pt)
                    src = ps[:, 2 + (c.pt - 1) % 2, :].rearrange("p (k t) -> p k t", k=2)
                    V.tensor_tensor(oT_lo[:, k:k + 2, :], src, oT_hi[:, k:k + 2, :].bitcast(f32),
                                    ALU.subtract).then_inc(s_subT, 1)
                run(others)
                transposed_by_tile()
                projected()
                post_norm(S1, N_POST, split=4)
                c.pt += 4
                transposed_by_tile()
                run(linear(2, 4, lambda b, t: ZU[:, t, 512 * b:512 * b + 512], 512, N_PRE))
                c.pt += 4
                attention(4, lambda n: S1[:, n % 2, 512 * (n // 2):512 * (n // 2) + 512]
                          .rearrange("p (h d) -> p h d", h=2), MEM_HD)
                transposed(hT_lo, hT_hi, 0, (2, 2, 2, 2))
                projected()
                post_norm(S1, N_POST2, split=2 if L == 0 else 0, then="gain" if L == 0 else "norm")
                transposed_by_tile()
                if L == 0:
                    dve.wait_ge(s_rstd, c.norm)
                    ffn(0, FFN0[0], 0, NT)
                    hidT(0, NSTEP - 1, 0, 0, NT)
                    dve.wait_ge(s_used, FFN0[0] + FFN_UNITS)
                    c.unit = c.done = LAYER0[1]
                    outputs_gained(lambda t: ps[:, 2 * t:2 * t + 2, :].rearrange("p b n -> p (b n)"), S1, True)
                    post_norm(S1, N_POST)
            hrow_lo = hT_lo[:, :, :].rearrange("p (t a) b -> p t (a b)", t=NT)
            hrow_hi = hT_hi[:, :, :].rearrange("p (t a) b -> p t (a b)", t=NT)

            def bc(v):
                return v.unsqueeze(2).broadcast_to([P, NT, NE])

            io8 = iota[:, 0:NE].unsqueeze(1).broadcast_to([P, NT, NE])

            def first_max(src, m, onehot):
                link(V.tensor_reduce(m, src, AX, ALU.max))
                link(V.tensor_tensor(EQ, src, bc(m), ALU.is_equal))
                link(V.tensor_scalar(CC, EQ, -99.0, 99.0, ALU.mult, ALU.add))
                link(V.tensor_tensor(CC, CC, io8, ALU.add))
                link(V.tensor_reduce(I1, CC, AX, ALU.min))
                link(V.tensor_tensor(onehot, CC, bc(I1), ALU.is_equal))

            dve.wait_ge(s_acc, c.rdy + 1)
            lg = ps[:, acc_bank(c.acc), 0:16].rearrange("p (t e) -> p t e", t=NT)
            link(V.tensor_tensor(LG, lg, brt[:, :].unsqueeze(1).broadcast_to([P, NT, NE]), ALU.add))
            first_max(LG, M1, OH1)
            link(V.tensor_scalar(L2, OH1, -3.0e38, None, ALU.mult))
            link(V.tensor_tensor(L2, L2, LG, ALU.add))
            first_max(L2, M2, OH2)
            V.tensor_tensor(W1, M2, M1, ALU.subtract).then_inc(s_topd, 1)
            rows_done(V.tensor_tensor(MASK, OH1, OH2, ALU.add))
            dve.wait_ge(s_hrow_hi, 1)
            V.tensor_tensor(hrow_lo, ZU[:, :, 0:D], hrow_hi.bitcast(f32), ALU.subtract).then_inc(s_hrow, 1)
            dve.wait_ge(s_tope, 1)
            link(V.tensor_scalar(W1, EX, 1.0, None, ALU.add))
            link(V.reciprocal(W1, W1))
            link(V.tensor_tensor(W2, EX, W1, ALU.mult))
            link(V.tensor_tensor(OH1, OH1, bc(W1), ALU.mult))
            link(V.tensor_tensor(OH2, OH2, bc(W2), ALU.mult))
            link(V.tensor_tensor(GATE, OH1, OH2, ALU.add))
            V.memset(S1[:, :, :], 0.0).then_inc(s_added, 1)
            dve.wait_ge(s_rows, c.rows)
            dve.wait_ge(s_acc, c.rdy + 2)
            rk = ps[:, acc_bank(c.acc + 1), 0:16].rearrange("p (t e) -> p t e", t=NT)
            link(V.tensor_scalar(RANKM, MASK, -1000.0, 1000.0, ALU.mult, ALU.add))
            V.tensor_tensor(RANKM, RANKM, rk, ALU.add).then_inc(s_rank, 1)
            link(V.tensor_reduce(MX, ps[:, acc_bank(c.acc + 1), 16:24], AX, ALU.max))
            link(V.tensor_scalar(NR, MX, float(P), 1.0, ALU.is_gt, ALU.add))
            V.tensor_copy(rounds[:, :], NR).then_inc(s_rounds, 1)
            dve.wait_ge(s_rounds, 1)
            nr = dve.value_load(rounds[0:1, 0:1], min_val=1, max_val=2)

            def one_hot(e, q, pr, r):
                if e == 0:
                    dve.wait_ge(s_rank, r + 1)
                else:
                    dve.wait_ge(s_gath, q * 2 + 1)
                for t in range(NT):
                    ins = V.tensor_scalar(oh[:, t, :], iota[:, :], RANKM[:, t, bass.ds(pr * 2 + e, 1)], None, ALU.is_equal)
                ins.then_inc(s_oh, 1)

            def banks(e):
                return ps[:, 2 * e:2 * e + 2, :].rearrange("p b (k s) -> p (b k) s", k=4)

            def gather_lo(e, q):
                dve.wait_ge(s_gath_hi, q * 2 + (e + 1))
                V.tensor_tensor(oT_lo[:, :, 0:P], banks(e), oT_hi[:, :, 0:P].bitcast(f32),
                                ALU.subtract).then_inc(s_gath_lo, 1)

            def y_lo(e, q):
                dve.wait_ge(s_yhi, q * 2 + (e + 1))
                V.tensor_tensor(oT_lo[:, :, P:2 * P], banks(e), oT_hi[:, :, P:2 * P].bitcast(f32),
                                ALU.subtract).then_inc(s_ylo, 1)

            def add_scattered(e, q, pr):
                for n in range(4):
                    t, hf = n // 2, n % 2
                    dve.wait_ge(s_scat, q * 8 + (4 * e + n + 1))
                    if n == 0:
                        dve.wait_ge(s_added, q * 8 + (4 * e + 1))
                    bk = (2 * e, 2 * e + 1, 6, 7)[n]
                    dst = S1[:, t, 512 * hf:512 * hf + 512]
                    V.scalar_tensor_tensor(dst, ps[:, bk, :], GATE[:, t, bass.ds(pr * 2 + e, 1)], dst,
                                           ALU.mult, ALU.add).then_inc(s_added, 1)

            with dve.Fori(0, nr) as r:
                with dve.Fori(0, NE // 2) as pr:
                    q = dve.snap(r * (NE // 2) + pr)
                    it = dve.snap(q * 11)
                    u0, st = FFN0[1], NSTEP
                    one_hot(0, q, pr, r)
                    for k in (0, 1):
                        dve_split(dve, u0 + k, it)
                    gather_lo(0, q)
                    one_hot(1, q, pr, r)
                    ffn(st, u0, it, 1)
                    gather_lo(1, q)
                    hidT(st, NSTEP - 1, 0, it, 1)
                    for k in (0, 1):
                        dve_split(dve, u0 + FFN_UNITS + k, it)
                    y_lo(0, q)
                    ffn(st + NSTEP, u0 + FFN_UNITS, it, 1, between=lambda: add_scattered(0, q, pr))
                    hidT(st + NSTEP, NSTEP - 1, 0, it, 1)
                    y_lo(1, q)
                    add_scattered(1, q, pr)
                V.tensor_scalar(RANKM, RANKM, -float(P), None, ALU.add).then_inc(s_rank, 1)
            dve.wait_ge(s_added, nr * (4 * NE) + 1)
            outputs_rows = scratch.rearrange("p (t d) -> p t d", t=NT)
            outputs_gained(lambda t: S1[:, t, :], outputs_rows, False)
            post_norm(outputs_rows, N_POST, then="end")

        @blk.tensor
        def _(pe):
            T = nc.tensor
            c = Counts()

            def three(out, a_hi, a_lo, b_hi, b_lo, start, stop):
                T.matmul(out, a_hi, b_hi, start=start, stop=False)
                T.matmul(out, a_hi, b_lo, start=False, stop=False)
                return T.matmul(out, a_lo, b_hi, start=False, stop=stop)

            def unit(us, it, nk, w, k0, act, outs, first, last):
                pe.wait_ge(s_lo, it * LOOP_UNITS + (us + 1))
                a_hi, a_lo = act
                for k in range(nk):
                    for a, bk, c0, n in outs:
                        col = k * w + c0
                        b_hi = w_hi[:, hi_slot(us), col:col + n]
                        b_lo = w_lo[:, hi_slot(us), col:col + n]
                        ins = three(ps[:, bk, 0:n], a(a_hi, k0 + k), a(a_lo, k0 + k), b_hi, b_lo,
                                    first and k == 0, last and k == nk - 1)
                ins.then_inc(s_used, 1)

            def tok(t):
                return lambda src, k: src[:, k, P * t:P * t + P]

            def claim(n):
                if c.acc + n > 4:
                    pe.wait_ge(s_acc_free, c.acc + n - 4)

            def block(w, nks, act):
                claim(2)
                outs = [(tok(t), acc_bank(c.acc + t), 0, w) for t in range(NT)]
                k0 = 0
                for n, nk in enumerate(nks):
                    unit(c.done, 0, nk, w, k0, act, outs, n == 0, n == len(nks) - 1)
                    c.done += 1
                    k0 += nk
                    if n == len(nks) - 1:
                        c.acc += 2
                    yield

            def split_T(src, widths):
                k = 0
                for w in widths:
                    claim(1)
                    for n in range(w * NT):
                        kk, t = k + n // NT, n % NT
                        ins = T.transpose(ps[:, acc_bank(c.acc), P * n:P * n + P], src(t)[:, P * kk:P * kk + P],
                                          ident[:, :])
                    ins.then_inc(s_acc, 1)
                    c.acc += 1
                    c.rdy += 1
                    k += w

            def blocks(n, w, nks, act):
                for b in range(n):
                    yield from block(w, nks, act)

            def split_ready():
                pe.wait_ge(s_acc_free, c.acc)

            def split_T_by_tile(src, ready):
                for t in range(NT):
                    ready(t)
                    for k0 in (0, 4):
                        claim(1)
                        for n in range(4):
                            ins = T.transpose(ps[:, acc_bank(c.acc), P * n:P * n + P],
                                              src[:, t, P * (k0 + n):P * (k0 + n) + P], ident[:, :])
                        ins.then_inc(s_acc, 1)
                        c.acc += 1
                        c.rdy += 1

            def plain_T(cols, heads, width):
                for h in range(0, heads, 2):
                    if c.pt >= 2:
                        pe.wait_ge(s_pt_copied, c.pt - 1)
                    for n in range(2 * min(2, heads - h)):
                        hh, t = h + n // 2, n % 2
                        ins = T.transpose(ps[0:width, 2 + c.pt % 2, P * n:P * n + P], cols(t, hh), ident[:, :])
                    ins.then_inc(s_pt, 1)
                    c.pt += 1

            def attention(n, scores, values, hd, fill=(), units=0):
                u0 = c.sc
                copied = {}
                for s in range(n + 2):
                    if s < n:
                        u = u0 + s
                        if u >= 2:
                            pe.wait_ge(s_p, u - 1)
                        if s == 0:
                            pe.wait_ge(s_pt_copied, c.pt)
                        for hh in range(2):
                            pairs = scores(s, hh)
                            for m, (q, k) in enumerate(pairs):
                                ins = T.matmul(ps[:, u % 2, 256 * hh:256 * hh + 256], q, k, start=m == 0,
                                               stop=m == len(pairs) - 1)
                        ins.then_inc(s_sc, 1)
                    share(fill, units, s, n + 2)
                    if 1 <= s <= n:
                        u = u0 + s - 1
                        pe.wait_ge(s_p, u + 1)
                        pe.wait_ge(s_pt_copied, c.pt)
                        for m in range(4):
                            ins = T.transpose(ps[:, 2, P * m:P * m + P], Pr[:, u % 2, P * m:P * m + P], ident[:, :])
                        ins.then_inc(s_pt, 1)
                        c.pt += 1
                        copied[s - 1] = c.pt
                    if s >= 2:
                        u = u0 + s - 2
                        pe.wait_ge(s_pt_copied, copied[s - 2])
                        if s >= 3:
                            pe.wait_ge(s_pv_free, c.pv)
                        for hh in range(2):
                            for kt in range(2):
                                ins = T.matmul(ps[:, 3, hd * hh:hd * hh + hd],
                                               PT[:, u % 2, 256 * hh + P * kt:256 * hh + P * kt + P],
                                               values(s - 2, hh, kt), start=kt == 0, stop=kt == 1)
                        ins.then_inc(s_pv, 1)
                        c.pv += 1
                pe.wait_ge(s_pv_free, c.pv)
                c.sc += n

            def gated():
                for half in range(2):
                    yield from block(512, (2, 2, 2, 2), (hT_hi, hT_lo))
                    yield from block(512, (2, 2), (oT_hi, oT_lo))

            def hid_T(step0, j, par, it, nt):
                pe.wait_ge(s_hid, it * 2 + (step0 + j + 1))
                for k in range(2):
                    for t in range(nt):
                        ins = T.transpose(ps[:, 6 + par, P * (k * nt + t):P * (k * nt + t) + P],
                                          hid[:, FB * t + P * k:FB * t + P * k + P], ident[:, :])
                ins.then_inc(s_hidT, 1)

            def gate_up(us, it, step0, j, par, nt, act, half):
                if half == 0 and j > 0:
                    pe.wait_ge(s_hid, it * 2 + (step0 + j - (0 if nt == 2 else 1)))
                outs = [(tok(t), 4 + (t if nt == 2 else par), 0, 512) for t in range(nt)]
                for k in range(2):
                    unit(us + k, it, 2, 512, 4 * half + 2 * k, act, outs, half == 0 and k == 0, half == 1 and k == 1)

            def down(us, it, step0, j, nt, y0, first, last):
                pe.wait_ge(s_hidT_lo, it * 2 + (step0 + j + 1))
                for k in range(2):
                    outs = [(tok(t), y0 + 2 * t + hf, 512 * hf, 512) for t in range(nt) for hf in range(2)]
                    unit(us + k, it, 1, 1024, k, (hidT_hi, hidT_lo), outs, first and k == 0, last and k == 1)

            def ffn_steps(step0, u0, it0, nt, act, y0):
                def pair(it, first):
                    for j in range(2):
                        u = u0 + 4 + 6 * j
                        gate_up(u, it, step0, j + 1, (j + 1) % 2, nt, act, 0)
                        hid_T(step0, j, j, it, nt)
                        gate_up(u + 2, it, step0, j + 1, (j + 1) % 2, nt, act, 1)
                        down(u + 4, it, step0, j, nt, y0, first and j == 0, False)

                pair(it0, True)
                with pe.Fori(1, (NSTEP - 1) // 2) as i:
                    pair(it0 + i, False)

            def ffn_end(step0, u0, it0, nt, y0):
                hid_T(step0, NSTEP - 1, 0, it0, nt)
                down(u0 + FFN_UNITS - 2, it0, step0, NSTEP - 1, nt, y0, False, True)

            def rows_ready():
                c.rows += 1
                pe.wait_ge(s_rows, c.rows)

            def gained_T(src):
                split_T_by_tile(src, lambda t: pe.wait_ge(s_norm, NT * c.pre + t + 1))
                c.pre += 1

            pe.wait_ge(s_ident, 16)
            for L in range(DEPTH):
                gained_T(ZU)
                split_ready()
                run(blocks(3, W1C, (2, 2, 2, 2), (hT_hi, hT_lo)))
                rows_ready()
                split_T(lambda t: ZU[:, t, 0:C_ROPE], (1, 1, 1, 2))
                split_ready()
                run(blocks(2, Q_LORA, (2, 1), (oT_hi, oT_lo)))
                claim(4)
                for k in range(2):
                    unit(c.done, 0, 1, 1024, 3 + k, (oT_hi, oT_lo),
                         [(tok(t), acc_bank(c.acc + 2 * t + hf), 512 * hf, 512) for t in range(NT) for hf in range(2)],
                         k == 0, k == 1)
                    c.done += 1
                c.acc += 4
                c.pre += 1
                pe.wait_ge(s_norm, NT * c.pre)
                split_T(lambda t: S1[:, t, :], (2, 2, 2, 2))
                assert c.rdy == T_MEM[L] and c.acc == LAYER_BANKS * L + KV_BANK
                split_ready()
                others = blocks(4, 512, (2, 2, 2, 2), (oT_hi, oT_lo))
                run(others, 4)
                rows_ready()
                plain_T(lambda t, h: ZU[:, t, QK_MLA * h:QK_MLA * h + QK_MLA], MLA_H, QK_MLA)
                plain_T(lambda t, h: ZU[:, t, 768 + QK_MLA * h:768 + QK_MLA * h + QK_MLA], MLA_H, QK_MLA)

                def mla_scores(s, hh):
                    h, t = 2 * (s // 2) + hh, s % 2
                    return [(qT[0:QK_MLA, h, P * t:P * t + P], kT[0:QK_MLA, h, :])]

                def mla_values(s, hh, kt):
                    c0 = 1536 + MLA_V * (2 * (s // 2) + hh)
                    return ZU[:, kt, c0:c0 + MLA_V]

                attention(8, mla_scores, mla_values, HD, others, 12)
                split_T(lambda t: ZU[:, t, 0:BW], (2, 2))
                pe.wait_ge(s_gqa, L + 1)
                plain_T(lambda t, h: Z[:, t, C_GQA + P * h:C_GQA + P * h + P], GQA_QH // GQA_KVH, P)
                plain_T(lambda t, h: Z[:, t, C_GQA + BW:C_GQA + BW + P], 1, P)

                group = GQA_QH // GQA_KVH

                def gqa_scores(s, hh):
                    h, t = 2 * (s // 2) + hh, s % 2
                    r = HD * (h // group)
                    return [(qT[r:r + HD, h % group, P * t:P * t + P], kT[r:r + HD, 0, :])]

                def gqa_values(s, hh, kt):
                    c0 = C_GQA + HD * (GQA_QH + GQA_KVH + (2 * (s // 2) + hh) // group)
                    return Z[:, kt, c0:c0 + HD]

                split_ready()
                attention(8, gqa_scores, gqa_values, HD, gated(), 12)
                split_T(lambda t: ZU[:, t, 0:BW], (2, 2))
                run(blocks(3, W2C, (2, 2, 2, 2), (hT_hi, hT_lo)))
                for c0 in (0, 512):
                    rows_ready()
                    plain_T(lambda t, h: Z[:, t, c0 + P * h:c0 + P * h + P], DIFF_H // 2, P)

                def diff_scores(s, m):
                    h, t = s // 2, s % 2
                    n, r = 2 * (h // 4) + m, DQK * (h % 4)
                    return [(qT[r:r + DQK, n, P * t:P * t + P], kT[r:r + DQK, n, :])]

                def diff_values(s, m, kt):
                    c0 = 1024 + DV * (s // 2)
                    return Z[:, kt, c0:c0 + DV]

                attention(16, diff_scores, diff_values, DV, gated(), 12)
                gates = gated()
                run(gates, 4)
                rows_ready()
                plain_T(lambda t, k: ZU[:, t, P * k:P * k + P], 4, P)
                pe.wait_ge(s_subT, 2 * (L + 1))
                run(gates)
                merged = c.acc
                split_T_by_tile(S1, lambda t: pe.wait_ge(s_acc_free, merged - 2 + 2 * t))
                split_ready()
                run(blocks(2, 512, (2, 2, 2, 2), (hT_hi, hT_lo)))
                pe.wait_ge(s_kmem, 16 * (L + 1))
                plain_T(lambda t, h: ZU[:, t, 1024 + P * h:1024 + P * h + P], 8, P)
                gained_T(ZU)
                split_ready()
                run(blocks(2, 512, (2, 2, 2, 2), (hT_hi, hT_lo)))
                for half in range(2):
                    pe.wait_ge(s_acc_free, c.acc - 2 + 2 * half)
                    plain_T(lambda t, h: ZU[:, t, 512 * half + P * h:512 * half + P * h + P], 4, P)

                def mem_scores(s, hh):
                    h, t = 2 * (s // 2) + hh, s % 2
                    return [(qT[:, 2 * h + k, P * t:P * t + P], kT[:, 2 * h + k, :]) for k in range(2)]

                def mem_values(s, hh, kt):
                    h = 2 * (s // 2) + hh
                    return Z[:, kt, MEM_HD * h:MEM_HD * h + MEM_HD]

                pe.wait_ge(s_vmem, 16 * (L + 1))
                attention(4, mem_scores, mem_values, MEM_HD)
                split_T(lambda t: S1[:, t, :], (2, 2, 2, 2))
                split_ready()
                run(blocks(2, 512, (2, 2, 2, 2), (hT_hi, hT_lo)))
                gained_T(ZU)
                split_ready()
                if L == 0:
                    for half in range(2):
                        gate_up(FFN0[0] + 2 * half, 0, 0, 0, 0, NT, (hT_hi, hT_lo), half)
                    ffn_steps(0, FFN0[0], 0, NT, (hT_hi, hT_lo), 0)
                    ffn_end(0, FFN0[0], 0, NT, 0)
                    c.done = LAYER0[1]
            pe.wait_ge(s_wrl, 1)
            claim(2)
            bk = acc_bank(c.acc)
            for t in range(NT):
                for k in range(8):
                    ins = three(ps[:, bk, NE * t:NE * t + NE], hT_hi[:, k, P * t:P * t + P],
                                hT_lo[:, k, P * t:P * t + P], wr_hi[:, k, :], wr_lo[:, k, :], k == 0, k == 7)
            ins.then_inc(s_acc, 1)
            pe.wait_ge(s_tri, 32)
            rows_ready()
            bk = acc_bank(c.acc + 1)
            T.matmul(ps[:, bk, 0:NE], tri, MASK[:, 0, :], start=True, stop=True)
            T.matmul(ps[:, bk, NE:2 * NE], tri, MASK[:, 1, :], start=True, stop=False)
            T.matmul(ps[:, bk, NE:2 * NE], ones, MASK[:, 0, :], start=False, stop=True)
            T.matmul(ps[:, bk, 2 * NE:3 * NE], ones, MASK[:, 0, :], start=True, stop=False)
            T.matmul(ps[:, bk, 2 * NE:3 * NE], ones, MASK[:, 1, :], start=False, stop=True).then_inc(s_acc, 1)
            pe.wait_ge(s_hrow, 1)
            pe.wait_ge(s_rounds, 1)
            nr = pe.value_load(rounds[0:1, 0:1], min_val=1, max_val=2)
            rows_hi = hT_hi[:, :, :].rearrange("p (t a) b -> p t (a b)", t=NT)
            rows_lo = hT_lo[:, :, :].rearrange("p (t a) b -> p t (a b)", t=NT)

            def gather(e, q):
                pe.wait_ge(s_oh, q * 2 + (e + 1))
                pe.wait_ge(s_added, q * 8 + 1)
                for t in range(NT):
                    T.transpose(ps[:, 7, P * t:P * t + P], oh[:, t, :].bitcast(f32), ident[:, :])
                for k in range(8):
                    out = ps[:, 2 * e + k // 4, P * (k % 4):P * (k % 4) + P]
                    for n in range(4):
                        t, src = n // 2, (rows_hi, rows_lo)[n % 2]
                        ins = T.matmul(out, src[:, t, P * k:P * k + P], oh[:, t, :], start=n == 0, stop=n == 3)
                ins.then_inc(s_gath, 1)

            def scatter(e, q):
                pe.wait_ge(s_ylo, q * 2 + (e + 1))
                pe.wait_ge(s_ohT, q * 2 + 2)
                for n in range(4):
                    t, hf = n // 2, n % 2
                    bk = (2 * e, 2 * e + 1, 6, 7)[n]
                    for m, src in enumerate((oT_hi, oT_lo)):
                        ins = T.matmul(ps[:, bk, :], ohT[:, e, P * t:P * t + P], src[:, 4 * hf:4 * hf + 4, P:2 * P],
                                       start=m == 0, stop=m == 1)
                    ins.then_inc(s_scat, 1)

            def expert_start(e, q, it):
                pe.wait_ge(s_gath_lo, q * 2 + (e + 1))
                pe.wait_ge(s_hid, it * 2 + (NSTEP + NSTEP * e))
                for half in range(2):
                    gate_up(FFN0[1] + FFN_UNITS * e + 2 * half, it, NSTEP * (e + 1), 0, 0, 1, (oT_hi, oT_lo), half)

            with pe.Fori(0, nr) as r:
                with pe.Fori(0, NE // 2) as pr:
                    q = pe.snap(r * (NE // 2) + pr)
                    it = pe.snap(q * 11)
                    gather(0, q)
                    expert_start(0, q, it)
                    ffn_steps(NSTEP, FFN0[1], it, 1, (oT_hi, oT_lo), 0)
                    gather(1, q)
                    ffn_end(NSTEP, FFN0[1], it, 1, 0)
                    expert_start(1, q, it)
                    scatter(0, q)
                    pe.wait_ge(s_added, q * 8 + 5)
                    ffn_steps(2 * NSTEP, FFN0[1] + FFN_UNITS, it, 1, (oT_hi, oT_lo), 2)
                    ffn_end(2 * NSTEP, FFN0[1] + FFN_UNITS, it, 1, 2)
                    scatter(1, q)


_INS = ['x', 'mem', 'mix_pre_g', 'mix_post_g', 'w_in', 'mla_q_norm_g', 'mla_w_q_up', 'mla_kv_norm_g', 'mla_w_kv_up',
        'gqa_q_norm_g', 'gqa_k_norm_g', 'diff_lambda_q1', 'diff_lambda_k1', 'diff_lambda_q2', 'diff_lambda_k2',
        'diff_subln_g', 'w_branch', 'w_out', 'mem_pre_g', 'mem_post_g', 'mem_norm_g', 'mem_wq', 'mem_wkv', 'mem_wo',
        'ffn_pre_g', 'ffn_post_g', 'dense_w_gate', 'dense_w_up', 'dense_w_down', 'moe_w_router', 'moe_b_router',
        'moe_w_gate', 'moe_w_up', 'moe_w_down']


def rope_table():
    import numpy as np
    f = np.float32

    def cos_sin(pos, rot):
        inv = f(500000.0) ** (-np.arange(0, rot, 2, dtype=f) / f(rot))
        ang = pos.astype(f)[:, None] * inv.astype(f)[None, :]
        return np.cos(ang), np.sin(ang)

    pos = np.arange(SEQ)
    cm, sm = cos_sin(pos, ROT)
    cr, sr = cos_sin(pos // 64, HD // 2)
    cc, sc = cos_sin(pos % 64, HD // 2)
    cp, sp = cos_sin(pos, DROT)
    return np.concatenate([cm, sm, cr, cc, sr, sc, cp, sp], axis=1).astype(f)


def constants():
    import numpy as np
    return np.stack([np.eye(P), np.tile(np.arange(P), (P, 1)), np.triu(np.ones((P, P)), 1), np.ones((P, P))]).astype(np.float32)


def kernel(**inputs):
    import numpy as _np
    import concourse.bacc as _bacc
    from concourse import mybir as _mybir
    from concourse.bass_utils import run_bass_kernel_spmd as _run

    nc = _bacc.Bacc("TRN2", target_bir_lowering=False, num_devices=1)
    arrays, aps = {}, {}
    named = [(name, _np.ascontiguousarray(inputs[name])) for name in _INS]
    named += [("rope", rope_table()), ("consts", constants())]
    for name, a in named:
        arrays[f"in_{name}_dram"] = a
        aps[name] = nc.dram_tensor(f"in_{name}_dram", a.shape, _mybir.dt.from_np(a.dtype), kind="ExternalInput").ap()
    aps["out"] = nc.dram_tensor("out_0_dram", (1, SEQ, D), _mybir.dt.float32, kind="ExternalOutput").ap()
    build(nc, aps)
    r = _run(nc, [arrays], core_ids=[0])
    return r.results[0]["out_0_dram"]
```

```python
import concourse.bass as bass
from concourse import mybir
from contextlib import ExitStack
from itertools import islice

D = 1024
SEQ = 256
P = 128
NT = SEQ // P
DEPTH = 2
MEM_LEN = 256
EPS = 1e-6
MLA_H, Q_LORA, KV_LORA, NOPE, ROT, MLA_V = 8, 384, 256, 64, 32, 64
GQA_QH, GQA_KVH, HD = 8, 2, 64
DIFF_H, DQK, DV, DROT = 8, 32, 64, 8
BW = 512
MEM_H, MEM_HD = 4, 256
F = 2816
NE = 8
QK_MLA = NOPE + ROT
C_ROPE = Q_LORA + KV_LORA
C_GQA = C_ROPE + ROT
N1 = C_GQA + (GQA_QH + 2 * GQA_KVH) * HD
N2 = 3 * DIFF_H * DV
GATE0 = N1 + N2
W1C, W2C = N1 // 3, N2 // 3
FB = 256
NSTEP = F // FB
LAMBDA_INIT = [0.8 - 0.6 * (2.718281828459045 ** (-0.3 * layer)) for layer in range(DEPTH)]
SG_Q, SG_KV, SG_GQ, SG_GK, SG_SUB, SG_LAM, SG_N = 0, 384, 640, 704, 768, 832, 960
RC_M, RS_M, RC_A, RS_A, RC_P, RS_P, R_N = 0, 16, 32, 64, 96, 100, 104
RAW_SLOTS, UNIT_SLOTS = 6, 4
KV_BANK, LAYER_BANKS = 26, 92
LAYER_PV = (MLA_H + GQA_QH + 2 * DIFF_H + MEM_H) * NT // 2
ACC_LAYER = 4 + 4 + 4 + 4 + 4 + 4 + 4
N_MIX, N_MEM, N_LAT, N_DIFF, N_POST, N_PRE, N_POST2, N_FFN, N_COLS = 0, 2, 4, 8, 24, 28, 30, 34, 36
LOOP_UNITS = 12


def unit_widths():
    w = [2 * W1C] * 12
    w += [2 * Q_LORA, Q_LORA] * 2
    w += [1024] * 2
    w += [1024] * 16
    w += [1024] * 12
    w += [2 * W2C] * 12
    w += [1024] * 12 * 2
    w += [1024] * (8 + 8 + 8)
    return w


def run(work, units=None):
    for _ in islice(work, units):
        pass


def share(fill, units, s, steps):
    run(fill, -(-(s + 1) * units // steps) + (-s * units // steps))


class Counts:

    def __init__(self):
        self.unit = 0
        self.done = 0
        self.acc = 0
        self.rdy = 0
        self.acc_hi = 0
        self.pt = 0
        self.sc = 0
        self.pv = 0
        self.gates = 0
        self.rows = 0
        self.norm = 0
        self.gain = 0
        self.pre = 0
        self.branches = 0
        self.sq1 = 0
        self.post = 0
        self.sums = 0
        self.chain = 0


def build(nc, A):
    f32, f32r, i32 = mybir.dt.float32, mybir.dt.float32r, mybir.dt.int32
    ACT, ALU, AX = mybir.ActivationFunctionType, mybir.AluOpType, mybir.AxisListType.X
    ctx = ExitStack()
    WIDTHS = unit_widths()
    LAYER_UNITS = len(WIDTHS)
    FFN_UNITS = 6 * NSTEP
    LAYER0 = [0, LAYER_UNITS + FFN_UNITS]
    FFN0 = [LAYER_UNITS, 2 * LAYER_UNITS + FFN_UNITS]

    def width_of(u):
        for layer in range(DEPTH):
            if LAYER0[layer] <= u < LAYER0[layer] + LAYER_UNITS:
                return WIDTHS[u - LAYER0[layer]]
        return 1024

    with ctx:
        def sb(name, shape, dt=f32):
            return ctx.enter_context(nc.sbuf_tensor(name, shape, dt))

        def sem(name):
            return ctx.enter_context(nc.semaphore(name))

        raw = sb("raw", [P, RAW_SLOTS, 2048])
        w_hi = sb("w_hi", [P, UNIT_SLOTS, 1024], f32r)
        w_lo = sb("w_lo", [P, UNIT_SLOTS, 1024], f32r)
        x = sb("x", [P, NT, D])
        S1 = sb("S1", [P, NT, D])
        ZU = sb("ZU", [P, NT, 2048])
        hT_hi = sb("hT_hi", [P, 8, SEQ], f32r)
        hT_lo = sb("hT_lo", [P, 8, SEQ], f32r)
        oT_hi = sb("oT_hi", [P, 8, SEQ], f32r)
        oT_lo = sb("oT_lo", [P, 8, SEQ], f32r)
        Z = sb("Z", [P, NT, N2])
        qT = sb("qT", [P, 8, SEQ])
        kT = sb("kT", [P, 8, SEQ])
        Pr = sb("Pr", [P, 2, 512])
        PT = sb("PT", [P, 2, 512])
        E4 = sb("E4", [P, 2, 512])
        hidT_hi = sb("hidT_hi", [P, 2, 256], f32r)
        hidT_lo = sb("hidT_lo", [P, 2, 256], f32r)
        gains = sb("gains", [P, 2, D])
        sg = sb("sg", [P, SG_N])
        rope = sb("rope", [P, NT, R_N])
        ident = sb("ident", [P, P])
        iota = sb("iota", [P, P])
        oh = sb("oh", [P, NT, P], f32r)
        ohT = sb("ohT", [P, 2, SEQ], f32r)
        wr = sb("wr", [P, 8, NE])
        wr_split = sb("wr_split", [P, 8, 2 * NE], f32r)
        brt = sb("brt", [P, NE])
        misc = sb("misc", [P, 4 * N_COLS + 32])
        ssq, ms, rstd, mhalf = (misc[:, N_COLS * n:N_COLS * (n + 1)] for n in range(4))
        m0 = 4 * N_COLS
        nmax, sums, rsum = (misc[:, m0 + 8 * n:m0 + 8 * n + 8].rearrange("p (u h) -> p u h", h=2) for n in range(3))
        lam = misc[:, m0 + 24:m0 + 28]
        nlam = misc[:, m0 + 28:m0 + 29]
        rounds = sb("rounds", [P, 1], i32)
        ps = ctx.enter_context(nc.psum_tensor("ps", [P, 8, 512], f32))

        kv_dram = [nc.dram_tensor(f"kv_spill{L}", (MEM_LEN, 2 * D), f32, kind="Internal").ap() for L in range(DEPTH)]
        T_MEM = [ACC_LAYER * L + 12 for L in range(DEPTH)]

        scratch = kT[:, :, :].rearrange("p a b -> p (a b)")
        rows_hi = hT_hi[:, :, :].rearrange("p (t a) b -> p t (a b)", t=NT)
        rows_lo = hT_lo[:, :, :].rearrange("p (t a) b -> p t (a b)", t=NT)
        y_next = qT[:, :, :].rearrange("p (t a) b -> p t (a b)", t=NT)
        sl = E4[:, 0, :]
        hid = E4[:, 1, :]
        Zf = Z[:, :, :].rearrange("p a b -> p (a b)")
        tri, ones = Zf[:, 0:128], Zf[:, 128:256]

        def small(n):
            v = Zf[:, 256 + 16 * n:272 + 16 * n]
            return v.rearrange("p (t e) -> p t e", t=2)

        LG, CC, OH1, OH2, L2, GATE, MASK, RANKM = (small(n) for n in range(8))
        M1, M2, I1, EX, W1, W2 = (Zf[:, 420 + 2 * n:422 + 2 * n] for n in range(6))
        MX, NR, DOWN = Zf[:, 440:441], Zf[:, 441:442], Zf[:, 442:450]

        s_x = [sem(f"x_landed{t}") for t in range(NT)]
        s_ident = sem("identity_landed")
        s_const = sem("constants_landed")
        s_tri = sem("triangle_landed")
        s_raw = [sem(f"raw_landed{n}") for n in range(RAW_SLOTS)]
        s_hi = sem("unit_hi_ready")
        s_lo = sem("unit_lo_ready")
        s_used = sem("unit_used")
        s_gain = [sem(f"gain_landed{n}") for n in range(2)]
        s_gain_first = sem("first_gain_landed")
        s_norm = sem("gained_tiles_ready")
        s_res = sem("residual_tiles_ready")
        s_sg = sem("small_gains_landed")
        s_mem = sem("mem_landed")
        s_spill = sem("memory_kv_spilled")
        s_kmem = sem("memory_keys_landed")
        s_vmem = sem("memory_values_landed")
        s_gqa = sem("gqa_rows_ready")
        s_pv = sem("attention_out_ready")
        s_pv_free = sem("attention_out_copied")
        s_ssq = sem("squares_summed")
        s_sq1 = sem("second_tile_squares_summed")
        s_y0 = sem("dense_outputs_gained")
        s_pool = sem("pool_chain")
        s_rstd = sem("rstd_ready")
        s_rows = sem("rows_ready")
        s_acc = sem("acc_ready")
        s_acc_hi = sem("acc_hi_copied")
        s_acc_free = sem("acc_free")
        s_gexp = sem("gate_tanh_ready")
        s_pt = sem("pt_ready")
        s_pt_copied = sem("pt_copied")
        s_sc = sem("scores_ready")
        s_max = sem("max_ready")
        s_p = sem("probs_ready")
        s_outT = sem("branch_outputs_lo_ready")
        s_subsq = sem("diff_squares_ready")
        s_lamq = sem("lambda_dots_ready")
        s_lame = sem("lambda_exp_ready")
        s_chain = sem("dve_chain")
        s_wr = sem("router_hi_ready")
        s_wrl = sem("router_lo_ready")
        s_silu = sem("silu_ready")
        s_hid = sem("hidden_ready")
        s_hidT = sem("hiddenT_ready")
        s_hidT_hi = sem("hiddenT_hi_copied")
        s_hidT_lo = sem("hiddenT_lo_ready")
        s_yhi = sem("y_hi_copied")
        s_ylo = sem("y_lo_ready")
        s_hrow_hi = sem("rows_hi_ready")
        s_hrow = sem("rows_lo_ready")
        s_topd = sem("top_gap_ready")
        s_tope = sem("top_exp_ready")
        s_rank = sem("ranks_ready")
        s_rounds = sem("rounds_ready")
        s_oh = sem("onehot_ready")
        s_gath = sem("gather_ready")
        s_ohT = sem("onehotT_copied")
        s_gath_hi = sem("gather_hi_copied")
        s_gath_lo = sem("gather_lo_ready")
        s_scat = sem("scatter_ready")
        s_added = sem("scatter_added")
        s_final = sem("result_ready")
        s_out = sem("out_stored")

        def acc_bank(a):
            return 4 + a % 4

        def hi_slot(us):
            return us % UNIT_SLOTS

        def raw_of(us):
            t = us // 2
            off = width_of(us - 1) if us % 2 else 0
            return raw[:, t % RAW_SLOTS, off:off + width_of(us)]

        def act_split(act, us, it=0):
            w = width_of(us)
            if us % 2 == 0:
                act.wait_ge(s_raw[(us // 2) % RAW_SLOTS], it * 32 + 32 * (us // LOOP_UNITS + 1))
            if us >= UNIT_SLOTS:
                act.wait_ge(s_used, it * LOOP_UNITS + (us - UNIT_SLOTS + 1))
            nc.scalar.activation(w_hi[:, hi_slot(us), 0:w], raw_of(us), ACT.Copy).then_inc(s_hi, 1)

        def dve_split(dve, us, it=0):
            w = width_of(us)
            dve.wait_ge(s_hi, it * LOOP_UNITS + (us + 1))
            nc.vector.tensor_tensor(w_lo[:, hi_slot(us), 0:w], raw_of(us),
                                    w_hi[:, hi_slot(us), 0:w].bitcast(f32), ALU.subtract).then_inc(s_lo, 1)

        blk = ctx.enter_context(nc.Block())

        @blk.sync
        def _(sp):
            for t in range(NT):
                sp.dma_start(x[:, t, :], A["x"][0][P * t:P * t + P, :]).then_inc(s_x[t], 16)
            sp.dma_start(gains[:, 0, :], A["mix_pre_g"][0].partition_broadcast(P)).then_inc(s_gain_first, 16)
            n = [0]

            def chunks(W, k0, nk, c0, nc_):
                return W[k0 * P:(k0 + nk) * P, c0:c0 + nc_].rearrange("(k p) n -> p k n", p=P)

            def put(ts, parts, it=0):
                if ts >= RAW_SLOTS:
                    sp.wait_ge(s_lo, it * LOOP_UNITS + 2 * (ts - RAW_SLOTS) + 2)
                slot = ts % RAW_SLOTS
                for off, nk, w, src in parts:
                    dst = raw[:, slot, off:off + nk * w].rearrange("p (k n) -> p k n", k=nk)
                    sp.dma_start(dst, src).then_inc(s_raw[slot], 16)

            def block(W, k_chunks, c0, w):
                for k0 in range(0, k_chunks, 4):
                    nk = min(4, k_chunks - k0)
                    parts = [(0, 2, w, chunks(W, k0, 2, c0, w)),
                             (2 * w, nk - 2, w, chunks(W, k0 + 2, nk - 2, c0, w))]
                    put(n[0], parts)
                    n[0] += 1

            def gate_up(Wg, Wu, row0, col, tile0, it):
                for h in range(2):
                    if tile0 + h >= RAW_SLOTS:
                        sp.wait_ge(s_lo, it * LOOP_UNITS + 2 * (tile0 + h - RAW_SLOTS) + 2)
                    slot = (tile0 + h) % RAW_SLOTS
                    for g, W in enumerate((Wg, Wu)):
                        dst = raw[:, slot, :].rearrange("p (k g n) -> p k g n", k=4, g=2)[:, :, g, :]
                        src = W[bass.ds(row0 + 512 * h, 512), bass.ds(col, FB)]
                        sp.dma_start(dst, src.rearrange("(k p) n -> p k n", p=P)).then_inc(s_raw[slot], 16)

            def down(Wd, row0, tile0, it):
                sp.wait_ge(s_lo, it * LOOP_UNITS + 2 * (tile0 - RAW_SLOTS) + 2)
                slot = tile0 % RAW_SLOTS
                for h in range(2):
                    sp.dma_start(raw[:, slot, 1024 * h:1024 * h + 1024],
                                 Wd[bass.ds(row0 + P * h, P), :]).then_inc(s_raw[slot], 16)

            def ffn(Wg, Wu, Wd, row_in, row_h, tile0, it0):
                gate_up(Wg, Wu, row_in, 0, tile0, it0)
                with sp.Fori(0, (NSTEP - 1) // 2) as i:
                    it = it0 + i
                    for j in range(2):
                        gate_up(Wg, Wu, row_in, i * (2 * FB) + FB * (j + 1), tile0 + 2 + 3 * j, it)
                        down(Wd, row_h + i * (2 * FB) + FB * j, tile0 + 4 + 3 * j, it)
                down(Wd, row_h + FB * (NSTEP - 1), tile0 + 3 * NSTEP - 1, it0)

            for L in range(DEPTH):
                w_in = A["w_in"][L]
                for b in range(3):
                    block(w_in, 8, W1C * b, W1C)
                for b in range(2):
                    block(A["mla_w_q_up"][L], 3, Q_LORA * b, Q_LORA)
                put(n[0], [(1024 * k, 1, 1024, chunks(A["mla_w_kv_up"][L], k, 1, 0, 1024)) for k in range(2)])
                n[0] += 1

                def gated(br):
                    for half in range(2):
                        block(w_in, 8, GATE0 + D * br + 512 * half, 512)
                        block(A["w_branch"][L, br], 4, 512 * half, 512)

                for b in range(4):
                    block(A["mem_wkv"][L], 8, 512 * b, 512)
                gated(0)
                for b in range(3):
                    block(w_in, 8, N1 + W2C * b, W2C)
                gated(1)
                gated(2)
                for name, cols in (("w_out", D), ("mem_wq", D), ("mem_wo", D)):
                    for b in range(cols // 512):
                        block(A[name][L], 8, 512 * b, 512)
                if L == 0:
                    ffn(A["dense_w_gate"][0], A["dense_w_up"][0], A["dense_w_down"][0], 0, 0, n[0], 0)
                    n[0] += 3 * NSTEP
            Wg = A["moe_w_gate"][0].rearrange("e k n -> (e k) n")
            Wu = A["moe_w_up"][0].rearrange("e k n -> (e k) n")
            Wd = A["moe_w_down"][0].rearrange("e f n -> (e f) n")

            def experts(r):
                with sp.Fori(0, NE // 2) as pr:
                    it = sp.snap(pr * 11 + 11 * (NE // 2) * r)
                    for e in range(2):
                        ffn(Wg, Wu, Wd, pr * (2 * D) + D * e, pr * (2 * F) + F * e, n[0] + 3 * NSTEP * e, it)

            experts(0)
            sp.wait_ge(s_rounds, 1)
            nr = sp.value_load(rounds[0:1, 0:1], min_val=1, max_val=2)
            with sp.If(nr > 1):
                experts(1)
            for t in range(NT):
                sp.wait_ge(s_final, t + 1)
                sp.dma_start(A["out"][0][P * t:P * t + P, :], x[:, t, :]).then_inc(s_out, 16)
            sp.wait_ge(s_out, 16 * NT)

        @blk.gpsimd
        def _(pool):
            GAINS = ["mix_pre_g", "mem_norm_g", "mix_post_g", "mem_pre_g", "mem_post_g", "ffn_pre_g", "ffn_post_g"]
            order = [(g, L) for L in range(DEPTH) for g in GAINS]
            chain, requests, used = [0], [0], [0]

            def load_gain(k):
                g, L = order[k]
                nc.gpsimd.dma_start(gains[:, k % 2, :], A[g][L].partition_broadcast(P)).then_inc(s_gain[k % 2], 16)

            def load_small(L):
                for name, c in (("mla_q_norm_g", SG_Q), ("mla_kv_norm_g", SG_KV), ("gqa_q_norm_g", SG_GQ),
                                ("gqa_k_norm_g", SG_GK), ("diff_subln_g", SG_SUB), ("diff_lambda_q1", SG_LAM),
                                ("diff_lambda_k1", SG_LAM + 32), ("diff_lambda_q2", SG_LAM + 64),
                                ("diff_lambda_k2", SG_LAM + 96)):
                    w = A[name].shape[1]
                    nc.gpsimd.dma_start(sg[:, c:c + w], A[name][L].partition_broadcast(P)).then_inc(s_sg, 16)

            def step(ins):
                chain[0] += 1
                ins.then_inc(s_pool, 1)
                pool.wait_ge(s_pool, chain[0])

            def rsqrt(*parts, scale=1.0, halves=False):
                requests[0] += 1
                pool.wait_ge(s_ssq, requests[0])
                if halves:
                    c0, c1, _ = parts[0]
                    step(nc.gpsimd.tensor_tensor(ssq[:, c0:c1], ssq[:, c0:c1], ssq[:, c1:2 * c1 - c0], ALU.add))
                f = 1.0 / (scale * scale)
                for c0, c1, n in parts:
                    step(nc.gpsimd.tensor_scalar(ms[:, c0:c1], ssq[:, c0:c1], f / n, f * EPS, ALU.mult, ALU.add))
                c0, c1 = parts[0][0], parts[-1][1]
                nc.gpsimd.tensor_tensor(rstd[:, c0:c1], ms[:, c0:c1], mhalf[:, c0:c1], ALU.pow).then_inc(s_rstd, 1)

            def norm(c0, scale=1.0, halves=False):
                rsqrt((c0, c0 + NT, D), scale=scale, halves=halves)
                post = "post" in order[used[0]][0]
                used[0] += 1
                if used[0] + 1 < len(order):
                    same = [g for g, _ in order[:used[0]] if ("post" in g) == post]
                    pool.wait_ge(s_res if post else s_norm, NT * len(same))
                    load_gain(used[0] + 1)

            def mem_rows():
                nc.gpsimd.dma_start(S1[:, :, :], A["mem"][0].rearrange("(t p) d -> p t d", p=P)).then_inc(s_mem, 16)

            kv_rows = [kv_dram[L].rearrange("(t p) n -> p t n", p=P) for L in range(DEPTH)]

            def spill(L, b):
                pool.wait_ge(s_acc_free, LAYER_BANKS * L + KV_BANK + 2 * (b + 1))
                nc.gpsimd.dma_start(kv_rows[L][:, :, 512 * b:512 * b + 512], E4[:, :, :]).then_inc(s_spill, 16)

            def gqa_rows(L):
                QKH, H2 = GQA_QH + GQA_KVH, HD // 2
                W = QKH * HD
                S = S1[:, :, :].rearrange("p t d -> p (t d)")
                sq, hs = S[:, 0:W], S[:, 2 * W:2 * W + 3 * QKH]
                G = nc.gpsimd
                spill(L, 0)
                for t in range(NT):
                    v = Z[:, t, C_GQA:C_GQA + W]
                    heads = v.rearrange("p (h d) -> p h d", d=HD)
                    step(G.tensor_tensor(sq, v, v, ALU.mult))
                    w = HD // 2
                    sh = sq.rearrange("p (h d) -> p h d", d=HD)
                    while w >= 1:
                        step(G.tensor_tensor(sh[:, :, 0:w], sh[:, :, 0:w], sh[:, :, w:2 * w], ALU.add))
                        w //= 2
                    step(G.tensor_scalar(hs[:, 0:QKH].unsqueeze(2), sh[:, :, 0:1], 1.0 / HD, EPS, ALU.mult, ALU.add))
                    step(G.tensor_tensor(hs[:, QKH:2 * QKH], hs[:, 0:QKH], mhalf[:, 0:QKH], ALU.pow))
                    step(G.tensor_tensor(heads, heads, hs[:, QKH:2 * QKH].unsqueeze(2).broadcast_to([P, QKH, HD]), ALU.mult))
                    step(G.tensor_tensor(heads[:, 0:GQA_QH, :], heads[:, 0:GQA_QH, :],
                                         sg[:, SG_GQ:SG_GQ + HD].unsqueeze(1).broadcast_to([P, GQA_QH, HD]), ALU.mult))
                    step(G.tensor_tensor(heads[:, GQA_QH:, :], heads[:, GQA_QH:, :],
                                         sg[:, SG_GK:SG_GK + HD].unsqueeze(1).broadcast_to([P, GQA_KVH, HD]), ALU.mult))
                    spill(L, 1 + t)
                    v4 = v.rearrange("p (h a d) -> p h a d", a=2, d=H2)
                    a = S[:, 0:W].rearrange("p (h a d) -> p h a d", a=2, d=H2)
                    b = S[:, W:2 * W].rearrange("p (h a d) -> p h a d", a=2, d=H2)
                    co = rope[:, t, RC_A:RC_A + H2].unsqueeze(1).broadcast_to([P, QKH, H2])
                    si = rope[:, t, RS_A:RS_A + H2].unsqueeze(1).broadcast_to([P, QKH, H2])
                    for h in range(2):
                        step(G.tensor_tensor(a[:, :, h, :], v4[:, :, h, :], co, ALU.mult))
                        step(G.tensor_tensor(b[:, :, h, :], v4[:, :, h, :], si, ALU.mult))
                    for h, op in ((0, ALU.subtract), (1, ALU.add)):
                        by_pair = [w[:, 0:GQA_QH, m, :].rearrange("p (g h) d -> p h g d", g=GQA_KVH)
                                   for w, m in ((a, h), (b, 1 - h))]
                        step(G.tensor_tensor(v4[:, 0:GQA_QH, h, :].rearrange("p (h g) d -> p h g d", g=GQA_KVH),
                                             by_pair[0], by_pair[1], op))
                        ins = G.tensor_tensor(v4[:, GQA_QH:, h, :], a[:, GQA_QH:, h, :], b[:, GQA_QH:, 1 - h, :], op)
                        if h == 0:
                            step(ins)
                    if t == 0:
                        step(ins)
                    else:
                        ins.then_inc(s_gqa, 1)
                spill(L, 3)

            def sub_rows(L):
                pool.wait_ge(s_pv_free, LAYER_PV * L + LAYER_PV - MEM_H)
                for t in range(NT):
                    ins = nc.gpsimd.tensor_tensor(scratch[:, BW * t:BW * t + BW], ZU[:, t, 0:BW], ZU[:, t, 0:BW], ALU.mult)
                ins.then_inc(s_subsq, 1)
                pool.wait_ge(s_subsq, 2 * L + 1)
                for t in range(NT):
                    v = ZU[:, t, 0:BW].rearrange("p (h d) -> p h d", d=DV)
                    ins = nc.gpsimd.tensor_tensor(v, v, sg[:, SG_SUB:SG_SUB + DV].unsqueeze(1).broadcast_to([P, DIFF_H, DV]),
                                                  ALU.mult)
                ins.then_inc(s_subsq, 1)

            step(nc.gpsimd.memset(mhalf[:, :], -0.5))
            load_gain(1)
            load_small(0)
            mem_rows()
            pool.wait_ge(s_const, 64)
            for L in range(DEPTH):
                norm(N_MIX, 0.5)
                norm(N_MEM)
                rsqrt((N_LAT, N_LAT + 2, Q_LORA), (N_LAT + 2, N_LAT + 4, KV_LORA))
                pool.wait_ge(s_acc, T_MEM[L])
                gqa_rows(L)
                pool.wait_ge(s_rows, 5 * L + 4)
                pool.wait_ge(s_spill, 64 * (L + 1))
                nc.gpsimd.dma_start(ZU[:, :, 1024:2048], kv_rows[L][:, :, 0:D]).then_inc(s_kmem, 16)
                sub_rows(L)
                rsqrt((N_DIFF, N_DIFF + 16, DV), scale=1.0 - LAMBDA_INIT[L])
                pool.wait_ge(s_rows, 5 * L + 5)
                nc.gpsimd.dma_start(Z[:, :, 0:D], kv_rows[L][:, :, D:2 * D]).then_inc(s_vmem, 16)
                if L + 1 < DEPTH:
                    load_small(L + 1)
                for c0 in (N_POST, N_PRE, N_POST2, N_FFN):
                    norm(c0, halves=c0 in (N_POST, N_POST2))
                if L + 1 == DEPTH:
                    nc.gpsimd.dma_start(tri, A["consts"][2]).then_inc(s_tri, 16)
                    nc.gpsimd.dma_start(ones, A["consts"][3]).then_inc(s_tri, 16)
                    nc.gpsimd.memset(S1[:, :, :], 0.0).then_inc(s_added, 1)
                norm(N_POST)
                if L + 1 < DEPTH:
                    mem_rows()

        @blk.scalar
        def _(act):
            act.dma_start(ident[:, :], A["consts"][0]).then_inc(s_ident, 16)
            act.dma_start(rope[:, :, :], A["rope"].rearrange("(t p) c -> p t c", p=P)).then_inc(s_const, 16)
            act.dma_start(iota[:, :], A["consts"][1]).then_inc(s_const, 16)
            act.dma_start(wr[:, :, :], A["moe_w_router"][0].rearrange("(k p) e -> p k e", p=P)).then_inc(s_const, 16)
            act.dma_start(brt[:, :], A["moe_b_router"][0].partition_broadcast(P)).then_inc(s_const, 16)
            c = Counts()

            def advance(limit):
                while c.unit < limit:
                    act_split(act, c.unit)
                    c.unit += 1

            def acc_hi(dst):
                c.rdy += 1
                act.wait_ge(s_acc, c.rdy)
                nc.scalar.activation(dst, bank(c.acc, dst), ACT.Copy).then_inc(s_acc_hi, 1)
                c.acc += 1

            def bank(a, dst):
                w = 1
                for n in dst.shape[1:]:
                    w *= n
                v = ps[:, acc_bank(a), 0:w]
                return v.rearrange("p (k t) -> p k t", k=dst.shape[1]) if len(dst.shape) == 3 else v

            def pt_copy(dst, scale=1.0, bank=None):
                act.wait_ge(s_pt, c.pt + 1)
                rows = dst.shape[0]
                if bank is None:
                    bank = 2 + c.pt % 2
                src = ps[0:rows, bank, 0:SEQ * dst.shape[1]].rearrange("p (h t) -> p h t", t=SEQ) if len(dst.shape) == 3 \
                    else ps[0:rows, bank, 0:dst.shape[1]]
                nc.scalar.activation(dst, src, ACT.Copy, scale=scale).then_inc(s_pt_copied, 1)
                c.pt += 1

            def attention(n, fill=(), units=0):
                pt_of, first = {}, c.sc
                for s in range(n + 2):
                    if s < n:
                        u = c.sc
                        act.wait_ge(s_max, u + 1)
                        if s >= 2:
                            act.wait_ge(s_pt, pt_of[s - 2] + 1)
                        for hh in range(2):
                            ins = nc.scalar.activation(Pr[:, u % 2, 256 * hh:256 * hh + 256],
                                                       ps[:, u % 2, 256 * hh:256 * hh + 256], ACT.Exp,
                                                       bias=nmax[:, u % 4, hh:hh + 1],
                                                       accum_out=sums[:, u % 4, hh:hh + 1])
                        ins.then_inc(s_p, 1)
                        c.sc += 1
                    if 1 <= s <= n:
                        pt_of[s - 1] = c.pt
                        v = (first + s - 1) % 2
                        pt_copy(PT[:, v, :], bank=2)
                    share(fill, units, s, n + 2)

            def squares(parts, ready, between=None):
                if c.sums:
                    act.wait_ge(s_ssq, c.sums)
                at = 0
                junk = (Pr, PT)
                for i, (src, col) in enumerate(parts):
                    ready(i)
                    w = 1
                    for n in src.shape[1:]:
                        w *= n
                    dst = junk[at // 1024][:, :, :].rearrange("p a b -> p (a b)")[:, at % 1024:at % 1024 + w]
                    at += w
                    if len(src.shape) == 3:
                        dst = dst.rearrange("p (a b) -> p a b", a=src.shape[1])
                    ins = nc.scalar.activation(dst, src, ACT.Square, accum_out=ssq[:, col:col + 1])
                    if between is not None and i == 0:
                        ins.then_inc(s_sq1, 1)
                        act.wait_ge(*between)
                ins.then_inc(s_ssq, 1)
                c.sums += 1

            def x_squares(col, updated=True):
                squares([(x[:, t, :], col + t) for t in range(NT)],
                        lambda t: act.wait_ge(s_res, NT * c.post - NT + t + 1) if updated else act.wait_ge(s_x[t], 16))

            def projected(col, split):
                assert c.acc % 4 == 0
                for half in range(2):
                    c.done += 4
                    advance(c.done + (4 if half == 0 else 0))
                    act.wait_ge(s_used, c.done)
                    for t in (1, 0):
                        if t == 0:
                            act.wait_ge(s_acc_free, c.acc + 1)
                        k = 2 * half + t
                        ins = nc.scalar.activation((Pr, PT)[half][:, t, :], ps[:, 4 + k, :], ACT.Square,
                                                   accum_out=ssq[:, col + k:col + k + 1])
                        if t == 1:
                            ins.then_inc(s_sq1, 1)
                    c.acc += 2
                ins.then_inc(s_ssq, 1)
                c.sums += 1
                c.post += 1
                advance(c.done + split)

            def transposed(hi, k0, widths):
                for w in widths:
                    acc_hi(hi[:, k0:k0 + w, :])
                    k0 += w

            def transposed_by_tile(hi):
                for t in range(NT):
                    for k0 in (0, 4):
                        acc_hi(hi[:, k0:k0 + 4, P * t:P * t + P])

            def branch_outputs():
                for k in (0, 2):
                    pt_copy(oT_hi[:, k:k + 2, :])

            def linear(blocks, units, accs=2):
                for b in range(blocks):
                    for n in range(units):
                        c.done += 1
                        advance(c.done + 4)
                        yield
                    c.acc += accs

            def gated():
                for half in range(2):
                    for n in range(6):
                        c.done += 1
                        advance(c.done + 4)
                        if n == 3:
                            act.wait_ge(s_used, c.done)
                            act.wait_ge(s_acc_free, c.acc)
                            for t in range(NT):
                                ins = nc.scalar.activation(E4[:, t, :], ps[:, acc_bank(c.acc + t), :], ACT.Tanh,
                                                           scale=rstd[:, N_MIX + t:N_MIX + t + 1])
                            ins.then_inc(s_gexp, 1)
                        yield
                    c.acc += 4

            def ffn(step0, u0, it0, nt, start=True, steps=True, before=None):
                def silu(j, k, it, last):
                    act.wait_ge(s_used, it * LOOP_UNITS + last)
                    if not (step0 + j == 0):
                        act.wait_ge(s_hid, it * 2 + (step0 + j))
                    if nt == 1:
                        ins = nc.scalar.activation(sl[:, 0:FB], ps[:, 4 + k, 0:FB], ACT.Silu)
                    else:
                        for t in range(NT):
                            ins = nc.scalar.activation(sl[:, FB * t:FB * t + FB], ps[:, 4 + t, 0:FB], ACT.Silu,
                                                       scale=rstd[:, N_FFN + t:N_FFN + t + 1])
                    ins.then_inc(s_silu, 1)

                def hidT(j, par, it):
                    act.wait_ge(s_hidT, it * 2 + (step0 + j + 1))
                    nc.scalar.activation(hidT_hi[:, :, 0:P * nt],
                                         ps[:, 6 + par, 0:2 * P * nt].rearrange("p (k t) -> p k t", k=2),
                                         ACT.Copy).then_inc(s_hidT_hi, 1)

                if start:
                    for k in (2, 3):
                        act_split(act, u0 + k, it0)
                    if before is not None:
                        before()
                    for k in (4, 5):
                        act_split(act, u0 + k, it0)
                    silu(0, 0, it0, u0 + 4)
                if not steps:
                    return
                with act.Fori(0, (NSTEP - 1) // 2) as i:
                    it = it0 + i
                    for j in range(2):
                        u = u0 + 4 + 6 * j
                        for k in (2, 3):
                            act_split(act, u + k, it)
                        hidT(j, j, it)
                        for k in (4, 5):
                            act_split(act, u + k, it)
                        silu(j + 1, (j + 1) % 2, it, u + 4)
                        for k in (6, 7):
                            act_split(act, u + k, it)

            def ffn_tail(step0, it0, nt):
                act.wait_ge(s_hidT, it0 * 2 + (step0 + NSTEP))
                nc.scalar.activation(hidT_hi[:, :, 0:P * nt],
                                     ps[:, 6, 0:2 * P * nt].rearrange("p (k t) -> p k t", k=2),
                                     ACT.Copy).then_inc(s_hidT_hi, 1)

            for L in range(DEPTH):
                if L == 0:
                    x_squares(N_MIX, False)
                transposed_by_tile(hT_hi)
                if L > 0:
                    advance(c.done + 4)
                    x_squares(N_MIX)
                if L == 0:
                    advance(4)
                if L == 0:
                    act.wait_ge(s_const, 64)
                    nc.scalar.activation(wr_split[:, :, 0:NE], wr[:, :, :], ACT.Copy).then_inc(s_wr, 1)
                w_in = linear(3, 4)
                run(w_in, 2)
                act.wait_ge(s_mem, 16 * (L + 1))
                squares([(S1[:, t, :], N_MEM + t) for t in range(NT)], lambda t: None)
                run(w_in, 2)
                act.wait_ge(s_lamq, L + 1)
                nc.scalar.activation(lam[:, 2:4], lam[:, 0:2], ACT.Exp).then_inc(s_lame, 1)
                run(w_in, 5)
                act.wait_ge(s_acc_free, c.acc)
                squares([(Z[:, t, 0:Q_LORA], N_LAT + t) for t in range(NT)] +
                        [(Z[:, t, Q_LORA:C_ROPE], N_LAT + 2 + t) for t in range(NT)], lambda i: None)
                run(w_in)
                transposed(oT_hi, 0, (1, 1, 1, 2))
                run(linear(2, 2))
                run(linear(1, 2, 4))
                transposed(oT_hi, 0, (2, 2, 2, 2))
                others = linear(4, 4)
                run(others, 4)
                for h in range(0, MLA_H, 2):
                    pt_copy(qT[0:QK_MLA, h:h + 2, :], QK_MLA ** -0.5)
                for h in range(0, MLA_H, 2):
                    pt_copy(kT[0:QK_MLA, h:h + 2, :])
                attention(8, others, 12)
                run(others)
                for h in range(0, 4, 2):
                    pt_copy(qT[:, h:h + 2, :], HD ** -0.5)
                pt_copy(kT[:, 0:1, :])
                branch_outputs()
                others = gated()
                attention(8, others, 12)
                run(others)
                w_in = linear(3, 4)
                run(w_in, 4)
                branch_outputs()
                run(w_in)
                for h in range(0, 4, 2):
                    pt_copy(qT[:, h:h + 2, :], DQK ** -0.5)
                for h in range(0, 4, 2):
                    pt_copy(kT[:, h:h + 2, :])
                others = gated()
                attention(16, others, 12)
                run(others)
                gates = gated()
                run(gates, 4)
                c.sums += 1
                branch_outputs()
                run(gates)
                transposed_by_tile(hT_hi)
                projected(N_POST, 1)
                for h in range(0, 8, 2):
                    pt_copy(kT[:, h:h + 2, :])
                transposed_by_tile(hT_hi)
                advance(c.done + 4)
                x_squares(N_PRE)
                run(linear(2, 4))
                for h in range(0, 8, 2):
                    pt_copy(qT[:, h:h + 2, :], MEM_HD ** -0.5)
                attention(4)
                transposed(hT_hi, 0, (2, 2, 2, 2))
                projected(N_POST2, 1 if L == 0 else 0)
                transposed_by_tile(hT_hi if L == 0 else oT_hi)
                if L == 0:
                    advance(c.done + 2)
                    x_squares(N_FFN)
                    ffn(0, FFN0[0], 0, NT, before=lambda: act.wait_ge(s_rstd, c.sums))
                    ffn_tail(0, 0, NT)
                    c.unit = c.done = LAYER0[1]
                    act.wait_ge(s_used, c.done)
                    squares([(ps[:, 2 * t:2 * t + 2, :], N_POST + t) for t in (1, 0)], lambda t: None, (s_y0, 1))
                    c.post += 1
                    advance(c.done + 1)
                else:
                    x_squares(N_FFN)
            act.wait_ge(s_rstd, c.sums)
            for t in range(NT):
                ins = nc.scalar.activation(rows_hi[:, t, :], ZU[:, t, 0:D], ACT.Copy, scale=rstd[:, N_FFN + t:N_FFN + t + 1])
            ins.then_inc(s_hrow_hi, 1)
            act.wait_ge(s_topd, 1)
            nc.scalar.activation(EX, W1, ACT.Exp).then_inc(s_tope, 1)
            act.wait_ge(s_rounds, 1)
            nr = act.value_load(rounds[0:1, 0:1], min_val=1, max_val=2)

            def gather_hi(e, q):
                act.wait_ge(s_gath, q * 2 + (e + 1))
                nc.scalar.activation(ohT[:, e, :], ps[:, 7, 0:SEQ], ACT.Copy).then_inc(s_ohT, 1)
                nc.scalar.activation(oT_hi[:, :, 0:P],
                                     ps[:, 2 * e:2 * e + 2, :].rearrange("p b (k s) -> p (b k) s", k=4),
                                     ACT.Copy).then_inc(s_gath_hi, 1)

            def y_hi(e, q):
                act.wait_ge(s_used, q * (11 * LOOP_UNITS) + (FFN0[1] + FFN_UNITS * (e + 1)))
                nc.scalar.activation(oT_hi[:, :, P:2 * P],
                                     ps[:, 2 * e:2 * e + 2, :].rearrange("p b (k s) -> p (b k) s", k=4),
                                     ACT.Copy).then_inc(s_yhi, 1)

            def start(e, q, it, before=None):
                u = FFN0[1] + FFN_UNITS * e
                for k in (0, 1):
                    act_split(act, u + k, it)
                gather_hi(e, q)
                ffn(NSTEP * (e + 1), u, it, 1, steps=False, before=before)

            def pair(q, last):
                it = act.snap(q * 11)
                ffn(NSTEP, FFN0[1], it, 1, start=False)
                ffn_tail(NSTEP, it, 1)
                start(1, q, it, lambda: y_hi(0, q))
                ffn(2 * NSTEP, FFN0[1] + FFN_UNITS, it, 1, start=False)
                ffn_tail(2 * NSTEP, it, 1)
                if last:
                    y_hi(1, q)
                else:
                    start(0, act.snap(q + 1), act.snap(it + 11), lambda: y_hi(1, q))

            with act.Fori(0, nr) as r:
                q0 = act.snap(r * (NE // 2))
                start(0, q0, act.snap(q0 * 11))
                with act.Fori(0, NE // 2 - 1) as pr:
                    pair(act.snap(q0 + pr), False)
                pair(act.snap(q0 + (NE // 2 - 1)), True)
            act.wait_ge(s_added, nr * (4 * NE) + 1)
            squares([(S1[:, t, :], N_POST + t) for t in range(NT)], lambda t: None)

        @blk.vector
        def _(dve):
            V = nc.vector
            c = Counts()

            def link(ins):
                c.chain += 1
                ins.then_inc(s_chain, 1)
                dve.wait_ge(s_chain, c.chain)

            def advance(limit):
                while c.unit < limit:
                    dve_split(dve, c.unit)
                    c.unit += 1

            def rows_done(ins):
                c.rows += 1
                ins.then_inc(s_rows, 1)

            def transposed(lo, hi, k0, widths):
                for w in widths:
                    dve.wait_ge(s_acc_hi, c.acc_hi + 1)
                    src = ps[:, acc_bank(c.acc), 0:w * SEQ].rearrange("p (k t) -> p k t", k=w)
                    V.tensor_tensor(lo[:, k0:k0 + w, :], src, hi[:, k0:k0 + w, :].bitcast(f32),
                                    ALU.subtract).then_inc(s_acc_free, 1)
                    c.acc += 1
                    c.rdy += 1
                    c.acc_hi += 1
                    k0 += w

            def transposed_by_tile(lo=hT_lo, hi=hT_hi):
                for t in range(NT):
                    for k0 in (0, 4):
                        dve.wait_ge(s_acc_hi, c.acc_hi + 1)
                        src = ps[:, acc_bank(c.acc), :].rearrange("p (k t) -> p k t", k=4)
                        part = (slice(None), slice(k0, k0 + 4), slice(P * t, P * t + P))
                        V.tensor_tensor(lo[part], src, hi[part].bitcast(f32), ALU.subtract).then_inc(s_acc_free, 1)
                        c.acc += 1
                        c.rdy += 1
                        c.acc_hi += 1

            def linear(blocks, units, dst, w, col, factor=1.0, free=None):
                for b in range(blocks):
                    for n in range(units):
                        c.done += 1
                        if n == units - 1:
                            dve.wait_ge(s_rstd, c.norm)
                            dve.wait_ge(s_used, c.done)
                            if free is not None:
                                free(b)
                            for t in range(NT):
                                to = dst(b, t)
                                for d, src in to if isinstance(to, list) else [(to, ps[:, acc_bank(c.acc), 0:w])]:
                                    ins = V.tensor_scalar(d, src, rstd[:, col + t:col + t + 1], factor, ALU.mult, ALU.mult)
                                ins.then_inc(s_acc_free, 1)
                                c.acc += 1
                        if (b, n) != (blocks - 1, units - 1):
                            advance(c.done + 4)
                        yield

            def own_rows():
                if c.acc:
                    dve.wait_ge(s_acc_free, c.acc)
                if c.pv:
                    dve.wait_ge(s_pv_free, c.pv)

            def wait_gain():
                k = c.gain
                if k == 0:
                    dve.wait_ge(s_gain_first, 16)
                else:
                    dve.wait_ge(s_gain[k % 2], 16 * ((k + 1) // 2))
                c.gain += 1
                return k % 2

            def pre_gain(src, dst, landed=False):
                g = wait_gain()
                for t in range(NT):
                    if landed:
                        dve.wait_ge(s_x[t], 16)
                    V.tensor_tensor(dst[:, t, 0:D], src[:, t, :], gains[:, g, :], ALU.mult).then_inc(s_norm, 1)
                c.pre += 1
                c.norm += 1

            def residual_gained():
                g = wait_gain()
                if c.post:
                    dve.wait_ge(s_res, NT * c.post)
                for t in range(NT):
                    ins = V.tensor_tensor(ZU[:, t, 0:D], x[:, t, :], gains[:, g, :], ALU.mult)
                link(ins)
                return g

            def projected():
                assert c.acc % 4 == 0
                g = wait_gain()
                g2 = residual_gained()
                for half in range(2):
                    c.done += 4
                    advance(c.done + (4 if half == 0 else 0))
                    dve.wait_ge(s_used, c.done)
                    cols = slice(512 * half, 512 * half + 512)
                    for t in range(NT):
                        if t == 1:
                            c.sq1 += 1
                            dve.wait_ge(s_sq1, c.sq1)
                        V.tensor_tensor(S1[:, t, cols], ps[:, 4 + 2 * half + t, :], gains[:, g, cols],
                                        ALU.mult).then_inc(s_acc_free, 1)
                        c.acc += 1
                    own_rows()
                    ins = V.tensor_tensor(y_next[:, :, cols], S1[:, :, cols],
                                          gains[:, g2, cols].unsqueeze(1).broadcast_to([P, NT, 512]), ALU.mult)
                link(ins)

            def dense_outputs():
                g = wait_gain()
                g2 = residual_gained()
                dve.wait_ge(s_used, FFN0[0] + FFN_UNITS)
                for t in range(NT):
                    if t == 1:
                        c.sq1 += 1
                        dve.wait_ge(s_sq1, c.sq1)
                    ins = V.tensor_tensor(S1[:, t, :], ps[:, 2 * t:2 * t + 2, :].rearrange("p b n -> p (b n)"),
                                          gains[:, g, :], ALU.mult)
                    if t == 0:
                        ins.then_inc(s_y0, 1)
                        dve.wait_ge(s_y0, 1)
                    else:
                        link(ins)
                for t in range(NT):
                    ins = V.tensor_tensor(y_next[:, t, :], S1[:, t, :], gains[:, g2, :], ALU.mult)
                link(ins)

            def next_rows(col, split):
                advance(c.done + split)
                c.norm += 1
                dve.wait_ge(s_rstd, c.norm)
                for t in range(NT):
                    V.scalar_tensor_tensor(ZU[:, t, 0:D], y_next[:, t, :], rstd[:, col + t:col + t + 1], ZU[:, t, 0:D],
                                           ALU.mult, ALU.add).then_inc(s_norm, 1)
                c.norm += 1

            def residual(rows, col, done):
                for t in range(NT):
                    V.scalar_tensor_tensor(x[:, t, :], rows[:, t, :], rstd[:, col + t:col + t + 1], x[:, t, :],
                                           ALU.mult, ALU.add).then_inc(done, 1)
                c.post += 1

            def rotate(view, dst, cos0, sin0, heads, half, tiles=range(NT)):
                n = heads * 2 * half
                own_rows()
                for t in tiles:
                    v = view(t)
                    a = scratch[:, 0:n].rearrange("p (h a d) -> p h a d", h=heads, a=2)
                    b = scratch[:, n:2 * n].rearrange("p (h a d) -> p h a d", h=heads, a=2)
                    co = rope[:, t, cos0:cos0 + half].unsqueeze(1).unsqueeze(1).broadcast_to([P, heads, 2, half])
                    si = rope[:, t, sin0:sin0 + half].unsqueeze(1).unsqueeze(1).broadcast_to([P, heads, 2, half])
                    V.tensor_tensor(a, v, co, ALU.mult)
                    link(V.tensor_tensor(b, v, si, ALU.mult))
                    d = dst(t)
                    V.tensor_tensor(d[0], a[:, :, 0, :], b[:, :, 1, :], ALU.subtract)
                    ins = V.tensor_tensor(d[1], a[:, :, 1, :], b[:, :, 0, :], ALU.add)
                    if t != tiles[-1]:
                        link(ins)
                return ins

            def branch_outputs():
                for k in (0, 2):
                    c.pt += 1
                    dve.wait_ge(s_pt_copied, c.pt)
                    src = ps[:, 2 + (c.pt - 1) % 2, :].rearrange("p (k t) -> p k t", k=2)
                    V.tensor_tensor(oT_lo[:, k:k + 2, :], src, oT_hi[:, k:k + 2, :].bitcast(f32),
                                    ALU.subtract).then_inc(s_outT, 1)

            def attention(n, out, hd, diff=False, fill=(), units=0):
                u0 = c.sc
                for s in range(n + 2):
                    if s < n:
                        u = u0 + s
                        dve.wait_ge(s_sc, u + 1)
                        V.tensor_reduce(nmax[:, u % 4, :], ps[:, u % 2, :].rearrange("p (h k) -> p h k", h=2), AX,
                                        ALU.max, negate=True).then_inc(s_max, 1)
                    if 1 <= s <= n:
                        u = u0 + s - 1
                        dve.wait_ge(s_p, u + 1)
                        link(V.reciprocal(rsum[:, u % 4, :], sums[:, u % 4, :]))
                        if diff:
                            link(V.tensor_tensor(rsum[:, u % 4, 1:2], rsum[:, u % 4, 1:2], nlam[:, :], ALU.mult))
                    if s >= 2:
                        u = u0 + s - 2
                        c.pv += 1
                        dve.wait_ge(s_pv, c.pv)
                        dst = out(s - 2)
                        if diff:
                            link(V.tensor_scalar(dst, ps[:, 3, hd:2 * hd], rsum[:, u % 4, 1:2], None, ALU.mult))
                            V.scalar_tensor_tensor(dst, ps[:, 3, 0:hd], rsum[:, u % 4, 0:1], dst, ALU.mult,
                                                   ALU.add).then_inc(s_pv_free, 1)
                        else:
                            V.tensor_tensor(dst, ps[:, 3, 0:2 * hd].rearrange("p (h d) -> p h d", h=2),
                                            rsum[:, u % 4, :].unsqueeze(2).broadcast_to([P, 2, hd]),
                                            ALU.mult).then_inc(s_pv_free, 1)
                    share(fill, units, s, n + 2)
                c.sc += n
                c.pt += n

            def gated(br):
                for half in range(2):
                    for n in range(6):
                        c.done += 1
                        if n == 5:
                            c.gates += 1
                            dve.wait_ge(s_gexp, c.gates)
                            dve.wait_ge(s_used, c.done)
                            bank = c.acc
                            for t in range(NT):
                                m, g = S1[:, t, 512 * half:512 * half + 512], E4[:, t, :]
                                link(V.scalar_tensor_tensor(g, g, 1.0, ps[:, acc_bank(bank + 2 + t), :], ALU.add, ALU.mult))
                                if br == 0:
                                    V.tensor_scalar(m, g, 0.5, None, ALU.mult).then_inc(s_acc_free, 2)
                                else:
                                    V.scalar_tensor_tensor(m, g, 0.5, m, ALU.mult, ALU.add).then_inc(s_acc_free, 2)
                            c.acc += 4
                        if (half, n) != (1, 5):
                            advance(c.done + 4)
                        yield

            def ffn(step0, u0, it0, nt, start=True, steps=True, before=None, between=None):
                def hidden(j, k, it):
                    dve.wait_ge(s_silu, it * 2 + (step0 + j + 1))
                    if not (step0 + j == 0):
                        dve.wait_ge(s_hidT, it * 2 + (step0 + j))
                    if nt == 1:
                        ins = V.tensor_tensor(hid[:, 0:FB], sl[:, 0:FB], ps[:, 4 + k, FB:2 * FB], ALU.mult)
                    else:
                        for t in range(NT):
                            a = slice(FB * t, FB * t + FB)
                            ins = V.scalar_tensor_tensor(hid[:, a], ps[:, 4 + t, FB:2 * FB],
                                                         rstd[:, N_FFN + t:N_FFN + t + 1], sl[:, a], ALU.mult, ALU.mult)
                    ins.then_inc(s_hid, 1)

                if start:
                    for k in (2, 3):
                        dve_split(dve, u0 + k, it0)
                    if before is not None:
                        before()
                    for k in (4, 5):
                        dve_split(dve, u0 + k, it0)
                    hidden(0, 0, it0)
                    if between is not None:
                        between()
                if not steps:
                    return
                with dve.Fori(0, (NSTEP - 1) // 2) as i:
                    it = it0 + i
                    for j in range(2):
                        u = u0 + 4 + 6 * j
                        for k in (2, 3):
                            dve_split(dve, u + k, it)
                        hidT(step0, j, j, it, nt)
                        for k in (4, 5):
                            dve_split(dve, u + k, it)
                        hidden(j + 1, (j + 1) % 2, it)
                        for k in (6, 7):
                            dve_split(dve, u + k, it)

            def hidT(step0, j, par, it, nt):
                dve.wait_ge(s_hidT_hi, it * 2 + (step0 + j + 1))
                V.tensor_tensor(hidT_lo[:, :, 0:P * nt],
                                ps[:, 6 + par, 0:2 * P * nt].rearrange("p (k t) -> p k t", k=2),
                                hidT_hi[:, :, 0:P * nt].bitcast(f32), ALU.subtract).then_inc(s_hidT_lo, 1)

            pre_gain(x, ZU, landed=True)
            for L in range(DEPTH):
                transposed_by_tile()
                if L > 0:
                    advance(c.done + 2)
                    residual(S1, N_POST, s_res)
                advance(c.done + 4)
                w_in = linear(3, 4, lambda b, t: Z[:, t, W1C * b:W1C * b + W1C], W1C, N_MIX, 2.0)
                run(w_in, 2)
                dve.wait_ge(s_sg, 16 * 9 * (L + 1))
                lq = sg[:, SG_LAM:SG_LAM + 128].rearrange("p (m a d) -> p m a d", m=2, a=2)
                lp = scratch[:, 0:64].rearrange("p (m d) -> p m d", m=2)
                link(V.tensor_tensor(lp, lq[:, :, 0, :], lq[:, :, 1, :], ALU.mult))
                V.tensor_reduce(lam[:, 0:2], lp, AX, ALU.add).then_inc(s_lamq, 1)
                run(w_in, 3)
                if L == 0:
                    dve.wait_ge(s_wr, 1)
                    V.tensor_tensor(wr_split[:, :, NE:2 * NE], wr[:, :, :], wr_split[:, :, 0:NE].bitcast(f32),
                                    ALU.subtract).then_inc(s_wrl, 1)
                dve.wait_ge(s_ssq, c.norm + 1)
                pre_gain(S1, S1)
                run(w_in, 3)
                own_rows()
                for t in range(NT):
                    for c0, c1, g in ((0, Q_LORA, SG_Q), (Q_LORA, C_ROPE, SG_KV)):
                        ins = V.tensor_tensor(ZU[:, t, c0:c1], Z[:, t, c0:c1], sg[:, g:g + c1 - c0], ALU.mult)
                rows_done(ins)
                c.norm += 1
                run(w_in, 2)
                dve.wait_ge(s_lame, L + 1)
                link(V.tensor_tensor(nlam[:, :], lam[:, 3:4], lam[:, 2:3], ALU.subtract))
                link(V.tensor_scalar(nlam[:, :], nlam[:, :], -LAMBDA_INIT[L], None, ALU.add))
                run(w_in)
                transposed(oT_lo, oT_hi, 0, (1, 1, 1, 2))
                run(linear(2, 2, lambda b, t: ZU[:, t, Q_LORA * b:Q_LORA * b + Q_LORA], Q_LORA, N_LAT))
                KF = ZU[:, :, 768:1536].rearrange("p t (h d) -> p t h d", d=QK_MLA)
                VM = ZU[:, :, 1536:2048]
                c.done += 2
                dve.wait_ge(s_used, c.done)
                for n in range(4):
                    t, hf = n // 2, n % 2
                    kv = ps[:, acc_bank(c.acc), :].rearrange("p (h a d) -> p h a d", h=4, a=2)
                    f = rstd[:, N_LAT + 2 + t:N_LAT + 3 + t]
                    V.tensor_scalar(KF[:, t, 4 * hf:4 * hf + 4, 0:NOPE], kv[:, :, 0, :], f, None, ALU.mult)
                    V.tensor_scalar(VM[:, t, 256 * hf:256 * hf + 256].rearrange("p (h d) -> p h d", h=4),
                                    kv[:, :, 1, :], f, None, ALU.mult).then_inc(s_acc_free, 1)
                    c.acc += 1
                transposed(oT_lo, oT_hi, 0, (2, 2, 2, 2))
                advance(c.done + 4)

                def spilled(b):
                    if 4 * L + b > 0:
                        dve.wait_ge(s_spill, 16 * (4 * L + b))

                others = linear(4, 4, lambda b, t: E4[:, t, :], 512, N_MEM, free=spilled)
                Q = ZU[:, :, 0:768].rearrange("p t (h d) -> p t h d", d=QK_MLA)
                KR = Z[:, :, C_ROPE:C_ROPE + ROT]
                for t in range(NT):
                    link(rotate(lambda t: Q[:, t, :, NOPE:].rearrange("p h (a d) -> p h a d", a=2),
                                lambda t: (Q[:, t, :, NOPE:NOPE + 16], Q[:, t, :, NOPE + 16:]), RC_M, RS_M, MLA_H, 16,
                                (t,)))
                    run(others, 1)
                link(rotate(lambda t: KR[:, t, :].rearrange("p (h a d) -> p h a d", h=1, a=2),
                            lambda t: (KR[:, t, 0:16].unsqueeze(1), KR[:, t, 16:32].unsqueeze(1)), RC_M, RS_M, 1, 16))
                for t in range(NT):
                    ins = V.tensor_copy(KF[:, t, :, NOPE:], KR[:, t, :].unsqueeze(1).broadcast_to([P, MLA_H, ROT]))
                rows_done(ins)
                run(others, 2)
                O = ZU[:, :, 0:BW]

                def out_pair(n):
                    return O[:, n % 2, P * (n // 2):P * (n // 2) + P].rearrange("p (h d) -> p h d", h=2)

                c.pt += 8
                attention(8, out_pair, HD, fill=others, units=12)
                run(others)
                c.pt += 3
                branch_outputs()
                dve.wait_ge(s_spill, 64 * (L + 1))
                others = gated(0)
                attention(8, out_pair, HD, fill=others, units=12)
                run(others)
                def diff_rows(b, t):
                    src = ps[:, acc_bank(c.acc), :]
                    if b == 2:
                        return [(Z[:, t, 2 * W2C:3 * W2C], src)]
                    return [(Z[:, t, W2C * b + 256 * n:W2C * b + 256 * n + 256].rearrange("p (m h d) -> p h m d", m=2, d=DQK),
                             src[:, 256 * n:256 * n + 256].rearrange("p (h m d) -> p h m d", m=2, d=DQK)) for n in range(2)]

                w_in = linear(3, 4, diff_rows, W2C, N_MIX, 2.0)
                run(w_in, 4)
                branch_outputs()
                for b in range(2):
                    run(w_in, 1 if b == 0 else 4)
                    R = Z[:, :, 512 * b:512 * b + 512].rearrange("p t (h d) -> p t h d", d=DQK)
                    rows_done(rotate(lambda t: R[:, t, :, 0:DROT].rearrange("p h (a d) -> p h a d", a=2),
                                     lambda t: (R[:, t, :, 0:4], R[:, t, :, 4:8]), RC_P, RS_P, 16, 4))
                run(w_in)
                c.pt += 4
                others = gated(1)
                attention(16, lambda n: O[:, n % 2, DV * (n // 2):DV * (n // 2) + DV], DV, diff=True, fill=others, units=12)
                run(others)
                others = gated(2)
                heads = [O[:, t, :].rearrange("p (h d) -> p h d", d=DV) for t in range(NT)]
                run(others, 1)
                dve.wait_ge(s_subsq, 2 * L + 1)
                for t in range(NT):
                    ins = V.tensor_reduce(ssq[:, N_DIFF + 8 * t:N_DIFF + 8 * t + 8],
                                          scratch[:, BW * t:BW * t + BW].rearrange("p (h d) -> p h d", d=DV), AX, ALU.add)
                ins.then_inc(s_ssq, 1)
                c.norm += 1
                run(others, 1)
                dve.wait_ge(s_rstd, c.norm)
                for t, v in enumerate(heads):
                    f = rstd[:, N_DIFF + 8 * t:N_DIFF + 8 * t + 8].unsqueeze(2).broadcast_to([P, DIFF_H, DV])
                    ins = V.tensor_tensor(v, v, f, ALU.mult)
                rows_done(ins)
                run(others, 2)
                branch_outputs()
                run(others)
                transposed_by_tile()
                projected()
                next_rows(N_POST, 1)
                c.pt += 4
                transposed_by_tile()
                advance(c.done + 2)
                residual(S1, N_POST, s_res)
                run(linear(2, 4, lambda b, t: ZU[:, t, 512 * b:512 * b + 512], 512, N_PRE))
                c.pt += 4
                attention(4, lambda n: S1[:, n % 2, 512 * (n // 2):512 * (n // 2) + 512]
                          .rearrange("p (h d) -> p h d", h=2), MEM_HD)
                transposed(hT_lo, hT_hi, 0, (2, 2, 2, 2))
                projected()
                next_rows(N_POST2, 1 if L == 0 else 0)
                if L == 0:
                    transposed_by_tile()
                    advance(c.done + 2)
                    residual(S1, N_POST2, s_res)
                    ffn(0, FFN0[0], 0, NT, before=lambda: dve.wait_ge(s_rstd, c.norm))
                    hidT(0, NSTEP - 1, 0, 0, NT)
                    c.unit = c.done = LAYER0[1]
                    dense_outputs()
                    next_rows(N_POST, 1)
            transposed_by_tile(oT_lo, oT_hi)
            residual(S1, N_POST2, s_res)

            def bc(v):
                return v.unsqueeze(2).broadcast_to([P, NT, NE])

            def first_max(src, m, onehot):
                link(V.tensor_reduce(m, src, AX, ALU.max))
                for t in range(NT):
                    ins = V.scalar_tensor_tensor(CC[:, t, :], src[:, t, :], m[:, t:t + 1], DOWN, ALU.is_equal, ALU.mult)
                link(ins)
                link(V.tensor_reduce(I1, CC, AX, ALU.max))
                link(V.tensor_tensor(onehot, CC, bc(I1), ALU.is_equal))

            link(V.tensor_scalar(DOWN, iota[:, 0:NE], -1.0, float(NE), ALU.mult, ALU.add))
            dve.wait_ge(s_acc, c.rdy + 1)
            dve.wait_ge(s_rstd, c.norm)
            for part in range(2):
                for t in range(NT):
                    c0 = 2 * NE * t + NE * part
                    ins = V.scalar_tensor_tensor(LG[:, t, :], ps[:, acc_bank(c.acc), c0:c0 + NE],
                                                 rstd[:, N_FFN + t:N_FFN + t + 1],
                                                 LG[:, t, :] if part else brt[:, :], ALU.mult, ALU.add)
                link(ins)
            first_max(LG, M1, OH1)
            link(V.scalar_tensor_tensor(L2, OH1, -3.0e38, LG, ALU.mult, ALU.add))
            first_max(L2, M2, OH2)
            rows_done(V.tensor_tensor(MASK, OH1, OH2, ALU.add))
            V.tensor_tensor(W1, M2, M1, ALU.subtract).then_inc(s_topd, 1)
            dve.wait_ge(s_rows, c.rows)
            link(V.tensor_scalar(RANKM, MASK, -1000.0, 1000.0, ALU.mult, ALU.add))
            dve.wait_ge(s_hrow_hi, 1)
            for t in range(NT):
                ins = V.scalar_tensor_tensor(rows_lo[:, t, :], ZU[:, t, 0:D], rstd[:, N_FFN + t:N_FFN + t + 1],
                                             rows_hi[:, t, :].bitcast(f32), ALU.mult, ALU.subtract)
            ins.then_inc(s_hrow, 1)
            dve.wait_ge(s_tope, 1)
            link(V.tensor_scalar(W1, EX, 1.0, None, ALU.add))
            link(V.reciprocal(W1, W1))
            link(V.tensor_tensor(W2, EX, W1, ALU.mult))
            V.tensor_tensor(OH1, OH1, bc(W1), ALU.mult)
            link(V.tensor_tensor(OH2, OH2, bc(W2), ALU.mult))
            link(V.tensor_tensor(GATE, OH1, OH2, ALU.add))
            dve.wait_ge(s_acc, c.rdy + 2)
            link(V.tensor_reduce(MX, ps[:, acc_bank(c.acc + 1), 16:24], AX, ALU.max))
            link(V.tensor_scalar(NR, MX, float(P), 1.0, ALU.is_gt, ALU.add))
            V.tensor_copy(rounds[:, :], NR).then_inc(s_rounds, 1)
            rk = ps[:, acc_bank(c.acc + 1), 0:16].rearrange("p (t e) -> p t e", t=NT)
            V.tensor_tensor(RANKM, RANKM, rk, ALU.add).then_inc(s_rank, 1)
            dve.wait_ge(s_rounds, 1)
            nr = dve.value_load(rounds[0:1, 0:1], min_val=1, max_val=2)

            def one_hot(e, q, pr):
                dve.wait_ge(s_gath, q * 2 + e)
                mark(pr * 2 + e)

            def mark(expert):
                for t in range(NT):
                    ins = V.tensor_scalar(oh[:, t, :], iota[:, :], RANKM[:, t, bass.ds(expert, 1)] if
                                          not isinstance(expert, int) else RANKM[:, t, expert:expert + 1], None,
                                          ALU.is_equal)
                ins.then_inc(s_oh, 1)

            def banks(e):
                return ps[:, 2 * e:2 * e + 2, :].rearrange("p b (k s) -> p (b k) s", k=4)

            def gather_lo(e, q):
                dve.wait_ge(s_gath_hi, q * 2 + (e + 1))
                V.tensor_tensor(oT_lo[:, :, 0:P], banks(e), oT_hi[:, :, 0:P].bitcast(f32),
                                ALU.subtract).then_inc(s_gath_lo, 1)

            def y_lo(e, q):
                dve.wait_ge(s_yhi, q * 2 + (e + 1))
                V.tensor_tensor(oT_lo[:, :, P:2 * P], banks(e), oT_hi[:, :, P:2 * P].bitcast(f32),
                                ALU.subtract).then_inc(s_ylo, 1)

            def add_scattered(e, q, pr):
                for n in range(4):
                    t, hf = n // 2, n % 2
                    dve.wait_ge(s_scat, q * 8 + (4 * e + n + 1))
                    if n == 0:
                        dve.wait_ge(s_added, q * 8 + (4 * e + 1))
                    bk = (6, 7, 2 * e, 2 * e + 1)[n]
                    dst = S1[:, t, 512 * hf:512 * hf + 512]
                    gate = GATE[:, t, 2 * pr + e:2 * pr + e + 1] if isinstance(pr, int) else GATE[:, t, bass.ds(pr * 2 + e, 1)]
                    V.scalar_tensor_tensor(dst, ps[:, bk, :], gate, dst,
                                           ALU.mult, ALU.add).then_inc(s_added, 1)

            def start(e, q, it, pr, before=None, between=None, following=None):
                u = FFN0[1] + FFN_UNITS * e
                for k in (0, 1):
                    dve_split(dve, u + k, it)
                gather_lo(e, q)
                if following is not None:
                    following()
                ffn(NSTEP * (e + 1), u, it, 1, steps=False, before=before, between=between)

            def pair(q, pr, last):
                it = dve.snap(q * 11)
                ffn(NSTEP, FFN0[1], it, 1, start=False)
                hidT(NSTEP, NSTEP - 1, 0, it, 1)
                if last:
                    nxt = None
                else:
                    q1, pr1 = dve.snap(q + 1), dve.snap(pr + 1)
                    nxt = lambda: one_hot(0, q1, pr1)
                start(1, q, it, pr, lambda: y_lo(0, q), lambda: add_scattered(0, q, pr), nxt)
                ffn(2 * NSTEP, FFN0[1] + FFN_UNITS, it, 1, start=False)
                hidT(2 * NSTEP, NSTEP - 1, 0, it, 1)
                if last:
                    y_lo(1, q)
                    add_scattered(1, q, pr)
                else:
                    start(0, q1, dve.snap(it + 11), pr1, lambda: y_lo(1, q), lambda: add_scattered(1, q, pr),
                          lambda: one_hot(1, q1, pr1))

            with dve.Fori(0, nr) as r:
                dve.wait_ge(s_rank, r + 1)
                mark(0)
                q0 = dve.snap(r * (NE // 2))
                start(0, q0, dve.snap(q0 * 11), 0, following=lambda: one_hot(1, q0, 0))
                with dve.Fori(0, NE // 2 - 1) as pr:
                    pair(dve.snap(q0 + pr), pr, False)
                pair(dve.snap(q0 + (NE // 2 - 1)), NE // 2 - 1, True)
                V.tensor_scalar(RANKM, RANKM, -float(P), None, ALU.add).then_inc(s_rank, 1)
            dve.wait_ge(s_added, nr * (4 * NE) + 1)
            g = wait_gain()
            y = scratch.rearrange("p (t d) -> p t d", t=NT)
            for t in range(NT):
                ins = V.tensor_tensor(y[:, t, :], S1[:, t, :], gains[:, g, :], ALU.mult)
            link(ins)
            c.norm += 1
            dve.wait_ge(s_rstd, c.norm)
            residual(y, N_POST, s_final)

        @blk.tensor
        def _(pe):
            T = nc.tensor
            c = Counts()

            def three(out, a_hi, a_lo, b_hi, b_lo, start, stop):
                T.matmul(out, a_hi, b_hi, start=start, stop=False)
                T.matmul(out, a_hi, b_lo, start=False, stop=False)
                return T.matmul(out, a_lo, b_hi, start=False, stop=stop)

            def unit(us, it, nk, w, k0, act, outs, first, last):
                pe.wait_ge(s_lo, it * LOOP_UNITS + (us + 1))
                a_hi, a_lo = act
                for k in range(nk):
                    for a, bk, c0, n in outs:
                        col = k * w + c0
                        b_hi = w_hi[:, hi_slot(us), col:col + n]
                        b_lo = w_lo[:, hi_slot(us), col:col + n]
                        ins = three(ps[:, bk, 0:n], a(a_hi, k0 + k), a(a_lo, k0 + k), b_hi, b_lo,
                                    first and k == 0, last and k == nk - 1)
                ins.then_inc(s_used, 1)

            def tok(t):
                return lambda src, k: src[:, k, P * t:P * t + P]

            def claim(n):
                if c.acc + n > 4:
                    pe.wait_ge(s_acc_free, c.acc + n - 4)

            def block(w, nks, act):
                claim(2)
                outs = [(tok(t), acc_bank(c.acc + t), 0, w) for t in range(NT)]
                k0 = 0
                for n, nk in enumerate(nks):
                    unit(c.done, 0, nk, w, k0, act, outs, n == 0, n == len(nks) - 1)
                    c.done += 1
                    k0 += nk
                    if n == len(nks) - 1:
                        c.acc += 2
                    yield

            def split_T(src, widths):
                k = 0
                for w in widths:
                    claim(1)
                    for n in range(w * NT):
                        kk, t = k + n // NT, n % NT
                        ins = T.transpose(ps[:, acc_bank(c.acc), P * n:P * n + P], src(t)[:, P * kk:P * kk + P],
                                          ident[:, :])
                    ins.then_inc(s_acc, 1)
                    c.acc += 1
                    c.rdy += 1
                    k += w

            def blocks(n, w, nks, act):
                for b in range(n):
                    yield from block(w, nks, act)

            def split_ready():
                pe.wait_ge(s_acc_free, c.acc)

            def split_T_by_tile(src, ready):
                for t in range(NT):
                    ready(t)
                    for k0 in (0, 4):
                        claim(1)
                        for n in range(4):
                            ins = T.transpose(ps[:, acc_bank(c.acc), P * n:P * n + P],
                                              src[:, t, P * (k0 + n):P * (k0 + n) + P], ident[:, :])
                        ins.then_inc(s_acc, 1)
                        c.acc += 1
                        c.rdy += 1

            def plain_T(cols, heads, width):
                for h in range(0, heads, 2):
                    if c.pt >= 2:
                        pe.wait_ge(s_pt_copied, c.pt - 1)
                    for n in range(2 * min(2, heads - h)):
                        hh, t = h + n // 2, n % 2
                        ins = T.transpose(ps[0:width, 2 + c.pt % 2, P * n:P * n + P], cols(t, hh), ident[:, :])
                    ins.then_inc(s_pt, 1)
                    c.pt += 1

            def attention(n, scores, values, hd, fill=(), units=0):
                u0 = c.sc
                copied = {}
                for s in range(n + 2):
                    if s < n:
                        u = u0 + s
                        if u >= 2:
                            pe.wait_ge(s_p, u - 1)
                        if s == 0:
                            pe.wait_ge(s_pt_copied, c.pt)
                        for hh in range(2):
                            pairs = scores(s, hh)
                            for m, (q, k) in enumerate(pairs):
                                ins = T.matmul(ps[:, u % 2, 256 * hh:256 * hh + 256], q, k, start=m == 0,
                                               stop=m == len(pairs) - 1)
                        ins.then_inc(s_sc, 1)
                    share(fill, units, s, n + 2)
                    if 1 <= s <= n:
                        u = u0 + s - 1
                        pe.wait_ge(s_p, u + 1)
                        pe.wait_ge(s_pt_copied, c.pt)
                        for m in range(4):
                            ins = T.transpose(ps[:, 2, P * m:P * m + P], Pr[:, u % 2, P * m:P * m + P], ident[:, :])
                        ins.then_inc(s_pt, 1)
                        c.pt += 1
                        copied[s - 1] = c.pt
                    if s >= 2:
                        u = u0 + s - 2
                        pe.wait_ge(s_pt_copied, copied[s - 2])
                        if s >= 3:
                            pe.wait_ge(s_pv_free, c.pv)
                        for hh in range(2):
                            for kt in range(2):
                                ins = T.matmul(ps[:, 3, hd * hh:hd * hh + hd],
                                               PT[:, u % 2, 256 * hh + P * kt:256 * hh + P * kt + P],
                                               values(s - 2, hh, kt), start=kt == 0, stop=kt == 1)
                        ins.then_inc(s_pv, 1)
                        c.pv += 1
                c.sc += n

            def gated():
                for half in range(2):
                    yield from block(512, (2, 2, 2, 2), (hT_hi, hT_lo))
                    pe.wait_ge(s_outT, 2 * c.branches)
                    yield from block(512, (2, 2), (oT_hi, oT_lo))

            def branch_outputs_T():
                plain_T(lambda t, k: ZU[:, t, P * k:P * k + P], BW // P, P)
                c.branches += 1

            def hid_T(step0, j, par, it, nt):
                pe.wait_ge(s_hid, it * 2 + (step0 + j + 1))
                for k in range(2):
                    for t in range(nt):
                        ins = T.transpose(ps[:, 6 + par, P * (k * nt + t):P * (k * nt + t) + P],
                                          hid[:, FB * t + P * k:FB * t + P * k + P], ident[:, :])
                ins.then_inc(s_hidT, 1)

            def gate_up(us, it, step0, j, par, nt, act, half):
                if half == 0 and j > 0:
                    pe.wait_ge(s_hid, it * 2 + (step0 + j - (0 if nt == 2 else 1)))
                outs = [(tok(t), 4 + (t if nt == 2 else par), 0, 512) for t in range(nt)]
                for k in range(2):
                    unit(us + k, it, 2, 512, 4 * half + 2 * k, act, outs, half == 0 and k == 0, half == 1 and k == 1)

            def down(us, it, step0, j, nt, y0, first, last):
                pe.wait_ge(s_hidT_lo, it * 2 + (step0 + j + 1))
                for k in range(2):
                    outs = [(tok(t), y0 + 2 * t + hf, 512 * hf, 512) for t in range(nt) for hf in range(2)]
                    unit(us + k, it, 1, 1024, k, (hidT_hi, hidT_lo), outs, first and k == 0, last and k == 1)

            def ffn_steps(step0, u0, it0, nt, act, y0, free=None):
                def pair(it, first):
                    for j in range(2):
                        u = u0 + 4 + 6 * j
                        gate_up(u, it, step0, j + 1, (j + 1) % 2, nt, act, 0)
                        if first and j == 0 and free is not None:
                            free()
                        hid_T(step0, j, j, it, nt)
                        gate_up(u + 2, it, step0, j + 1, (j + 1) % 2, nt, act, 1)
                        down(u + 4, it, step0, j, nt, y0, first and j == 0, False)

                pair(it0, True)
                with pe.Fori(1, (NSTEP - 1) // 2) as i:
                    pair(it0 + i, False)

            def ffn_end(step0, u0, it0, nt, y0):
                hid_T(step0, NSTEP - 1, 0, it0, nt)
                down(u0 + FFN_UNITS - 2, it0, step0, NSTEP - 1, nt, y0, False, True)

            def rows_ready():
                c.rows += 1
                pe.wait_ge(s_rows, c.rows)

            def gained_T(src):
                split_T_by_tile(src, lambda t: pe.wait_ge(s_norm, NT * c.pre + t + 1))
                c.pre += 1

            pe.wait_ge(s_ident, 16)
            for L in range(DEPTH):
                gained_T(ZU)
                split_ready()
                run(blocks(3, W1C, (2, 2, 2, 2), (hT_hi, hT_lo)))
                rows_ready()
                split_T(lambda t: ZU[:, t, 0:C_ROPE], (1, 1, 1, 2))
                split_ready()
                run(blocks(2, Q_LORA, (2, 1), (oT_hi, oT_lo)))
                claim(4)
                for k in range(2):
                    unit(c.done, 0, 1, 1024, 3 + k, (oT_hi, oT_lo),
                         [(tok(t), acc_bank(c.acc + 2 * t + hf), 512 * hf, 512) for t in range(NT) for hf in range(2)],
                         k == 0, k == 1)
                    c.done += 1
                c.acc += 4
                c.pre += 1
                pe.wait_ge(s_norm, NT * c.pre)
                split_T(lambda t: S1[:, t, :], (2, 2, 2, 2))
                assert c.rdy == T_MEM[L] and c.acc == LAYER_BANKS * L + KV_BANK
                split_ready()
                others = blocks(4, 512, (2, 2, 2, 2), (oT_hi, oT_lo))
                run(others, 4)
                rows_ready()
                plain_T(lambda t, h: ZU[:, t, QK_MLA * h:QK_MLA * h + QK_MLA], MLA_H, QK_MLA)
                plain_T(lambda t, h: ZU[:, t, 768 + QK_MLA * h:768 + QK_MLA * h + QK_MLA], MLA_H, QK_MLA)

                def mla_scores(s, hh):
                    h, t = 2 * (s // 2) + hh, s % 2
                    return [(qT[0:QK_MLA, h, P * t:P * t + P], kT[0:QK_MLA, h, :])]

                def mla_values(s, hh, kt):
                    c0 = 1536 + MLA_V * (2 * (s // 2) + hh)
                    return ZU[:, kt, c0:c0 + MLA_V]

                attention(8, mla_scores, mla_values, HD, others, 12)
                run(others)
                pe.wait_ge(s_pv_free, c.pv)
                pe.wait_ge(s_gqa, L + 1)
                plain_T(lambda t, h: Z[:, t, C_GQA + P * h:C_GQA + P * h + P], GQA_QH // GQA_KVH, P)
                plain_T(lambda t, h: Z[:, t, C_GQA + BW:C_GQA + BW + P], 1, P)

                group = GQA_QH // GQA_KVH

                def gqa_scores(s, hh):
                    h, t = 2 * (s // 2) + hh, s % 2
                    r = HD * (h // group)
                    return [(qT[r:r + HD, h % group, P * t:P * t + P], kT[r:r + HD, 0, :])]

                def gqa_values(s, hh, kt):
                    c0 = C_GQA + HD * (GQA_QH + GQA_KVH + (2 * (s // 2) + hh) // group)
                    return Z[:, kt, c0:c0 + HD]

                branch_outputs_T()
                attention(8, gqa_scores, gqa_values, HD, gated(), 12)
                w_in = blocks(3, W2C, (2, 2, 2, 2), (hT_hi, hT_lo))
                run(w_in, 4)
                pe.wait_ge(s_pv_free, c.pv)
                branch_outputs_T()
                run(w_in)
                for c0 in (0, 512):
                    rows_ready()
                    plain_T(lambda t, h: Z[:, t, c0 + P * h:c0 + P * h + P], DIFF_H // 2, P)

                def diff_scores(s, m):
                    h, t = s // 2, s % 2
                    n, r = 2 * (h // 4) + m, DQK * (h % 4)
                    return [(qT[r:r + DQK, n, P * t:P * t + P], kT[r:r + DQK, n, :])]

                def diff_values(s, m, kt):
                    c0 = 1024 + DV * (s // 2)
                    return Z[:, kt, c0:c0 + DV]

                attention(16, diff_scores, diff_values, DV, gated(), 12)
                gates = gated()
                run(gates, 4)
                rows_ready()
                branch_outputs_T()
                run(gates)
                merged = c.acc
                split_T_by_tile(S1, lambda t: pe.wait_ge(s_acc_free, merged - 2 + 2 * t))
                split_ready()
                run(blocks(2, 512, (2, 2, 2, 2), (hT_hi, hT_lo)))
                pe.wait_ge(s_kmem, 16 * (L + 1))
                plain_T(lambda t, h: ZU[:, t, 1024 + P * h:1024 + P * h + P], 8, P)
                gained_T(ZU)
                split_ready()
                run(blocks(2, 512, (2, 2, 2, 2), (hT_hi, hT_lo)))
                for half in range(2):
                    pe.wait_ge(s_acc_free, c.acc - 2 + 2 * half)
                    plain_T(lambda t, h: ZU[:, t, 512 * half + P * h:512 * half + P * h + P], 4, P)

                def mem_scores(s, hh):
                    h, t = 2 * (s // 2) + hh, s % 2
                    return [(qT[:, 2 * h + k, P * t:P * t + P], kT[:, 2 * h + k, :]) for k in range(2)]

                def mem_values(s, hh, kt):
                    h = 2 * (s // 2) + hh
                    return Z[:, kt, MEM_HD * h:MEM_HD * h + MEM_HD]

                pe.wait_ge(s_vmem, 16 * (L + 1))
                attention(4, mem_scores, mem_values, MEM_HD)
                pe.wait_ge(s_pv_free, c.pv)
                split_T(lambda t: S1[:, t, :], (2, 2, 2, 2))
                split_ready()
                run(blocks(2, 512, (2, 2, 2, 2), (hT_hi, hT_lo)))
                gained_T(ZU)
                split_ready()
                if L == 0:
                    for half in range(2):
                        gate_up(FFN0[0] + 2 * half, 0, 0, 0, 0, NT, (hT_hi, hT_lo), half)
                    ffn_steps(0, FFN0[0], 0, NT, (hT_hi, hT_lo), 0)
                    ffn_end(0, FFN0[0], 0, NT, 0)
                    c.done = LAYER0[1]
            pe.wait_ge(s_wrl, 1)
            claim(2)
            bk = acc_bank(c.acc)
            for t in range(NT):
                for k in range(8):
                    for m, src in enumerate((oT_hi, oT_lo)):
                        ins = T.matmul(ps[:, bk, 2 * NE * t:2 * NE * t + 2 * NE], src[:, k, P * t:P * t + P],
                                       wr_split[:, k, :], start=k == 0 and m == 0, stop=k == 7 and m == 1)
            ins.then_inc(s_acc, 1)
            pe.wait_ge(s_tri, 32)
            rows_ready()
            bk = acc_bank(c.acc + 1)
            T.matmul(ps[:, bk, 0:NE], tri, MASK[:, 0, :], start=True, stop=True)
            T.matmul(ps[:, bk, NE:2 * NE], tri, MASK[:, 1, :], start=True, stop=False)
            T.matmul(ps[:, bk, NE:2 * NE], ones, MASK[:, 0, :], start=False, stop=True)
            T.matmul(ps[:, bk, 2 * NE:3 * NE], ones, MASK[:, 0, :], start=True, stop=False)
            T.matmul(ps[:, bk, 2 * NE:3 * NE], ones, MASK[:, 1, :], start=False, stop=True).then_inc(s_acc, 1)
            pe.wait_ge(s_hrow, 1)
            pe.wait_ge(s_rounds, 1)
            nr = pe.value_load(rounds[0:1, 0:1], min_val=1, max_val=2)

            def gather(e, q, added):
                pe.wait_ge(s_oh, q * 2 + (e + 1))
                pe.wait_ge(s_added, added)
                for t in range(NT):
                    T.transpose(ps[:, 7, P * t:P * t + P], oh[:, t, :].bitcast(f32), ident[:, :])
                for k in range(8):
                    out = ps[:, 2 * e + k // 4, P * (k % 4):P * (k % 4) + P]
                    for n in range(4):
                        t, src = n // 2, (rows_hi, rows_lo)[n % 2]
                        ins = T.matmul(out, src[:, t, P * k:P * k + P], oh[:, t, :], start=n == 0, stop=n == 3)
                ins.then_inc(s_gath, 1)

            def scatter(e, q):
                pe.wait_ge(s_ylo, q * 2 + (e + 1))
                pe.wait_ge(s_ohT, q * 2 + 2)
                for n in range(4):
                    t, hf = n // 2, n % 2
                    bk = (6, 7, 2 * e, 2 * e + 1)[n]
                    for m, src in enumerate((oT_hi, oT_lo)):
                        ins = T.matmul(ps[:, bk, :], ohT[:, e, P * t:P * t + P], src[:, 4 * hf:4 * hf + 4, P:2 * P],
                                       start=m == 0, stop=m == 1)
                    ins.then_inc(s_scat, 1)

            def expert_start(e, q, it):
                pe.wait_ge(s_gath_lo, q * 2 + (e + 1))
                pe.wait_ge(s_hid, it * 2 + (NSTEP + NSTEP * e))
                for half in range(2):
                    gate_up(FFN0[1] + FFN_UNITS * e + 2 * half, it, NSTEP * (e + 1), 0, 0, 1, (oT_hi, oT_lo), half)

            def steps(e, q, it):
                ffn_steps(NSTEP * (e + 1), FFN0[1] + FFN_UNITS * e, it, 1, (oT_hi, oT_lo), 2 * e,
                          lambda: pe.wait_ge(s_added, q * 8 + (4 * e + 1)))

            def last_down(e, it):
                down(FFN0[1] + FFN_UNITS * (e + 1) - 2, it, NSTEP * (e + 1), NSTEP - 1, 1, 2 * e, False, True)

            def pair(q, last):
                it = pe.snap(q * 11)
                steps(0, q, it)
                hid_T(NSTEP, NSTEP - 1, 0, it, 1)
                gather(1, q, q * 8 + 1)
                last_down(0, it)
                expert_start(1, q, it)
                scatter(0, q)
                steps(1, q, it)
                hid_T(2 * NSTEP, NSTEP - 1, 0, it, 1)
                if not last:
                    q1 = pe.snap(q + 1)
                    gather(0, q1, q * 8 + 5)
                last_down(1, it)
                if not last:
                    expert_start(0, q1, pe.snap(it + 11))
                scatter(1, q)

            with pe.Fori(0, nr) as r:
                q0 = pe.snap(r * (NE // 2))
                gather(0, q0, q0 * 8 + 1)
                expert_start(0, q0, pe.snap(q0 * 11))
                with pe.Fori(0, NE // 2 - 1) as pr:
                    pair(pe.snap(q0 + pr), False)
                pair(pe.snap(q0 + (NE // 2 - 1)), True)


_INS = ['x', 'mem', 'mix_pre_g', 'mix_post_g', 'w_in', 'mla_q_norm_g', 'mla_w_q_up', 'mla_kv_norm_g', 'mla_w_kv_up',
        'gqa_q_norm_g', 'gqa_k_norm_g', 'diff_lambda_q1', 'diff_lambda_k1', 'diff_lambda_q2', 'diff_lambda_k2',
        'diff_subln_g', 'w_branch', 'w_out', 'mem_pre_g', 'mem_post_g', 'mem_norm_g', 'mem_wq', 'mem_wkv', 'mem_wo',
        'ffn_pre_g', 'ffn_post_g', 'dense_w_gate', 'dense_w_up', 'dense_w_down', 'moe_w_router', 'moe_b_router',
        'moe_w_gate', 'moe_w_up', 'moe_w_down']


def rope_table():
    import numpy as np
    f = np.float32

    def cos_sin(pos, rot):
        inv = f(500000.0) ** (-np.arange(0, rot, 2, dtype=f) / f(rot))
        ang = pos.astype(f)[:, None] * inv.astype(f)[None, :]
        return np.cos(ang), np.sin(ang)

    pos = np.arange(SEQ)
    cm, sm = cos_sin(pos, ROT)
    cr, sr = cos_sin(pos // 64, HD // 2)
    cc, sc = cos_sin(pos % 64, HD // 2)
    cp, sp = cos_sin(pos, DROT)
    return np.concatenate([cm, sm, cr, cc, sr, sc, cp, sp], axis=1).astype(f)


def constants():
    import numpy as np
    return np.stack([np.eye(P), np.tile(np.arange(P), (P, 1)), np.triu(np.ones((P, P)), 1), np.ones((P, P))]).astype(np.float32)


def kernel(**inputs):
    import numpy as _np
    import concourse.bacc as _bacc
    from concourse import mybir as _mybir
    from concourse.bass_utils import run_bass_kernel_spmd as _run

    nc = _bacc.Bacc("TRN2", target_bir_lowering=False, num_devices=1)
    arrays, aps = {}, {}
    named = [(name, _np.ascontiguousarray(inputs[name])) for name in _INS]
    named += [("rope", rope_table()), ("consts", constants())]
    for name, a in named:
        arrays[f"in_{name}_dram"] = a
        aps[name] = nc.dram_tensor(f"in_{name}_dram", a.shape, _mybir.dt.from_np(a.dtype), kind="ExternalInput").ap()
    aps["out"] = nc.dram_tensor("out_0_dram", (1, SEQ, D), _mybir.dt.float32, kind="ExternalOutput").ap()
    build(nc, aps)
    r = _run(nc, [arrays], core_ids=[0])
    return r.results[0]["out_0_dram"]
```
